# Optimizing a Trainium2 kernel written in Bass

```python
import jax, jax.numpy as jnp
from jax import lax
import numpy as np

D_MODEL = 1024
BATCH = 1
SEQ = 512
DEPTH = 1

MEM_LEN = 256
EPS = 1e-6
ROPE_THETA = 10000.0
HG_HEADS = 4
HG_DK = 128
HG_DV = 128
HG_WIDTH = HG_HEADS * HG_DK
HG_CHUNK = 64
DSA_HEADS = 8
DSA_Q_LORA = 256
DSA_KV_LORA = 128
DSA_NOPE = 64
DSA_ROPE = 32
DSA_VDIM = 64
DSA_WIDTH = DSA_HEADS * DSA_VDIM
IDX_HEADS = 8
IDX_DIM = 64
TOPK_MAX = 256
Q_BLOCK = 128
MEM_HEADS = 4
MEM_DH = 128
MEM_WIDTH = MEM_HEADS * MEM_DH
D_FF = 4 * D_MODEL
N_BRANCH = 3
IN_SPLITS = (HG_WIDTH, HG_WIDTH, HG_WIDTH, HG_WIDTH,
             DSA_Q_LORA, DSA_KV_LORA, DSA_ROPE, IDX_DIM, IDX_HEADS,
             MEM_WIDTH,
             N_BRANCH * D_MODEL)
IN_WIDTH = sum(IN_SPLITS)

kernel_name = 'hybrid_hgrn2_dsa_memxattn_block'

def rmsnorm(x, w):
    x32 = x.astype(jnp.float32)
    y = x32 * lax.rsqrt(jnp.mean(x32 * x32, axis=-1, keepdims=True) + EPS)
    return (y * w.astype(jnp.float32)).astype(x.dtype)

def rope(x, pos):
    d = x.shape[-1]
    inv = ROPE_THETA ** (-jnp.arange(0, d, 2, dtype=jnp.float32) / d)
    ang = pos.astype(jnp.float32)[:, None] * inv[None, :]
    cos = jnp.cos(ang)[None, :, None, :]
    sin = jnp.sin(ang)[None, :, None, :]
    x32 = x.astype(jnp.float32)
    x1, x2 = x32[..., : d // 2], x32[..., d // 2:]
    return jnp.concatenate([x1 * cos - x2 * sin, x2 * cos + x1 * sin], axis=-1).astype(x.dtype)

def hgrn2_mix(q, f_logit, v, lb):
    B, T, _ = q.shape
    nc = T // HG_CHUNK
    f = lb + (1.0 - lb) * jax.nn.sigmoid(f_logit.astype(jnp.float32))
    log_f = jnp.log(f)
    k = 1.0 - f

    def to_chunks(a, d):
        return a.astype(jnp.float32).reshape(B, nc, HG_CHUNK, HG_HEADS, d).transpose(1, 0, 3, 2, 4)

    qc, kc, vc = to_chunks(q, HG_DK), to_chunks(k, HG_DK), to_chunks(v, HG_DV)
    bc = jnp.cumsum(to_chunks(log_f, HG_DK), axis=3)
    causal = jnp.tril(jnp.ones((HG_CHUNK, HG_CHUNK), dtype=bool))

    def step(S, inp):
        q_, k_, v_, b_ = inp
        o_inter = jnp.einsum('bhtk,bhkv->bhtv', q_ * jnp.exp(b_), S)
        diff = b_[:, :, :, None, :] - b_[:, :, None, :, :]
        decay = jnp.exp(jnp.where(causal[:, :, None], diff, -jnp.inf))
        A = jnp.einsum('bhtk,bhsk,bhtsk->bhts', q_, k_, decay)
        o = o_inter + jnp.einsum('bhts,bhsv->bhtv', A, v_)
        b_last = b_[:, :, -1:, :]
        S_new = (jnp.exp(b_last[:, :, 0, :])[..., None] * S
                 + jnp.einsum('bhsk,bhsv->bhkv', k_ * jnp.exp(b_last - b_), v_))
        return S_new, o

    S0 = jnp.zeros((B, HG_HEADS, HG_DK, HG_DV), jnp.float32)
    _, o = lax.scan(step, S0, (qc, kc, vc, bc))
    return o.transpose(1, 0, 3, 2, 4).reshape(B, T, HG_HEADS, HG_DV).astype(q.dtype)

def dsa_mix(c_q, c_kv, k_rope, k_idx, w_idx, pos, w_uq, w_qr, w_uk, w_uv, w_qidx, topk):
    B, T, _ = c_q.shape
    q_nope = jnp.einsum('btc,chn->bthn', c_q, w_uq)
    q_rope = rope(jnp.einsum('btc,chr->bthr', c_q, w_qr), pos)
    q_abs = jnp.einsum('bthn,hnc->bthc', q_nope, w_uk)
    q_cat = jnp.concatenate([q_abs, q_rope], axis=-1)
    q_idx = rope(jnp.einsum('btc,chd->bthd', c_q, w_qidx), pos)
    k_rope = rope(k_rope[:, :, None, :], pos)[:, :, 0]
    k_idx = rope(k_idx[:, :, None, :], pos)[:, :, 0]
    kv = jnp.concatenate([c_kv, k_rope], axis=-1)
    scale = (DSA_NOPE + DSA_ROPE) ** -0.5
    nb = T // Q_BLOCK
    key_pos = jnp.arange(T, dtype=jnp.int32)

    def blocks(a):
        return a.reshape(B, nb, Q_BLOCK, *a.shape[2:]).swapaxes(0, 1)

    def one_block(inp):
        qc_, qi_, wi_, tpos = inp
        s = jax.nn.relu(jnp.einsum('bthd,bsd->bths', qi_, k_idx).astype(jnp.float32) * IDX_DIM ** -0.5)
        score = jnp.einsum('bths,bth->bts', s, wi_.astype(jnp.float32) * IDX_HEADS ** -0.5)
        causal = key_pos[None, :] <= tpos[:, None]
        score = jnp.where(causal[None], score, -jnp.inf)
        _, idx = lax.top_k(score, topk)
        valid = idx <= tpos[None, :, None]
        sel = jax.vmap(lambda kv_b, idx_b: kv_b[idx_b])(kv, idx)
        logits = jnp.einsum('bthc,btkc->bthk', qc_, sel).astype(jnp.float32) * scale
        logits = jnp.where(valid[:, :, None, :], logits, -jnp.inf)
        p = jax.nn.softmax(logits, axis=-1).astype(sel.dtype)
        return jnp.einsum('bthk,btkc->bthc', p, sel[..., :DSA_KV_LORA])

    o_lat = lax.map(one_block, (blocks(q_cat), blocks(q_idx), blocks(w_idx), pos.reshape(nb, Q_BLOCK)))
    o_lat = o_lat.swapaxes(0, 1).reshape(B, T, DSA_HEADS, DSA_KV_LORA)
    return jnp.einsum('bthc,hcv->bthv', o_lat, w_uv).reshape(B, T, DSA_WIDTH)

def mem_cross(q, mem, mem_norm_w, w_mem_kv):
    B, T, _ = q.shape
    mn = rmsnorm(mem, mem_norm_w)
    kvm = mn @ w_mem_kv
    k_m = kvm[..., :MEM_WIDTH].reshape(B, -1, MEM_HEADS, MEM_DH)
    v_m = kvm[..., MEM_WIDTH:].reshape(B, -1, MEM_HEADS, MEM_DH)
    q_m = q.reshape(B, T, MEM_HEADS, MEM_DH)
    logits = jnp.einsum('bthd,bmhd->bhtm', q_m, k_m).astype(jnp.float32) * MEM_DH ** -0.5
    p = jax.nn.softmax(logits, axis=-1).astype(v_m.dtype)
    return jnp.einsum('bhtm,bmhd->bthd', p, v_m).reshape(B, T, MEM_WIDTH)

def setup_inputs(seed: int = 0) -> dict:
    key = jax.random.key(seed)
    ks = jax.random.split(key, 32)
    f32 = jnp.float32

    def nrm(k, shape, fan_in):
        return jax.random.normal(k, shape, f32) * fan_in ** -0.5

    def gain(k, shape):
        return 1.0 + 0.05 * jax.random.normal(k, shape, f32)

    L = DEPTH
    return {
        'x': jax.random.normal(ks[0], (BATCH, SEQ, D_MODEL), f32),
        'mem': jax.random.normal(ks[1], (BATCH, MEM_LEN, D_MODEL), f32),
        'attn_norm_w': gain(ks[2], (L, D_MODEL)),
        'w_in': nrm(ks[3], (L, D_MODEL, IN_WIDTH), D_MODEL),
        'hgrn_lower_bounds': 0.5 * jax.random.normal(ks[4], (L + 1, HG_WIDTH), f32),
        'hgrn_out_norm_w': gain(ks[5], (L, HG_WIDTH)),
        'dsa_q_norm_w': gain(ks[6], (L, DSA_Q_LORA)),
        'dsa_kv_norm_w': gain(ks[7], (L, DSA_KV_LORA)),
        'dsa_kidx_norm_w': gain(ks[8], (L, IDX_DIM)),
        'dsa_w_uq': nrm(ks[9], (L, DSA_Q_LORA, DSA_HEADS, DSA_NOPE), DSA_Q_LORA),
        'dsa_w_qr': nrm(ks[10], (L, DSA_Q_LORA, DSA_HEADS, DSA_ROPE), DSA_Q_LORA),
        'dsa_w_uk': nrm(ks[11], (L, DSA_HEADS, DSA_NOPE, DSA_KV_LORA), DSA_NOPE),
        'dsa_w_uv': nrm(ks[12], (L, DSA_HEADS, DSA_KV_LORA, DSA_VDIM), DSA_KV_LORA),
        'dsa_w_qidx': nrm(ks[13], (L, DSA_Q_LORA, IDX_HEADS, IDX_DIM), DSA_Q_LORA),
        'mem_norm_w': gain(ks[14], (L, D_MODEL)),
        'w_mem_kv': nrm(ks[15], (L, D_MODEL, 2 * MEM_WIDTH), D_MODEL),
        'w_br_hgrn': nrm(ks[16], (L, HG_WIDTH, D_MODEL), HG_WIDTH),
        'w_br_dsa': nrm(ks[17], (L, DSA_WIDTH, D_MODEL), DSA_WIDTH),
        'w_br_mem': nrm(ks[18], (L, MEM_WIDTH, D_MODEL), MEM_WIDTH),
        'w_out': nrm(ks[19], (L, D_MODEL, D_MODEL), D_MODEL),
        'mlp_norm_w': gain(ks[20], (L, D_MODEL)),
        'w_mlp_up': nrm(ks[21], (L, D_MODEL, D_FF), D_MODEL),
        'w_mlp_down': nrm(ks[22], (L, D_FF, D_MODEL), D_FF),
        'final_norm_w': gain(ks[23], (D_MODEL,)),
    }

def reference(x, mem, attn_norm_w, w_in, hgrn_lower_bounds, hgrn_out_norm_w, dsa_q_norm_w, dsa_kv_norm_w,
              dsa_kidx_norm_w, dsa_w_uq, dsa_w_qr, dsa_w_uk, dsa_w_uv, dsa_w_qidx, mem_norm_w, w_mem_kv,
              w_br_hgrn, w_br_dsa, w_br_mem, w_out, mlp_norm_w, w_mlp_up, w_mlp_down, final_norm_w):
    B, T, D = x.shape
    pos = jnp.arange(T, dtype=jnp.int32)
    topk = min(TOPK_MAX, T // 4)
    split_at = [int(s) for s in np.cumsum(IN_SPLITS)[:-1]]
    lb_all = jnp.cumsum(jax.nn.softmax(hgrn_lower_bounds.astype(jnp.float32), axis=0), axis=0)
    h = x
    for l in range(DEPTH):
        xn = rmsnorm(h, attn_norm_w[l])
        proj = xn @ w_in[l]
        hq, hf, hv, hg, cq, ckv, kr, kidx, widx, mq, gate_logits = jnp.split(proj, split_at, axis=-1)
        o_a = hgrn2_mix(hq, hf, hv, lb_all[l])
        o_a = rmsnorm(o_a, hgrn_out_norm_w[l].reshape(HG_HEADS, HG_DV)) * jax.nn.silu(hg.reshape(B, T, HG_HEADS, HG_DV))
        o_a = o_a.reshape(B, T, HG_WIDTH)
        o_b = dsa_mix(rmsnorm(cq, dsa_q_norm_w[l]), rmsnorm(ckv, dsa_kv_norm_w[l]), kr,
                      rmsnorm(kidx, dsa_kidx_norm_w[l]), widx, pos,
                      dsa_w_uq[l], dsa_w_qr[l], dsa_w_uk[l], dsa_w_uv[l], dsa_w_qidx[l], topk)
        o_c = mem_cross(mq, mem, mem_norm_w[l], w_mem_kv[l])
        gates = jax.nn.sigmoid(gate_logits).reshape(B, T, N_BRANCH, D)
        merged = (gates[:, :, 0] * (o_a @ w_br_hgrn[l])
                  + gates[:, :, 1] * (o_b @ w_br_dsa[l])
                  + gates[:, :, 2] * (o_c @ w_br_mem[l]))
        h = h + merged @ w_out[l]
        m = rmsnorm(h, mlp_norm_w[l])
        h = h + jnp.square(jax.nn.relu(m @ w_mlp_up[l])) @ w_mlp_down[l]
    return rmsnorm(h, final_norm_w)


_drawn_inputs = setup_inputs


def setup_inputs(seed=0):
    import zlib

    import numpy as np

    out = dict(_drawn_inputs(seed))
    spreads = {}
    factors = {'hgrn_out_norm_w': 15.557,
     'dsa_q_norm_w': 3.111,
     'dsa_kv_norm_w': 5.195,
     'dsa_kidx_norm_w': 3.577,
     'mem_norm_w': 8.0,
     'mlp_norm_w': 3.957}
    for name, (base, spread) in spreads.items():
        noise = np.random.default_rng([zlib.crc32(name.encode()), seed]).standard_normal(out[name].shape)
        drawn = base * np.exp(spread * noise) if base else spread * noise
        out[name] = __import__('jax').numpy.asarray(drawn.astype(out[name].dtype))
    for name, factor in factors.items():
        out[name] = (out[name] * factor).astype(out[name].dtype)
    return out
```

```python
from contextlib import ExitStack

import numpy as np

import concourse.bass as bass
from concourse import mybir

D = 1024
T = 512
M = 256
P = 128
KT = D // P
TT = T // P
MT = M // P
EPS = 1e-6
H = 4
C = 128
LEVELS = [64, 32, 16, 8, 4, 2, 1]
DH = 8
NOPE, ROPE, VD, LAT, QL = 64, 32, 64, 128, 256
IDX = 64
TOPK = 128
SM = QL + LAT + ROPE + IDX + DH
CKV, KR, KI, WI = QL, QL + LAT, QL + LAT + ROPE, QL + LAT + ROPE + IDX
DSA_SCALE = (NOPE + ROPE) ** -0.5
MEM_SCALE = P ** -0.5
NEG = -1.0e30
TAKEN = -3.0e38
FT = 4 * D // P
HALF = FT // 2

U_KM = 0
U_VM = U_KM + H
U_SMALL = U_VM + 4
U_MQ = U_SMALL + 4
U_HF = U_MQ + H
U_MERGE_MEM = U_HF + H
U_HQ = U_MERGE_MEM + 12
U_HG = U_HQ + H
U_HV = U_HG + H
U_MERGE_HG = U_HV + 4
U_MERGE_DSA = U_MERGE_HG + 12
U_OUT = U_MERGE_DSA + 12
U_MLP = U_OUT + 8
UNITS = U_MLP + 2 * (HALF + HALF)
STAGES = 2
SLOTS = 4

K_IDENT, K_ONES, K_TRI, K_TOP = 0, 128, 256, 384
N_CONST = 512
N_ROPE = TT * 192
V_ATTN, V_MEM, V_MLP, V_HG, V_LB = 0, 8, 16, 24, 28
N_COLS = 36
R_Q, R_KV, R_KI = 0, QL, QL + LAT
N_ROWS = QL + LAT + IDX
W_QI, W_QR, W_UQ, W_UK = 0, 1024, 1536, 2560
N_WDSA = 3072

ROUNDS = TOPK // 8
WIDTH = [P * (t + 1) for t in range(TT)]
BIAS_AT = [P * t * (t + 1) // 2 for t in range(TT)]
WORK_AT = [0, 0, WIDTH[1], WIDTH[1] + WIDTH[2]]


def bank_turns():
    uses, used, filled, turn = [], [0] * 8, [0] * 8, {}

    def use(key, bank, by_unit=False):
        turn[key] = (bank, used[bank], filled[bank])
        used[bank] += 1
        filled[bank] += not by_unit

    A, G, B = [0, 1, 2, 3], [4, 5], [6, 7]
    for k in range(KT):
        use(("memT", k), A[k % 4])
    for h in range(H):
        use(("km", h), G[h % 2], True)
    for mt in range(MT):
        use(("vm", mt), B[mt], True)
    for k in range(KT):
        use(("xT", k), (A + G)[k % 6])
    for t in range(TT):
        use(("small", t), A[t], True)
    for h in range(H):
        use(("mq", h), G[h % 2], True)
    for n in range(5):
        use(("smallT", n), A[n % 4])
    for t in range(TT):
        use(("qi", t), A[(1 + 2 * t) % 4])
        use(("qr", t), A[(2 + 2 * t) % 4])
    for h in range(H):
        use(("hf", h), G[h % 2], True)
        for half in range(2):
            g = 2 * h + half
            use(("mL", g), A[g % 2])
            use(("mP", g), A[2])
        use(("mO", h), A[3])
    for n in range(6):
        use(("qT", n), A[n % 4])
    for t in range(1, TT):
        for h in range(DH):
            use(("score", t, h), A[h % 4])
    for b in range(3):
        for j in range(KT):
            use(("gate", b, j), G[j % 2], True)
            use(("branch", b, j), B[j % 2], True)
        if b == 0:
            for h in range(H):
                use(("hq", h), G[h % 2], True)
            for n in range(len(LEVELS) + 1):
                for h in range(H):
                    use(("level", n, h), A[h])
            for h in range(H):
                use(("hg", h), G[h % 2], True)
            for t in range(TT):
                use(("hv", t), (G + B)[t], True)
            for h in range(H):
                use(("kdT", h), A[h])
            for h in range(H):
                use(("U", h), A[h])
            for h in range(H):
                use(("o", h), A[h])
            for h in range(H):
                use(("oss", h), A[h])
            for p in range(DH // 2):
                use(("qn", p), A[p])
            for h in range(DH):
                use(("qa", h), A[h % 4])
        if b == 1:
            for i in range(TT * DH):
                use(("S", i), A[i % 2])
                use(("PT", i), A[2])
                if i % 4 == 0:
                    use(("PV", i // 4), A[3])
            for p in range(DH // 2):
                use(("ob", p), A[p])
    for t in range(TT):
        use(("out", 0, t), A[t], True)
    for t in range(TT):
        use(("out", 1, t), (G + B)[t], True)
    for k in range(KT):
        use(("mT", k), (A + G + B)[k])
    for half in range(2):
        for f in range(HALF):
            use(("up", half, f), G[f % 2], True)
        for j in range(KT):
            use(("down", half, j), B[j % 2], True)
            if half:
                use(("yT", j), A[j % 2])
    return turn


def hybrid_block(nc, x, mem, stream, wdsa, wuv, const, rope, masks, cols, rows, last_row, out):
    f32, r32, u8 = mybir.dt.float32, mybir.dt.float32r, mybir.dt.uint8
    ALU, ACT, AX = mybir.AluOpType, mybir.ActivationFunctionType, mybir.AxisListType
    TURN = bank_turns()

    base = -(-nc.sbuf_base // 32) * 32
    top = [base]

    def place(name, shape, dt, at=None):
        size = int(np.prod(shape[1:])) * (1 if dt == u8 else 4)
        if at is None:
            at = top[0]
            top[0] += -(-size // 32) * 32
        return nc.alloc_sbuf_tensor_at(name, shape, dt, offset=at)

    stage = place("stage", [P, STAGES, D], f32)
    w_hi = place("w_hi", [P, SLOTS, D], r32)
    w_lo = place("w_lo", [P, SLOTS, D], r32)
    ACT_HI = top[0]
    act_hi = place("act_hi", [P, KT, T], r32)
    x_sq = place("x_sq", [P, D], f32, ACT_HI)
    act_lo = place("act_lo", [P, KT, T], r32)
    cst = place("cst", [P, N_CONST], f32)
    msk = place("msk", [P, len(LEVELS), P], u8)
    col = place("col", [P, N_COLS], f32)
    gate = place("gate", [P, 2, T], f32)
    stat = place("stat", [P, 192], f32)
    XR = top[0]
    xs = place("xs", [P, TT, D], f32)
    merged = place("merged", [P, KT, T], f32, XR)
    HB = top[0]
    top[0] += 8 * 8192
    R = [HB + 8192 * n for n in range(8)]
    DL = top[0]
    small = place("small", [P, TT, SM], f32)
    wd = place("wd", [P, N_WDSA], f32)
    cqT = place("cqT", [P, 2, T], f32)
    w_uv = place("w_uv", [P, DH * VD], f32)
    qrT = place("qrT", [P, 2, T], f32)
    ckvT = place("ckvT", [P, T], f32)
    krT = place("krT", [P, T], f32)
    kiT = place("kiT", [P, T], f32)
    WORK = top[0]
    work = place("work", [P, WIDTH[1] + WIDTH[2] + WIDTH[3]], f32)
    rp = place("rp", [P, TT, 192], f32, WORK)
    BIAS = top[0]
    bias = place("bias", [P, sum(WIDTH)], f32)
    row = place("row", [P, N_ROWS], f32, BIAS)
    memn = place("memn", [P, MT, D], f32, R[0])
    mn_hi = place("mn_hi", [P, KT, M], r32, R[4])
    mem_sq = place("mem_sq", [P, D], f32, R[4])
    mn_lo = place("mn_lo", [P, KT, M], r32, R[5])
    kmT = place("kmT", [P, H, M], f32, R[6])
    vm = place("vm", [P, MT, H * P], f32, R[6] + 4096)
    mqT = place("mqT", [P, H, T], f32, R[7])
    mP = place("mP", [P, 2, 2, M], f32, R[0])
    mPT = place("mPT", [P, 2, MT, 2 * P], f32, R[0] + 4096)
    oc_hi = place("oc_hi", [P, H, T], r32, R[1])
    oc_lo = place("oc_lo", [P, H, T], r32, R[2])
    qi_nat = place("qi_nat", [P, TT, DH * IDX], f32, R[4])
    qr_nat = place("qr_nat", [P, TT, DH * ROPE], f32, R[5])
    tmp1 = place("tmp1", [P, T], f32, R[5] + 4096)
    tmp2 = place("tmp2", [P, T], f32, R[5] + 6144)
    relu = place("relu", [P, 2, T], f32, R[5] + 4096)
    kr4 = place("kr4", [P, TT, P], f32, R[5])
    ki2 = place("ki2", [P, TT, P], f32, R[5] + 2048)
    qiT = place("qiT", [P, 4, T], f32, R[6])
    b = place("b", [P, H, T], f32, R[0])
    q = place("q", [P, H, T], f32, R[1])
    k = place("k", [P, H, T], f32, R[2])
    th = place("th", [P, H, T], f32, R[3])
    msk32 = place("msk32", [P, len(LEVELS), P], f32, R[3])
    v = place("v", [P, TT, H * P], f32, R[3])
    E = place("E", [P, H, T], f32, R[4])
    G = place("G", [P, H, T], f32, R[5])
    A = place("A", [P, H, T], f32, R[6])
    silu2 = place("silu2", [P, H, T], f32, R[7])
    kd = place("kd", [P, H, T], f32, R[4])
    S = place("S", [P, H, 3, P], f32, R[5])
    o = place("o", [P, H, T], f32, R[2])
    osq = place("osq", [P, H, T], f32, R[4])
    orstd = place("orstd", [P, H, T], f32, R[6])
    oa_hi = place("oa_hi", [P, H, T], r32, R[0])
    oa_lo = place("oa_lo", [P, H, T], r32, R[1])
    qa = place("qa", [P, DH, T], f32, R[4])
    qn = place("qn", [P, 4, T], f32, R[6])
    prob = place("prob", [P, 4, T], f32, R[6])
    probT = place("probT", [P, 4, T], f32, R[7])
    olat = place("olat", [P, DH, T], f32, R[2])
    ob_hi = place("ob_hi", [P, 4, T], r32, DL + TT * SM * 4)
    ob_lo = place("ob_lo", [P, 4, T], r32, DL + TT * SM * 4 + 8192)
    mg_hi = place("mg_hi", [P, KT, T], r32, R[0])
    mg_lo = place("mg_lo", [P, KT, T], r32, R[2])
    h1 = place("h1", [P, TT, D], f32, R[4])
    hn = place("hn", [P, TT, D], f32, R[6])
    u_hi = place("u_hi", [P, HALF, T], r32, R[0])
    u_lo = place("u_lo", [P, HALF, T], r32, DL)
    ypart = place("ypart", [P, KT, T], f32, R[6])
    ysum = place("ysum", [P, 2, T], f32, DL + 32768)
    fin_row = place("fin_row", [P, D], f32, DL + 32768 + 4096)
    res = place("res", [P, TT, D], f32, R[0])

    ident, ones = cst[:, K_IDENT:K_IDENT + P], cst[:, K_ONES:K_ONES + P]
    tri, top_mask = cst[:, K_TRI:K_TRI + P], cst[:, K_TOP:K_TOP + P]
    st = [0]

    def stats(n):
        st[0] += n
        return stat[:, st[0] - n:st[0]]

    m_ss, m_rs = stats(2), stats(2)
    x_ss, x_rs = stats(4), stats(4)
    s_ss = stats(12)
    s_rs = stats(12)
    lbx = stats(4 * 6)
    c0, c1 = stats(4), stats(4)
    m_max, m_nb, m_sum, m_inv = stats(16), stats(16), stats(16), stats(16)
    m8 = stats(8)
    d_max, d_sum, d_inv = stats(4), stats(4), stats(4)
    h_ss, h_rs = stats(4), stats(4)
    y_ss, y_rs = stats(4), stats(4)
    eps = stats(1)
    tick, tick_out = stats(1), stats(1)

    ctx = ExitStack()
    with ctx:
        bank = [ctx.enter_context(nc.psum_tensor(f"bank{n}", [P, T], f32)) for n in range(8)]

        def sem(name):
            return ctx.enter_context(nc.semaphore(name))

        stage_in = [sem(f"stage_in{n}") for n in range(STAGES)]
        hi_split, unit_split, unit_done = sem("hi_split"), sem("unit_split"), sem("unit_done")
        bank_full = [sem(f"bank_full{n}") for n in range(8)]
        bank_taken = [sem(f"bank_taken{n}") for n in range(8)]
        mem_in, const_in, rope_in, row_in = sem("mem_in"), sem("const_in"), sem("rope_in"), sem("row_in")
        x_in = [sem(f"x_in{t}") for t in range(TT)]
        wd_in, uv_in, xr_in, fin_in = sem("wd_in"), sem("uv_in"), sem("xr_in"), sem("fin_in")
        ticked = sem("ticked")
        dve_step, act_step = sem("dve_step"), sem("act_step")
        mem_squared, mem_mean, mem_rstd, mem_normed = (
            sem("mem_squared"), sem("mem_mean"), sem("mem_rstd"), sem("mem_normed"))
        x_squared, x_mean, x_rstd, x_normed = sem("x_squared"), sem("x_mean"), sem("x_rstd"), sem("x_normed")
        mem_hi_made, x_hi_made = sem("mem_hi_made"), sem("x_hi_made")
        small_squared, small_mean, small_rstd, small_ready = (
            sem("small_squared"), sem("small_mean"), sem("small_rstd"), sem("small_ready"))
        lb_diff, lb_exp = sem("lb_diff"), sem("lb_exp")
        q_roped = sem("q_roped")
        mem_maxed, mem_exped, mem_prob = sem("mem_maxed"), sem("mem_exped"), sem("mem_prob")
        oc_hi_made = sem("oc_hi_made")
        score_summed, bias_ready = sem("score_summed"), sem("bias_ready")
        gate_used, merged_added, merged_hi_made, merged_ready = (
            sem("gate_used"), sem("merged_added"), sem("merged_hi_made"), sem("merged_ready"))
        f_ready, log_f_ready, decay_ready = sem("f_ready"), sem("log_f_ready"), sem("decay_ready")
        diff_ready, exp_ready, G_ready, A_ready = (
            sem("diff_ready"), sem("exp_ready"), sem("G_ready"), sem("A_ready"))
        qd_ready, S_ready = sem("qd_ready"), sem("S_ready")
        silu_tanh = sem("silu_tanh")
        osq_ready, orstd_ready, oa_made, oa_hi_made, oa_ready = (
            sem("osq_ready"), sem("orstd_ready"), sem("oa_made"), sem("oa_hi_made"), sem("oa_ready"))
        logit_maxed, exped, prob_ready = sem("logit_maxed"), sem("exped"), sem("prob_ready")
        ob_hi_made = sem("ob_hi_made")
        h_squared, h_mean, h_rstd, h_normed, m_hi_made = (
            sem("h_squared"), sem("h_mean"), sem("h_rstd"), sem("h_normed"), sem("m_hi_made"))
        up_squared, up_hi_made, up_ready = sem("up_squared"), sem("up_hi_made"), sem("up_ready")
        y_squared, y_mean, y_rstd, res_ready, stored = (
            sem("y_squared"), sem("y_mean"), sem("y_rstd"), sem("res_ready"), sem("stored"))

        def full(e, key):
            n, _, fills = TURN[key]
            e.wait_ge(bank_full[n], fills + 1)

        def taken(e, key):
            n, uses, _ = TURN[key]
            e.wait_ge(bank_taken[n], uses + 1)

        def free(e, key):
            n, uses, _ = TURN[key]
            if uses:
                e.wait_ge(bank_taken[n], uses)

        def bank_of(key):
            return bank[TURN[key][0]]

        def take(instruction, key):
            instruction.then_inc(bank_taken[TURN[key][0]], 1)

        block = ctx.enter_context(nc.Block())

        @block.sync
        def _(sp):
            for u in range(STAGES):
                sp.dma_start(stage[:, u, :], stream[u]).then_inc(stage_in[u], 16)
            with sp.Fori(1, UNITS // STAGES) as i:
                for s in range(STAGES):
                    sp.wait_ge(unit_split, (i - 1) * STAGES + s + 1)
                    sp.dma_start(stage[:, s, :], stream[i * STAGES + s]).then_inc(stage_in[s], 16)
            for t in range(TT):
                sp.wait_ge(res_ready, t + 1)
                sp.dma_start(out[t * P:(t + 1) * P, :], res[:, t, :]).then_inc(stored, 16)
            sp.wait_ge(stored, 16 * TT)

        @block.gpsimd
        def _(pool):
            def split(u, s, first):
                g = s % STAGES
                pool.wait_ge(stage_in[g], (u // STAGES + 1) * 16 if first else (u - s) * 8 + (s // STAGES + 1) * 16)
                if not first:
                    pool.wait_ge(unit_done, u - (SLOTS - 1))
                    pool.wait_ge(ticked, u - (SLOTS - 1))
                    pool.tensor_tensor(tick_out, tick, tick, ALU.add).then_inc(ticked, 1)
                pool.tensor_scalar(w_hi[:, s, :], stage[:, g, :], 1.0, 1.0, ALU.mult, ALU.mult).then_inc(hi_split, 1)
                pool.wait_ge(hi_split, u + 1)
                pool.tensor_tensor(w_lo[:, s, :], stage[:, g, :], w_hi[:, s, :].bitcast(f32),
                                   ALU.subtract).then_inc(unit_split, 1)

            pool.memset(tick, 0.0).then_inc(ticked, 1)
            for s in range(SLOTS):
                split(s, s, True)
            with pool.Fori(1, UNITS // SLOTS) as i:
                for s in range(SLOTS):
                    split(i * SLOTS + s, s, False)

        @block.tensor
        def _(pe):
            def w(u):
                return u % SLOTS

            def three(out_ap, l_hi, l_lo, r_hi, r_lo, first, last):
                pe.matmul(out_ap, l_hi, r_hi, start=first, stop=False)
                pe.matmul(out_ap, l_hi, r_lo, start=False, stop=False)
                return pe.matmul(out_ap, l_lo, r_hi, start=False, stop=last)

            def t_unit(s, out_ap, a_hi, a_lo):
                for kk in range(KT):
                    ws = slice(kk * P, (kk + 1) * P)
                    last = three(out_ap, w_hi[:, s, ws], w_lo[:, s, ws], a_hi[:, kk, :], a_lo[:, kk, :],
                                 kk == 0, kk == KT - 1)
                last.then_inc(unit_done, 1)

            def n_unit(s, pair, pairs, outs, a_hi, a_lo, width):
                for kk in range(2):
                    kx = 2 * pair + kk
                    ws = slice(kk * 512, kk * 512 + width)
                    for t, out_ap in enumerate(outs):
                        ts = slice(t * P, (t + 1) * P)
                        last = three(out_ap, a_hi[:, kx, ts], a_lo[:, kx, ts], w_hi[:, s, ws], w_lo[:, s, ws],
                                     kx == 0, kx == 2 * pairs - 1)
                last.then_inc(unit_done, 1)

            def project(what, h, u0):
                pe.wait_ge(unit_split, u0 + h + 1)
                free(pe, (what, h))
                t_unit(w(u0 + h), bank_of((what, h))[:], act_hi, act_lo)

            def merge_unit(br, n, o_hi, o_lo, u0):
                pe.wait_ge(unit_split, u0 + n + 1)
                jp, part = n // 3, n % 3
                if part < 2:
                    j = 2 * jp + part
                    free(pe, ("gate", br, j))
                    t_unit(w(u0 + n), bank_of(("gate", br, j))[:], act_hi, act_lo)
                else:
                    for jj in range(2):
                        j = 2 * jp + jj
                        free(pe, ("branch", br, j))
                        for kk in range(4):
                            ws = slice((4 * jj + kk) * P, (4 * jj + kk + 1) * P)
                            last = three(bank_of(("branch", br, j))[:], w_hi[:, w(u0 + n), ws],
                                         w_lo[:, w(u0 + n), ws], o_hi[:, kk, :], o_lo[:, kk, :],
                                         kk == 0, kk == 3)
                    last.then_inc(unit_done, 1)

            def transposes(key, sources):
                free(pe, key)
                for n, src in enumerate(sources):
                    last = pe.transpose(bank_of(key)[:, n * P:(n + 1) * P], src, ident)
                last.then_inc(bank_full[TURN[key][0]], 1)

            def filled(instruction, key):
                instruction.then_inc(bank_full[TURN[key][0]], 1)

            pe.wait_ge(const_in, 48)
            pe.wait_ge(mem_normed, MT)
            for kk in range(KT):
                transposes(("memT", kk), [memn[:, mt, kk * P:(kk + 1) * P] for mt in range(MT)])
            for kk in range(KT):
                taken(pe, ("memT", kk))
            for h in range(H):
                pe.wait_ge(unit_split, U_KM + h + 1)
                free(pe, ("km", h))
                t_unit(w(U_KM + h), bank_of(("km", h))[:, 0:M], mn_hi, mn_lo)
            for n in range(4):
                pe.wait_ge(unit_split, U_VM + n + 1)
                n_unit(w(U_VM + n), n, 4, [bank_of(("vm", mt))[:] for mt in range(MT)], mn_hi, mn_lo, 512)
            pe.wait_ge(x_normed, TT)
            for kk in range(KT):
                transposes(("xT", kk), [xs[:, t, kk * P:(kk + 1) * P] for t in range(TT)])
            for kk in range(KT):
                taken(pe, ("xT", kk))
            for n in range(4):
                pe.wait_ge(unit_split, U_SMALL + n + 1)
                if n == 0:
                    for t in range(TT):
                        free(pe, ("small", t))
                n_unit(w(U_SMALL + n), n, 4, [bank_of(("small", t))[:, 0:SM] for t in range(TT)],
                       act_hi, act_lo, SM)
            for h in range(H):
                project("mq", h, U_MQ)
            pe.wait_ge(small_ready, 1)
            transposes(("smallT", 0), [small[:, t, 0:P] for t in range(TT)])
            transposes(("smallT", 1), [small[:, t, P:2 * P] for t in range(TT)])
            transposes(("smallT", 2), [small[:, t, CKV:CKV + P] for t in range(TT)])
            transposes(("smallT", 3), [kr4[:, t, :] for t in range(TT)])
            transposes(("smallT", 4), [ki2[:, t, :] for t in range(TT)])
            taken(pe, ("smallT", 0))
            taken(pe, ("smallT", 1))
            pe.wait_ge(wd_in, 16)
            for t in range(TT):
                for key, at, n in (("qi", W_QI, 512), ("qr", W_QR, 256)):
                    free(pe, (key, t))
                    for kk in range(2):
                        last = pe.matmul(bank_of((key, t))[:, 0:n], cqT[:, kk, t * P:(t + 1) * P],
                                         wd[:, at + kk * n:at + (kk + 1) * n], start=kk == 0, stop=kk == 1)
                    filled(last, (key, t))

            def mem_logits(g):
                h, half = g // 2, g % 2
                free(pe, ("mL", g))
                for n in range(2):
                    t = 2 * half + n
                    last = pe.matmul(bank_of(("mL", g))[:, n * M:(n + 1) * M], mqT[:, h, t * P:(t + 1) * P],
                                     kmT[:, h, :], start=True, stop=True)
                filled(last, ("mL", g))

            def mem_transposes(g):
                pe.wait_ge(mem_prob, g + 1)
                transposes(("mP", g), [mP[:, g % 2, n, mt * P:(mt + 1) * P] for mt in range(MT) for n in range(2)])

            def mem_values(g):
                h, half = g // 2, g % 2
                taken(pe, ("mP", g))
                if half == 0:
                    free(pe, ("mO", h))
                for mt in range(MT):
                    last = pe.matmul(bank_of(("mO", h))[:, half * M:(half + 1) * M],
                                     vm[:, mt, h * P:(h + 1) * P], mPT[:, g % 2, mt, :],
                                     start=mt == 0, stop=mt == MT - 1)
                if half:
                    filled(last, ("mO", h))

            taken(pe, ("mq", H - 2))
            taken(pe, ("mq", H - 1))
            taken(pe, ("km", H - 2))
            taken(pe, ("km", H - 1))
            taken(pe, ("vm", 0))
            taken(pe, ("vm", 1))
            mem_logits(0)
            mem_logits(1)
            for n in range(4):
                project("hf", n, U_HF)
                mem_transposes(2 * n)
                if n < 3:
                    mem_logits(2 * n + 2)
                mem_values(2 * n)
                mem_transposes(2 * n + 1)
                if n < 3:
                    mem_logits(2 * n + 3)
                mem_values(2 * n + 1)
            for n in range(4):
                pe.wait_ge(q_roped, TT)
                transposes(("qT", n), [qi_nat[:, t, n * P:(n + 1) * P] for t in range(TT)])
            for n in range(2):
                transposes(("qT", 4 + n), [qr_nat[:, t, n * P:(n + 1) * P] for t in range(TT)])
            taken(pe, ("smallT", 4))
            for n in range(4):
                taken(pe, ("qT", n))
            for p in range(2):
                taken(pe, ("mO", 2 * p + 1))
            scores = [(t, h) for t in range(1, TT) for h in range(DH)]
            for n in range(12):
                merge_unit(0, n, oc_hi, oc_lo, U_MERGE_MEM)
                for t, h in scores[2 * n:2 * n + 2]:
                    free(pe, ("score", t, h))
                    hs = slice(IDX * (h % 2), IDX * (h % 2) + IDX)
                    filled(pe.matmul(bank_of(("score", t, h))[:, 0:WIDTH[t]], qiT[hs, h // 2, t * P:(t + 1) * P],
                                     kiT[hs, 0:WIDTH[t]], start=True, stop=True), ("score", t, h))
            for h in range(H):
                project("hq", h, U_HQ)
            for n in range(len(LEVELS) + 1):
                diagonal = n == len(LEVELS)
                if not diagonal:
                    pe.wait_ge(G_ready, n + 1)
                for h in range(H):
                    free(pe, ("level", n, h))
                    for c in range(TT):
                        cs = slice(c * C, (c + 1) * C)
                        last = pe.matmul(bank_of(("level", n, h))[:, cs], (k if diagonal else G)[:, h, cs],
                                         (q if diagonal else G)[:, h, cs], start=True, stop=True)
                    filled(last, ("level", n, h))
                if n < H:
                    project("hg", n, U_HG)
                else:
                    pe.wait_ge(unit_split, U_HV + n - H + 1)
                    if n == H:
                        for t in range(TT):
                            free(pe, ("hv", t))
                    n_unit(w(U_HV + n - H), n - H, 4, [bank_of(("hv", t))[:] for t in range(TT)],
                           act_hi, act_lo, 512)
            pe.wait_ge(G_ready, len(LEVELS) + 1)
            for h in range(H):
                transposes(("kdT", h), [G[:, h, c * C:(c + 1) * C] for c in range(TT - 1)])
            for t in range(TT):
                taken(pe, ("hv", t))
            for h in range(H):
                taken(pe, ("kdT", h))
                free(pe, ("U", h))
                for c in range(TT - 1):
                    cs = slice(c * C, (c + 1) * C)
                    last = pe.matmul(bank_of(("U", h))[:, cs], kd[:, h, cs], v[:, c, h * P:(h + 1) * P],
                                     start=True, stop=True)
                filled(last, ("U", h))
            pe.wait_ge(A_ready, H)
            pe.wait_ge(qd_ready, 1)
            for h in range(H):
                free(pe, ("o", h))
                pe.wait_ge(S_ready, 3 * (h + 1))
                for c in range(TT):
                    cs = slice(c * C, (c + 1) * C)
                    last = pe.matmul(bank_of(("o", h))[:, cs], v[:, c, h * P:(h + 1) * P], A[:, h, cs],
                                     start=True, stop=c == 0)
                    if c:
                        last = pe.matmul(bank_of(("o", h))[:, cs], S[:, h, c - 1, :], q[:, h, cs],
                                         start=False, stop=True)
                filled(last, ("o", h))
            for h in range(H):
                pe.wait_ge(osq_ready, h + 1)
                free(pe, ("oss", h))
                filled(pe.matmul(bank_of(("oss", h))[:], ones, osq[:, h, :], start=True, stop=True), ("oss", h))
            for p in range(DH // 2):
                free(pe, ("qn", p))
                for kk in range(2):
                    last = pe.matmul(bank_of(("qn", p))[:], wd[:, W_UQ + kk * 512 + p * P:W_UQ + kk * 512 + (p + 1) * P],
                                     cqT[:, kk, :], start=kk == 0, stop=kk == 1)
                filled(last, ("qn", p))
            for h in range(DH):
                taken(pe, ("qn", h // 2))
                free(pe, ("qa", h))
                hs = slice(NOPE * (h % 2), NOPE * (h % 2) + NOPE)
                filled(pe.matmul(bank_of(("qa", h))[:], wd[hs, W_UK + (h // 2) * P:W_UK + (h // 2 + 1) * P],
                                 qn[hs, h // 2, :], start=True, stop=True), ("qa", h))

            def logits(i):
                t, h = i // DH, i % DH
                if i < DH:
                    taken(pe, ("qa", h))
                free(pe, ("S", i))
                out_ap = bank_of(("S", i))[:, 0:WIDTH[t]]
                rs = slice(ROPE * (h % 4), ROPE * (h % 4) + ROPE)
                pe.matmul(out_ap, qa[:, h, t * P:(t + 1) * P], ckvT[:, 0:WIDTH[t]], start=True, stop=False)
                filled(pe.matmul(out_ap, qrT[rs, h // 4, t * P:(t + 1) * P], krT[rs, 0:WIDTH[t]],
                                 start=False, stop=True), ("S", i))

            def prob_transposes(i):
                pe.wait_ge(prob_ready, i + 1)
                transposes(("PT", i), [prob[:, i % 4, s * P:(s + 1) * P] for s in range(i // DH + 1)])

            def latent_values(i):
                t, h = i // DH, i % DH
                taken(pe, ("PT", i))
                if i % 4 == 0:
                    free(pe, ("PV", i // 4))
                for s in range(t + 1):
                    last = pe.matmul(bank_of(("PV", i // 4))[:, (h % 4) * P:(h % 4 + 1) * P],
                                     small[:, s, CKV:CKV + LAT], probT[:, i % 4, s * P:(s + 1) * P],
                                     start=s == 0, stop=s == t)
                if i % 4 == 3:
                    filled(last, ("PV", i // 4))

            steps = TT * DH
            merge_at = {1: 0, 4: 1, 6: 2}
            logits(0)
            logits(1)
            pe.wait_ge(oa_ready, H)
            for i in range(steps):
                if i % 8 in merge_at:
                    merge_unit(1, 3 * (i // 8) + merge_at[i % 8], oa_hi, oa_lo, U_MERGE_HG)
                if i + 2 < steps:
                    logits(i + 2)
                prob_transposes(i)
                if i:
                    latent_values(i - 1)
            latent_values(steps - 1)
            pe.wait_ge(uv_in, 16)
            taken(pe, ("PV", steps // 4 - 1))
            for p in range(DH // 2):
                free(pe, ("ob", p))
                for n in range(2):
                    h = 2 * p + n
                    last = pe.matmul(bank_of(("ob", p))[VD * n:VD * (n + 1), :], w_uv[:, h * VD:(h + 1) * VD],
                                     olat[:, h, :], start=True, stop=True)
                filled(last, ("ob", p))
            for p in range(DH // 2):
                taken(pe, ("ob", p))
            for n in range(12):
                merge_unit(2, n, ob_hi, ob_lo, U_MERGE_DSA)
            for half in range(2):
                for n in range(4):
                    u = U_OUT + 4 * half + n
                    pe.wait_ge(unit_split, u + 1)
                    pe.wait_ge(merged_ready, 2 * n + 2)
                    if n == 0:
                        for t in range(TT):
                            free(pe, ("out", half, t))
                    n_unit(w(u), n, 4, [bank_of(("out", half, t))[:] for t in range(TT)], mg_hi, mg_lo, 512)
            pe.wait_ge(h_normed, TT)
            for kk in range(KT):
                transposes(("mT", kk), [hn[:, t, kk * P:(kk + 1) * P] for t in range(TT)])
            for kk in range(KT):
                taken(pe, ("mT", kk))
            for half in range(2):
                u_up = U_MLP + half * 2 * HALF
                u_down = u_up + HALF
                with pe.Fori(0, HALF // SLOTS) as i:
                    for s in range(SLOTS):
                        g, uses, _ = TURN["up", half, s]
                        pe.wait_ge(unit_split, i * SLOTS + (u_up + s + 1))
                        pe.wait_ge(bank_taken[g], i * (SLOTS // 2) + uses)
                        t_unit(s, bank[g][:], act_hi, act_lo)
                pe.wait_ge(up_ready, (half + 1) * HALF)

                def down_tile(i, n, half=half, u_down=u_down):
                    g, uses, _ = TURN["down", half, n]
                    for part in range(2):
                        s = 2 * n + part
                        pe.wait_ge(unit_split, i * SLOTS + (u_down + s + 1))
                        if part == 0:
                            pe.wait_ge(bank_taken[g], i + uses)
                        for kk in range(8):
                            ws = slice(kk * P, (kk + 1) * P)
                            f = 8 * part + kk
                            last = three(bank[g][:], w_hi[:, s, ws], w_lo[:, s, ws], u_hi[:, f, :], u_lo[:, f, :],
                                         f == 0, f == HALF - 1)
                        last.then_inc(unit_done, 1)

                def back(i, n):
                    g, uses, _ = TURN["down", 1, n]
                    a, a_uses, _ = TURN["yT", n]
                    pe.wait_ge(bank_taken[g], i + (uses + 1))
                    pe.wait_ge(bank_taken[a], i + a_uses)
                    for t in range(TT):
                        last = pe.transpose(bank[a][:, t * P:(t + 1) * P], ysum[:, n, t * P:(t + 1) * P], ident)
                    last.then_inc(bank_full[a], 1)

                if half == 0:
                    with pe.Fori(0, KT // 2) as i:
                        down_tile(i, 0)
                        down_tile(i, 1)
                else:
                    down_tile(0, 0)
                    down_tile(0, 1)
                    back(0, 0)
                    with pe.Fori(1, KT // 2) as i:
                        down_tile(i, 0)
                        back(i - 1, 1)
                        down_tile(i, 1)
                        back(i, 0)
                    back(KT // 2 - 1, 1)

        @block.scalar
        def _(act):
            count = [0]

            def link(instruction):
                count[0] += 1
                instruction.then_inc(act_step, 1)
                act.wait_ge(act_step, count[0])

            act.dma_start(memn[:], mem.rearrange("(n p) d -> p n d", p=P)).then_inc(mem_in, 16)
            act.dma_start(cst[:], const).then_inc(const_in, 16)
            act.dma_start(col[:], cols).then_inc(const_in, 16)
            act.dma_start(msk32[:], masks.rearrange("p (n c) -> p n c", c=P)).then_inc(const_in, 16)
            for t in range(TT):
                act.dma_start(xs[:, t, :], x[t * P:(t + 1) * P, :]).then_inc(x_in[t], 16)
            act.dma_start(rp[:], rope.rearrange("p (n c) -> p n c", c=192)).then_inc(rope_in, 16)
            act.dma_start(row[:], rows.to_broadcast([P, N_ROWS])).then_inc(row_in, 16)
            act.dma_start(wd[:], wdsa).then_inc(wd_in, 16)
            act.dma_start(w_uv[:], wuv).then_inc(uv_in, 16)

            def rstd(out_ap, in_ap, done):
                link(act.activation(out_ap, in_ap, ACT.Ln))
                act.activation(out_ap, out_ap, ACT.Exp, scale=-0.5).then_inc(done, 1)

            act.wait_ge(mem_in, 16)
            for mt in range(MT):
                link(act.activation(mem_sq[:], memn[:, mt, :], ACT.Square,
                                    accum_out=m_ss[:, mt:mt + 1]))
            act.activation(m_rs[:, 0:2], m_ss, ACT.Copy, scale=1.0 / D).then_inc(mem_squared, 1)
            act.wait_ge(mem_mean, 1)
            rstd(m_rs, m_rs, mem_rstd)
            act.wait_ge(const_in, 48)
            for kk in range(KT):
                full(act, ("memT", kk))
                act.activation(mn_hi[:, kk, :], bank_of(("memT", kk))[:, 0:M], ACT.Copy,
                               scale=col[:, V_MEM + kk:V_MEM + kk + 1]).then_inc(mem_hi_made, 1)
            for t in range(TT):
                act.wait_ge(x_in[t], 16)
                link(act.activation(x_sq[:], xs[:, t, :], ACT.Square,
                                    accum_out=x_ss[:, t:t + 1]))
            act.activation(x_rs, x_ss, ACT.Copy, scale=1.0 / D).then_inc(x_squared, 1)
            act.wait_ge(x_mean, 1)
            rstd(x_rs, x_rs, x_rstd)
            act.wait_ge(lb_diff, 1)
            act.activation(lbx[:, 12:20], lbx[:, 4:12], ACT.Exp).then_inc(lb_exp, 1)
            for h in range(H):
                act.wait_ge(unit_done, U_KM + h + 1)
                take(act.activation(kmT[:, h, :], bank_of(("km", h))[:, 0:M], ACT.Copy), ("km", h))
            for mt in range(MT):
                act.wait_ge(unit_done, U_VM + 4)
                take(act.activation(vm[:, mt, :], bank_of(("vm", mt))[:], ACT.Copy), ("vm", mt))
            for kk in range(KT):
                full(act, ("xT", kk))
                act.activation(act_hi[:, kk, :], bank_of(("xT", kk))[:], ACT.Copy,
                               scale=col[:, V_ATTN + kk:V_ATTN + kk + 1]).then_inc(x_hi_made, 1)
            for t in range(TT):
                act.wait_ge(unit_done, U_SMALL + 4)
                take(act.activation(small[:, t, :], bank_of(("small", t))[:, 0:SM], ACT.Copy), ("small", t))
                taken(act, ("small", t))
                for n, (at, size) in enumerate(((0, QL), (CKV, LAT), (KI, IDX))):
                    link(act.activation(tmp1[:, 0:size], small[:, t, at:at + size], ACT.Square,
                                        accum_out=s_ss[:, 3 * t + n:3 * t + n + 1]))
            act.activation(s_rs, s_ss, ACT.Copy).then_inc(small_squared, 1)
            act.wait_ge(small_mean, 1)
            rstd(s_rs, s_rs, small_rstd)
            for h in range(H):
                act.wait_ge(unit_done, U_MQ + h + 1)
                take(act.activation(mqT[:, h, :], bank_of(("mq", h))[:], ACT.Copy), ("mq", h))
            for n, dst in enumerate((cqT[:, 0, :], cqT[:, 1, :], ckvT[:], krT[:], kiT[:])):
                full(act, ("smallT", n))
                take(act.activation(dst, bank_of(("smallT", n))[:], ACT.Copy), ("smallT", n))

            def mem_exp(g):
                act.wait_ge(mem_maxed, g + 1)
                for n in range(2):
                    c = 2 * g + n
                    last = act.activation(mP[:, g % 2, n, :], bank_of(("mL", g))[:, n * M:(n + 1) * M], ACT.Exp,
                                          bias=m_nb[:, c:c + 1], scale=MEM_SCALE, accum_out=m_sum[:, c:c + 1])
                    if n == 0:
                        link(last)
                take(last, ("mL", g))

            def mem_copy(g):
                full(act, ("mP", g))
                take(act.activation(mPT[:, g % 2, :, :], bank_of(("mP", g))[:].rearrange("p (a c) -> p a c", a=2), ACT.Copy), ("mP", g))
                if g % 2:
                    full(act, ("mO", g // 2))
                    act.activation(oc_hi[:, g // 2, :], bank_of(("mO", g // 2))[:], ACT.Copy).then_inc(oc_hi_made, 1)

            def hf_tanh(h):
                act.wait_ge(unit_done, U_HF + h + 1)
                take(act.activation(th[:, h, :], bank_of(("hf", h))[:], ACT.Tanh, scale=0.5), ("hf", h))

            mem_exp(0)
            for g in range(1, 2 * H):
                if g >= 2:
                    full(act, ("mP", g - 2))
                mem_exp(g)
                mem_copy(g - 1)
                if g % 2:
                    hf_tanh(g // 2)
            mem_copy(2 * H - 1)
            for n in range(6):
                full(act, ("qT", n))
                dst = qiT[:, n, :] if n < 4 else qrT[:, n - 4, :]
                take(act.activation(dst, bank_of(("qT", n))[:], ACT.Copy), ("qT", n))

            def gate_tanh(br, j, u0):
                act.wait_ge(unit_done, u0 + 3 * (j // 2) + j % 2 + 1)
                if 8 * br + j >= 2:
                    act.wait_ge(gate_used, 8 * br + j - 1)
                take(act.activation(gate[:, j % 2, :], bank_of(("gate", br, j))[:], ACT.Tanh, scale=0.5),
                     ("gate", br, j))

            scores = [(t, h) for t in range(1, TT) for h in range(DH)]
            for n in range(12):
                if n % 3 < 2:
                    gate_tanh(0, 2 * (n // 3) + n % 3, U_MERGE_MEM)
                for m in (2 * n, 2 * n + 1):
                    t, h = scores[m]
                    full(act, ("score", t, h))
                    if m == 0:
                        act.wait_ge(q_roped, TT)
                    if m >= 2:
                        act.wait_ge(score_summed, m - 1)
                    take(act.activation(relu[:, m % 2, 0:WIDTH[t]], bank_of(("score", t, h))[:, 0:WIDTH[t]],
                                        ACT.Relu, scale=IDX ** -0.5), ("score", t, h))
            act.wait_ge(f_ready, 1)
            act.activation(b[:], b[:], ACT.Ln).then_inc(log_f_ready, 1)
            for h in range(H):
                act.wait_ge(unit_done, U_HQ + h + 1)
                take(act.activation(q[:, h, :], bank_of(("hq", h))[:], ACT.Copy), ("hq", h))
            for n, m in enumerate(LEVELS + [0]):
                act.wait_ge(diff_ready, n + 1)
                if m:
                    halves = E[:].rearrange("p h (n s m) -> p (h n) s m", s=2, m=m)
                    act.activation(halves[:, :, 0, :], halves[:, :, 0, :], ACT.Exp, scale=-1.0).then_inc(exp_ready, 1)
                    act.activation(halves[:, :, 1, :], halves[:, :, 1, :], ACT.Exp).then_inc(exp_ready, 1)
                else:
                    act.activation(E[:], E[:], ACT.Exp).then_inc(exp_ready, 2)
                if 1 <= n <= H:
                    act.wait_ge(unit_done, U_HG + n)
                    if n >= 3:
                        taken(act, ("hg", n - 3))
                    act.activation(gate[:, (n - 1) % 2, :], bank_of(("hg", n - 1))[:], ACT.Tanh,
                                   scale=0.5).then_inc(silu_tanh, 1)
            act.wait_ge(exp_ready, 2 * len(LEVELS) + 2)
            act.activation(b[:], b[:], ACT.Exp).then_inc(decay_ready, 1)
            for t in range(TT):
                act.wait_ge(unit_done, U_HV + 4)
                take(act.activation(v[:, t, :], bank_of(("hv", t))[:], ACT.Copy), ("hv", t))
            for h in range(H):
                full(act, ("kdT", h))
                act.wait_ge(G_ready, len(LEVELS) + 1)
                take(act.activation(kd[:, h, 0:3 * C], bank_of(("kdT", h))[:, 0:3 * C], ACT.Copy), ("kdT", h))
            for h in range(H):
                full(act, ("U", h))
            for h in range(H):
                full(act, ("o", h))
                act.activation(osq[:, h, :], bank_of(("o", h))[:], ACT.Square).then_inc(osq_ready, 1)
                take(act.activation(o[:, h, :], bank_of(("o", h))[:], ACT.Copy), ("o", h))
            for h in range(H):
                full(act, ("oss", h))
                take(act.activation(orstd[:, h, :], bank_of(("oss", h))[:], ACT.Ln, scale=1.0 / P, bias=eps),
                     ("oss", h))
            for h in range(H):
                taken(act, ("oss", h))
                act.activation(orstd[:, h, :], orstd[:, h, :], ACT.Exp, scale=-0.5).then_inc(orstd_ready, 1)
            for h in range(H):
                act.wait_ge(oa_made, h + 1)
                act.activation(oa_hi[:, h, :], o[:, h, :], ACT.Copy).then_inc(oa_hi_made, 1)
            act.wait_ge(oa_made, H)
            for p in range(DH // 2):
                full(act, ("qn", p))
                take(act.activation(qn[:, p, :], bank_of(("qn", p))[:], ACT.Copy), ("qn", p))
            for h in range(DH):
                full(act, ("qa", h))
                take(act.activation(qa[:, h, :], bank_of(("qa", h))[:], ACT.Copy), ("qa", h))

            steps = TT * DH

            def sparse_exp(i):
                t = i // DH
                act.wait_ge(logit_maxed, i + 1)
                act.activation(prob[:, i % 4, 0:WIDTH[t]], prob[:, i % 4, 0:WIDTH[t]], ACT.Exp,
                               bias=d_max[:, i % 4:i % 4 + 1], accum_out=d_sum[:, i % 4:i % 4 + 1]).then_inc(exped, 1)

            def sparse_copy(i):
                t = i // DH
                full(act, ("PT", i))
                if i >= 8 and i % 4 == 0:
                    full(act, ("PV", i // 4 - 1))
                take(act.activation(probT[:, i % 4, 0:WIDTH[t]], bank_of(("PT", i))[:, 0:WIDTH[t]], ACT.Copy),
                     ("PT", i))
                if i % 4 == 3:
                    g = i // 4
                    full(act, ("PV", g))
                    hs, ts = 4 * (g % 2), slice((g // 2) * P, (g // 2 + 1) * P)
                    take(act.activation(olat[:, hs:hs + 4, ts], bank_of(("PV", g))[:].rearrange("p (a c) -> p a c", a=4), ACT.Copy), ("PV", g))

            merge_at = {1: 0, 4: 1}
            sparse_exp(0)
            sparse_exp(1)
            for i in range(steps):
                if i % 8 in merge_at:
                    gate_tanh(1, 2 * (i // 8) + merge_at[i % 8], U_MERGE_HG)
                sparse_copy(i)
                if i + 2 < steps:
                    sparse_exp(i + 2)
            for p in range(DH // 2):
                full(act, ("ob", p))
                act.activation(ob_hi[:, p, :], bank_of(("ob", p))[:], ACT.Copy).then_inc(ob_hi_made, 1)
            act.dma_start(h1[:], x.rearrange("(n p) d -> p n d", p=P)).then_inc(xr_in, 16)
            for n in range(12):
                if n % 3 < 2:
                    gate_tanh(2, 2 * (n // 3) + n % 3, U_MERGE_DSA)
                else:
                    for j in (2 * (n // 3), 2 * (n // 3) + 1):
                        act.wait_ge(merged_added, KT + j + 1)
                        act.activation(mg_hi[:, j, :], merged[:, j, :], ACT.Copy, scale=0.5).then_inc(merged_hi_made, 1)
            act.dma_start(fin_row[:], last_row.to_broadcast([P, D])).then_inc(fin_in, 16)
            for t in range(TT):
                taken(act, ("out", 1, t))
                link(act.activation(hn[:, t, :], h1[:, t, :], ACT.Square, accum_out=h_ss[:, t:t + 1]))
            act.activation(h_rs, h_ss, ACT.Copy, scale=1.0 / D).then_inc(h_squared, 1)
            act.wait_ge(h_mean, 1)
            rstd(h_rs, h_rs, h_rstd)
            for kk in range(KT):
                full(act, ("mT", kk))
                act.activation(act_hi[:, kk, :], bank_of(("mT", kk))[:], ACT.Copy,
                               scale=col[:, V_MLP + kk:V_MLP + kk + 1]).then_inc(m_hi_made, 1)
            for half in range(2):
                u_up = U_MLP + half * 2 * HALF

                def relu_tile(i, s, first, half=half, u_up=u_up):
                    g, _, _ = TURN["up", half, s]
                    act.wait_ge(unit_done, i * SLOTS + (u_up + s + 1))
                    if not first:
                        act.wait_ge(up_ready, i * SLOTS + (half * HALF + s - 1))
                    act.activation(gate[:, s % 2, :], bank[g][:], ACT.Relu).then_inc(bank_taken[g], 1)

                def hi_tile(i, s, half=half):
                    act.wait_ge(up_squared, i * SLOTS + (half * HALF + s + 1))
                    act.activation(u_hi[:, i * SLOTS + s, :], gate[:, s % 2, :], ACT.Copy).then_inc(up_hi_made, 1)

                for s in range(SLOTS):
                    relu_tile(0, s, s < 2 and half == 0)
                    hi_tile(0, s)
                with act.Fori(1, HALF // SLOTS) as i:
                    for s in range(SLOTS):
                        relu_tile(i, s, False)
                        hi_tile(i, s)
                if half == 0:
                    u_down = u_up + HALF
                    with act.Fori(0, KT // 2) as i:
                        for n in range(2):
                            g, _, _ = TURN["down", 0, n]
                            act.wait_ge(unit_done, i * SLOTS + (u_down + 2 * n + 2))
                            act.activation(ypart[:, i * 2 + n, :], bank[g][:], ACT.Copy).then_inc(bank_taken[g], 1)
            for n in range(2):
                taken(act, ("yT", KT - 2 + n))
            for t in range(TT):
                link(act.activation(res[:, t, :], h1[:, t, :], ACT.Square, accum_out=y_ss[:, t:t + 1]))
                act.activation(y_rs[:, t:t + 1], y_ss[:, t:t + 1], ACT.Copy, scale=1.0 / D).then_inc(y_squared, 1)
            for t in range(TT):
                act.wait_ge(y_mean, t + 1)
                rstd(y_rs[:, t:t + 1], y_rs[:, t:t + 1], y_rstd)

        @block.vector
        def _(dve):
            count = [0]

            def link(instruction):
                count[0] += 1
                instruction.then_inc(dve_step, 1)
                dve.wait_ge(dve_step, count[0])

            link(dve.memset(eps, EPS))
            dve.wait_ge(const_in, 48)
            link(dve.tensor_copy(msk[:], msk32[:]))
            dve.wait_ge(mem_squared, 1)
            dve.tensor_scalar(m_rs, m_rs, EPS, None, ALU.add).then_inc(mem_mean, 1)
            dve.wait_ge(mem_rstd, 1)
            for mt in range(MT):
                dve.tensor_scalar(memn[:, mt, :], memn[:, mt, :], m_rs[:, mt:mt + 1], None,
                                  ALU.mult).then_inc(mem_normed, 1)
            dve.wait_ge(const_in, 48)
            a0, a1 = col[:, V_LB:V_LB + 4], col[:, V_LB + 4:V_LB + 8]
            link(dve.tensor_tensor(lbx[:, 0:4], a0, a1, ALU.max))
            link(dve.tensor_tensor(lbx[:, 4:8], a0, lbx[:, 0:4], ALU.subtract))
            dve.tensor_tensor(lbx[:, 8:12], a1, lbx[:, 0:4], ALU.subtract).then_inc(lb_diff, 1)
            for kk in range(KT):
                dve.wait_ge(mem_hi_made, kk + 1)
                take(dve.scalar_tensor_tensor(mn_lo[:, kk, :], bank_of(("memT", kk))[:, 0:M],
                                              col[:, V_MEM + kk:V_MEM + kk + 1], mn_hi[:, kk, :].bitcast(f32),
                                              ALU.mult, ALU.subtract), ("memT", kk))
            dve.wait_ge(x_squared, 1)
            dve.tensor_scalar(x_rs, x_rs, EPS, None, ALU.add).then_inc(x_mean, 1)
            dve.wait_ge(x_rstd, 1)
            for t in range(TT):
                dve.tensor_scalar(xs[:, t, :], xs[:, t, :], x_rs[:, t:t + 1], None, ALU.mult).then_inc(x_normed, 1)
            dve.wait_ge(lb_exp, 1)
            link(dve.tensor_tensor(lbx[:, 20:24], lbx[:, 12:16], lbx[:, 16:20], ALU.add))
            link(dve.reciprocal(lbx[:, 20:24], lbx[:, 20:24]))
            link(dve.tensor_tensor(lbx[:, 0:4], lbx[:, 12:16], lbx[:, 20:24], ALU.mult))
            link(dve.tensor_scalar(c1, lbx[:, 0:4], -0.5, 0.5, ALU.mult, ALU.add))
            link(dve.tensor_tensor(c0, lbx[:, 0:4], c1, ALU.add))
            for kk in range(KT):
                dve.wait_ge(x_hi_made, kk + 1)
                take(dve.scalar_tensor_tensor(act_lo[:, kk, :], bank_of(("xT", kk))[:],
                                              col[:, V_ATTN + kk:V_ATTN + kk + 1], act_hi[:, kk, :].bitcast(f32),
                                              ALU.mult, ALU.subtract), ("xT", kk))
            dve.wait_ge(small_squared, 1)
            rs3 = s_rs.rearrange("p (t n) -> p t n", n=3)
            for n, size in enumerate((QL, LAT, IDX)):
                last = dve.tensor_scalar(rs3[:, :, n], rs3[:, :, n], 1.0 / size, EPS, ALU.mult, ALU.add)
                if n < 2:
                    link(last)
            last.then_inc(small_mean, 1)
            dve.wait_ge(small_rstd, 1)
            dve.wait_ge(row_in, 16)
            dve.wait_ge(rope_in, 16)
            for n, (at, size, r0) in enumerate(((0, QL, R_Q), (CKV, LAT, R_KV), (KI, IDX, R_KI))):
                for t in range(TT):
                    part = small[:, t, at:at + size]
                    link(dve.scalar_tensor_tensor(part, part, s_rs[:, 3 * t + n:3 * t + n + 1],
                                                  row[:, r0:r0 + size], ALU.mult, ALU.mult))

            def rotate(dst, src, cc, ss, half, t1, t2):
                link(dve.tensor_tensor(t1, src, cc, ALU.mult))
                link(dve.tensor_tensor(t2[..., 0:half], src[..., half:2 * half], ss[..., 0:half], ALU.mult))
                link(dve.tensor_tensor(t2[..., half:2 * half], src[..., 0:half], ss[..., half:2 * half], ALU.mult))
                return dve.tensor_tensor(dst, t1, t2, ALU.add)

            link(rotate(kr4[:, :, 0:ROPE], small[:, :, KR:KR + ROPE], rp[:, :, 128:160], rp[:, :, 160:192], ROPE // 2,
                        tmp1[:, 0:TT * ROPE].rearrange("p (t c) -> p t c", c=ROPE),
                        tmp2[:, 0:TT * ROPE].rearrange("p (t c) -> p t c", c=ROPE)))
            link(dve.tensor_copy(kr4[:, :, ROPE:2 * ROPE], kr4[:, :, 0:ROPE]))
            link(dve.tensor_copy(kr4[:, :, 2 * ROPE:4 * ROPE], kr4[:, :, 0:2 * ROPE]))
            link(rotate(ki2[:, :, 0:IDX], small[:, :, KI:KI + IDX], rp[:, :, 0:64], rp[:, :, 64:128], IDX // 2,
                        tmp1[:, 0:TT * IDX].rearrange("p (t c) -> p t c", c=IDX),
                        tmp2[:, 0:TT * IDX].rearrange("p (t c) -> p t c", c=IDX)))
            link(dve.tensor_copy(ki2[:, :, IDX:2 * IDX], ki2[:, :, 0:IDX]))
            dve.tensor_scalar(small[:, :, WI:WI + DH], small[:, :, WI:WI + DH], DH ** -0.5, None,
                              ALU.mult).then_inc(small_ready, 1)

            full_small = [("smallT", 3), ("smallT", 4)]
            for key in full_small:
                full(dve, key)
            for t in range(TT):
                for key, dst, width, at in (("qi", qi_nat, IDX, 0), ("qr", qr_nat, ROPE, 128)):
                    full(dve, (key, t))
                    heads = lambda ap: ap.rearrange("p (h c) -> p h c", c=width)
                    n = DH * width
                    cc = rp[:, t, at:at + width].unsqueeze(1).to_broadcast([P, DH, width])
                    ss = rp[:, t, at + width:at + 2 * width].unsqueeze(1).to_broadcast([P, DH, width])
                    src = heads(bank_of((key, t))[:, 0:n])
                    t1, t2 = heads(tmp1[:, 0:n]), heads(tmp2[:, 0:n])
                    half = width // 2
                    link(dve.tensor_tensor(t1, src, cc, ALU.mult))
                    link(dve.tensor_tensor(t2[:, :, 0:half], src[:, :, half:width], ss[:, :, 0:half], ALU.mult))
                    take(dve.tensor_tensor(t2[:, :, half:width], src[:, :, 0:half], ss[:, :, half:width], ALU.mult),
                         (key, t))
                    taken(dve, (key, t))
                    last = dve.tensor_tensor(heads(dst[:, t, :]), t1, t2, ALU.add)
                    if key == "qi":
                        link(last)
                last.then_inc(q_roped, 1)
                dve.wait_ge(q_roped, t + 1)

            def mem_max(g):
                full(dve, ("mL", g))
                cs = slice(2 * g, 2 * g + 2)
                link(dve.tensor_reduce(m_max[:, cs], bank_of(("mL", g))[:].rearrange("p (a c) -> p a c", a=2),
                                       axis=AX.X, op=ALU.max))
                dve.tensor_scalar(m_nb[:, cs], m_max[:, cs], -MEM_SCALE, None, ALU.mult).then_inc(mem_maxed, 1)

            def mem_norm(g):
                taken(dve, ("mL", g))
                cs = slice(2 * g, 2 * g + 2)
                link(dve.reciprocal(m_inv[:, cs], m_sum[:, cs]))
                for n in range(2):
                    c = 2 * g + n
                    last = dve.tensor_scalar(mP[:, g % 2, n, :], mP[:, g % 2, n, :], m_inv[:, c:c + 1], None, ALU.mult)
                    if n == 0:
                        link(last)
                last.then_inc(mem_prob, 1)
                if g >= 3 and g % 2:
                    oc_low(g // 2 - 1)

            def oc_low(h):
                dve.wait_ge(oc_hi_made, h + 1)
                take(dve.tensor_tensor(oc_lo[:, h, :], bank_of(("mO", h))[:], oc_hi[:, h, :].bitcast(f32),
                                       ALU.subtract), ("mO", h))

            mem_max(0)
            mem_max(1)
            for g in range(2 * H):
                mem_norm(g)
                if g + 2 < 2 * H:
                    mem_max(g + 2)
            oc_low(H - 1)

            def gated(br, j, u0):
                taken(dve, ("gate", br, j))
                dve.wait_ge(unit_done, u0 + 3 * (j // 2) + 3)
                if br == 0:
                    take(dve.scalar_tensor_tensor(merged[:, j, :], gate[:, j % 2, :], 1.0,
                                                  bank_of(("branch", br, j))[:], ALU.add, ALU.mult), ("branch", br, j))
                    dve.memset(lbx[:, 0:1], 0.0).then_inc(gate_used, 1)
                else:
                    take(dve.scalar_tensor_tensor(gate[:, j % 2, :], gate[:, j % 2, :], 1.0,
                                                  bank_of(("branch", br, j))[:], ALU.add, ALU.mult), ("branch", br, j))
                    taken(dve, ("branch", br, j))
                    link(dve.tensor_tensor(merged[:, j, :], merged[:, j, :], gate[:, j % 2, :], ALU.add))
                    dve.memset(lbx[:, 0:1], 0.0).then_inc(gate_used, 1)
                dve.wait_ge(gate_used, 8 * br + j + 1)

            scores = [(t, h) for t in range(1, TT) for h in range(DH)]
            dve.wait_ge(x_normed, TT)

            def keys_of(t):
                return work[:, WORK_AT[t]:WORK_AT[t] + WIDTH[t]]

            def topk_round(t, r):
                if r == 0:
                    own = keys_of(t)[:, t * P:WIDTH[t]]
                    link(dve.tensor_tensor(own, own, tri, ALU.add))
                link(dve.max(m8, keys_of(t)))
                link(dve.match_replace(keys_of(t), m8, keys_of(t), TAKEN))
                if r == ROUNDS - 1:
                    link(dve.tensor_scalar(bias[:, BIAS_AT[t]:BIAS_AT[t] + WIDTH[t]], keys_of(t), TAKEN, NEG,
                                           ALU.not_equal, ALU.mult))

            link(dve.tensor_copy(bias[:, 0:P], tri))
            for n in range(12):
                if n % 3 == 2:
                    for jj in range(2):
                        gated(0, 2 * (n // 3) + jj, U_MERGE_MEM)
                for m in (2 * n, 2 * n + 1):
                    t, h = scores[m]
                    taken(dve, ("score", t, h))
                    acc = work[:, WORK_AT[t]:WORK_AT[t] + WIDTH[t]]
                    wi = small[:, t, WI + h:WI + h + 1]
                    if h == 0:
                        dve.tensor_scalar(acc, relu[:, m % 2, 0:WIDTH[t]], wi, None, ALU.mult).then_inc(score_summed, 1)
                    else:
                        dve.scalar_tensor_tensor(acc, relu[:, m % 2, 0:WIDTH[t]], wi, acc, ALU.mult,
                                                 ALU.add).then_inc(score_summed, 1)
                    dve.wait_ge(score_summed, m + 1)
                    if t > 1:
                        for r in range(2 * h, 2 * h + 2):
                            topk_round(t - 1, r)
            for h in range(H):
                taken(dve, ("hf", h))
                link(dve.tensor_scalar(b[:, h, :], th[:, h, :], c1[:, h:h + 1], c0[:, h:h + 1], ALU.mult, ALU.add))
                last = dve.tensor_scalar(k[:, h, :], b[:, h, :], -1.0, 1.0, ALU.mult, ALU.add)
                if h < H - 1:
                    link(last)
            last.then_inc(f_ready, 1)
            dve.wait_ge(log_f_ready, 1)
            for h in range(H):
                for c in range(TT):
                    seg = b[:, h, c * C:(c + 1) * C]
                    link(dve.tensor_tensor_scan(seg, ones, seg, 0.0, ALU.mult, ALU.add))

            for r in range(ROUNDS // 2):
                topk_round(TT - 1, r)

            def differences(n):
                m = (LEVELS + [0])[n]
                if m:
                    pairs = b[:].rearrange("p h (n m) -> p (h n) m", m=2 * m)
                    ref = pairs[:, :, m - 1:m].to_broadcast([P, H * T // (2 * m), 2 * m])
                    dve.tensor_tensor(E[:].rearrange("p h (n m) -> p (h n) m", m=2 * m), pairs, ref,
                                      ALU.subtract).then_inc(diff_ready, 1)
                else:
                    chunks = b[:].rearrange("p h (n m) -> p (h n) m", m=C)
                    ref = chunks[:, :, C - 1:C].to_broadcast([P, H * TT, C])
                    dve.tensor_tensor(E[:].rearrange("p h (n m) -> p (h n) m", m=C), ref, chunks,
                                      ALU.subtract).then_inc(diff_ready, 1)

            for h in range(H):
                taken(dve, ("hq", h))
            differences(0)
            for n, m in enumerate(LEVELS):
                dve.wait_ge(exp_ready, 2 * n + 2)
                if n:
                    for h in range(H):
                        full(dve, ("level", n - 1, h))
                view = lambda ap: ap[:].rearrange("p h (n s m) -> p (h n) s m", s=2, m=m)
                link(dve.tensor_tensor(view(G)[:, :, 0, :], view(k)[:, :, 0, :], view(E)[:, :, 0, :], ALU.mult))
                dve.tensor_tensor(view(G)[:, :, 1, :], view(q)[:, :, 1, :], view(E)[:, :, 1, :],
                                  ALU.mult).then_inc(G_ready, 1)
                dve.wait_ge(G_ready, n + 1)
                differences(n + 1)
                if 1 <= n <= H:
                    dve.wait_ge(silu_tanh, n)
                    take(dve.scalar_tensor_tensor(silu2[:, n - 1, :], gate[:, (n - 1) % 2, :], 1.0,
                                                  bank_of(("hg", n - 1))[:], ALU.add, ALU.mult), ("hg", n - 1))
                for h in range(H):
                    full(dve, ("level", n, h))
                    src = bank_of(("level", n, h))[:].rearrange("p (c m) -> p c m", m=C)
                    dst = A[:, h, :].rearrange("p (c m) -> p c m", m=C)
                    if n == 0:
                        take(dve.tensor_tensor(dst, src, top_mask.unsqueeze(1).to_broadcast([P, TT, C]), ALU.mult),
                             ("level", n, h))
                    else:
                        take(dve.copy_predicated(dst, msk[:, n - 1, :].unsqueeze(1).to_broadcast([P, TT, C]), src),
                             ("level", n, h))
                    taken(dve, ("level", n, h))
            n = len(LEVELS)
            for h in range(H):
                full(dve, ("level", n, h))
                src = bank_of(("level", n, h))[:].rearrange("p (c m) -> p c m", m=C)
                dst = A[:, h, :].rearrange("p (c m) -> p c m", m=C)
                take(dve.copy_predicated(dst, msk[:, n - 1, :].unsqueeze(1).to_broadcast([P, TT, C]), src),
                     ("level", n, h))
                taken(dve, ("level", n, h))
            link(dve.memset(lbx[:, 0:1], 0.0))
            dve.memset(lbx[:, 0:1], 0.0).then_inc(A_ready, H)
            dve.wait_ge(exp_ready, 2 * len(LEVELS) + 2)
            dve.tensor_tensor(G[:], k[:], E[:], ALU.mult).then_inc(G_ready, 1)
            dve.wait_ge(decay_ready, 1)
            dve.tensor_tensor(q[:], q[:], b[:], ALU.mult).then_inc(qd_ready, 1)
            for h in range(H):
                full(dve, ("kdT", h))
            for h in range(H):
                full(dve, ("U", h))
                for c in range(TT - 1):
                    got = bank_of(("U", h))[:, c * C:(c + 1) * C]
                    if c == 0:
                        last = dve.tensor_copy(S[:, h, c, :], got)
                    else:
                        last = dve.scalar_tensor_tensor(S[:, h, c, :], S[:, h, c - 1, :],
                                                        b[:, h, (c + 1) * C - 1:(c + 1) * C], got, ALU.mult, ALU.add)
                    last.then_inc(S_ready, 1)
                    dve.wait_ge(S_ready, 3 * h + c + 1)
                take(dve.memset(lbx[:, 0:1], 0.0), ("U", h))
                taken(dve, ("U", h))
            for h in range(H):
                dve.wait_ge(orstd_ready, h + 1)
                link(dve.scalar_tensor_tensor(o[:, h, :], o[:, h, :], col[:, V_HG + h:V_HG + h + 1],
                                              orstd[:, h, :], ALU.mult, ALU.mult))
                dve.scalar_tensor_tensor(o[:, h, :], o[:, h, :], 0.5, silu2[:, h, :], ALU.mult,
                                         ALU.mult).then_inc(oa_made, 1)
            for h in range(H):
                dve.wait_ge(oa_hi_made, h + 1)
                dve.tensor_tensor(oa_lo[:, h, :], o[:, h, :], oa_hi[:, h, :].bitcast(f32),
                                  ALU.subtract).then_inc(oa_ready, 1)

            steps = TT * DH

            def masked_max(i):
                t = i // DH
                full(dve, ("S", i))
                if i >= 4:
                    full(dve, ("PT", i - 4))
                p = prob[:, i % 4, 0:WIDTH[t]]
                take(dve.scalar_tensor_tensor(p, bank_of(("S", i))[:, 0:WIDTH[t]], DSA_SCALE,
                                              bias[:, BIAS_AT[t]:BIAS_AT[t] + WIDTH[t]], ALU.mult, ALU.add), ("S", i))
                taken(dve, ("S", i))
                dve.tensor_reduce(d_max[:, i % 4:i % 4 + 1], p, axis=AX.X, op=ALU.max, negate=True).then_inc(logit_maxed, 1)

            def normalise(i):
                t = i // DH
                dve.wait_ge(exped, i + 1)
                link(dve.reciprocal(d_inv[:, i % 4:i % 4 + 1], d_sum[:, i % 4:i % 4 + 1]))
                p = prob[:, i % 4, 0:WIDTH[t]]
                dve.tensor_scalar(p, p, d_inv[:, i % 4:i % 4 + 1], None, ALU.mult).then_inc(prob_ready, 1)

            for h in range(DH):
                taken(dve, ("qa", h))
            masked_max(0)
            masked_max(1)
            for i in range(steps):
                if i % 8 == 6:
                    for jj in range(2):
                        gated(1, 2 * (i // 8) + jj, U_MERGE_HG)
                normalise(i)
                if i + 2 < steps:
                    masked_max(i + 2)
                if i < ROUNDS // 2:
                    topk_round(TT - 1, ROUNDS // 2 + i)
            for p in range(DH // 2):
                dve.wait_ge(ob_hi_made, p + 1)
                take(dve.tensor_tensor(ob_lo[:, p, :], bank_of(("ob", p))[:], ob_hi[:, p, :].bitcast(f32),
                                       ALU.subtract), ("ob", p))
            for jp in range(4):
                for j in (2 * jp, 2 * jp + 1):
                    gated(2, j, U_MERGE_DSA)
                    dve.memset(lbx[:, 0:1], 0.0).then_inc(merged_added, KT + 1 if j == 0 else 1)
                for j in (2 * jp, 2 * jp + 1):
                    dve.wait_ge(merged_hi_made, j + 1)
                    dve.scalar_tensor_tensor(mg_lo[:, j, :], merged[:, j, :], 0.5, mg_hi[:, j, :].bitcast(f32),
                                             ALU.mult, ALU.subtract).then_inc(merged_ready, 1)
            dve.wait_ge(xr_in, 16)
            for half in range(2):
                dve.wait_ge(unit_done, U_OUT + 4 * half + 4)
                for t in range(TT):
                    part = h1[:, t, half * 512:(half + 1) * 512]
                    take(dve.tensor_tensor(part, part, bank_of(("out", half, t))[:], ALU.add), ("out", half, t))
            dve.wait_ge(h_squared, 1)
            dve.tensor_scalar(h_rs, h_rs, EPS, None, ALU.add).then_inc(h_mean, 1)
            dve.wait_ge(h_rstd, 1)
            for t in range(TT):
                dve.tensor_scalar(hn[:, t, :], h1[:, t, :], h_rs[:, t:t + 1], None, ALU.mult).then_inc(h_normed, 1)
            for kk in range(KT):
                dve.wait_ge(m_hi_made, kk + 1)
                take(dve.scalar_tensor_tensor(act_lo[:, kk, :], bank_of(("mT", kk))[:],
                                              col[:, V_MLP + kk:V_MLP + kk + 1], act_hi[:, kk, :].bitcast(f32),
                                              ALU.mult, ALU.subtract), ("mT", kk))
            for half in range(2):
                with dve.Fori(0, HALF // SLOTS) as i:
                    for s in range(SLOTS):
                        g, uses, _ = TURN["up", half, s]
                        dve.wait_ge(bank_taken[g], i * (SLOTS // 2) + (uses + 1))
                        dve.tensor_tensor(gate[:, s % 2, :], gate[:, s % 2, :], gate[:, s % 2, :],
                                          ALU.mult).then_inc(up_squared, 1)
                        dve.wait_ge(up_hi_made, i * SLOTS + (half * HALF + s + 1))
                        dve.tensor_tensor(u_lo[:, i * SLOTS + s, :], gate[:, s % 2, :],
                                          u_hi[:, i * SLOTS + s, :].bitcast(f32), ALU.subtract).then_inc(up_ready, 1)
            u_down = U_MLP + 3 * HALF

            def sum_tile(i, n, first):
                g, _, _ = TURN["down", 1, n]
                a, a_uses, a_fills = TURN["yT", n]
                dve.wait_ge(unit_done, i * SLOTS + (u_down + 2 * n + 2))
                if not first:
                    dve.wait_ge(bank_full[a], i + a_fills)
                dve.tensor_tensor(ysum[:, n, :], bank[g][:], ypart[:, i * 2 + n, :], ALU.add).then_inc(bank_taken[g], 1)

            def residual(i, n):
                a, _, a_fills = TURN["yT", n]
                dve.wait_ge(bank_full[a], i + (a_fills + 1))
                part = h1[:, :, bass.ds(i * (2 * P) + n * P, P)]
                dve.tensor_tensor(part, part, bank[a][:].rearrange("p (t c) -> p t c", c=P),
                                  ALU.add).then_inc(bank_taken[a], 1)

            sum_tile(0, 0, True)
            sum_tile(0, 1, True)
            residual(0, 0)
            with dve.Fori(1, KT // 2) as i:
                sum_tile(i, 0, False)
                residual(i - 1, 1)
                sum_tile(i, 1, False)
                residual(i, 0)
            residual(KT // 2 - 1, 1)
            dve.wait_ge(fin_in, 16)
            for t in range(TT):
                dve.wait_ge(y_squared, t + 1)
                dve.tensor_scalar(y_rs[:, t:t + 1], y_rs[:, t:t + 1], EPS, None, ALU.add).then_inc(y_mean, 1)
            for t in range(TT):
                dve.wait_ge(y_rstd, t + 1)
                dve.scalar_tensor_tensor(res[:, t, :], h1[:, t, :], y_rs[:, t:t + 1], fin_row[:], ALU.mult,
                                         ALU.mult).then_inc(res_ready, 1)


def constants():
    s, t = np.arange(P)[:, None], np.arange(P)[None, :]
    const = np.zeros((P, N_CONST), np.float32)
    const[:, K_IDENT:K_IDENT + P] = s == t
    const[:, K_ONES:K_ONES + P] = 1.0
    const[:, K_TRI:K_TRI + P] = np.where(t <= s, 0.0, NEG)

    def pair(m):
        return (s // (2 * m) == t // (2 * m)) & (s % (2 * m) < m) & (t % (2 * m) >= m)

    const[:, K_TOP:K_TOP + P] = pair(LEVELS[0])
    masks = np.concatenate([pair(m) for m in LEVELS[1:]] + [s == t], axis=1).astype(np.float32)
    rope = np.zeros((P, TT, 192), np.float32)
    pos = np.arange(T, dtype=np.float32)
    at = 0
    for d in (IDX, ROPE):
        inv = (np.float32(10000.0) ** (-np.arange(0, d, 2, dtype=np.float32) / np.float32(d))).astype(np.float32)
        ang = pos[:, None] * inv[None, :]
        cos, sin = np.cos(ang), np.sin(ang)
        table = np.concatenate([cos, cos, -sin, sin], axis=1)
        rope[:, :, at:at + 2 * d] = table.reshape(TT, P, 2 * d).transpose(1, 0, 2)
        at += 2 * d
    return const, masks, rope.reshape(P, N_ROPE)


def lay_out(inputs):
    a = {n: np.asarray(v) for n, v in inputs.items()}
    w_in, w_kv = a["w_in"][0], a["w_mem_kv"][0]
    hq, hf, hv, hg, sm = (n * 512 for n in range(5))
    mq, gates = sm + SM, sm + SM + 512

    def t_units(w, c0, n):
        return w[:, c0:c0 + n * P].reshape(KT, P, n, P).transpose(2, 1, 0, 3).reshape(n, P, D)

    def n_units(w, c0):
        return w[:, c0:c0 + 512].reshape(4, 2, P, 512).transpose(0, 2, 1, 3).reshape(4, P, D)

    def merge_units(n, w):
        g = t_units(w_in, gates + n * D, KT).reshape(4, 2, P, D)
        br = w.reshape(4, P, 4, 2, P).transpose(2, 1, 3, 0, 4).reshape(4, 1, P, D)
        return np.concatenate([g, br], axis=1).reshape(12, P, D)

    up, down = a["w_mlp_up"][0], a["w_mlp_down"][0]
    mlp = []
    for half in range(2):
        mlp.append(t_units(up, half * HALF * P, HALF))
        rows = down[half * HALF * P:(half + 1) * HALF * P]
        mlp.append(rows.reshape(2, 8, P, KT, P).transpose(3, 0, 2, 1, 4).reshape(HALF, P, D))
    stream = np.concatenate([
        t_units(w_kv, 0, H), n_units(w_kv, 512), n_units(w_in, sm), t_units(w_in, mq, H), t_units(w_in, hf, H),
        merge_units(2, a["w_br_mem"][0]), t_units(w_in, hq, H), t_units(w_in, hg, H), n_units(w_in, hv),
        merge_units(0, a["w_br_hgrn"][0]), merge_units(1, a["w_br_dsa"][0]),
        n_units(a["w_out"][0], 0), n_units(a["w_out"][0], 512)] + mlp)

    def rows_of(w, n):
        return w.reshape(2, P, n).transpose(1, 0, 2).reshape(P, 2 * n)

    uk = a["dsa_w_uk"][0].reshape(4, P, LAT).transpose(1, 0, 2).reshape(P, 4 * LAT)
    wdsa = np.concatenate([rows_of(a["dsa_w_qidx"][0], 512), rows_of(a["dsa_w_qr"][0], 256),
                           rows_of(a["dsa_w_uq"][0], 512), uk], axis=1)
    wuv = a["dsa_w_uv"][0].transpose(1, 0, 2).reshape(LAT, DH * VD)
    cols = np.concatenate([a["attn_norm_w"].reshape(KT, P), a["mem_norm_w"].reshape(KT, P),
                           a["mlp_norm_w"].reshape(KT, P), a["hgrn_out_norm_w"].reshape(H, P),
                           a["hgrn_lower_bounds"].reshape(2 * H, P)]).T
    rows = np.concatenate([a["dsa_q_norm_w"], a["dsa_kv_norm_w"], a["dsa_kidx_norm_w"]], axis=1)
    const, masks, rope = constants()
    return {"x": a["x"][0], "mem": a["mem"][0], "stream": stream, "wdsa": wdsa, "wuv": wuv, "const": const,
            "rope": rope, "masks": masks, "cols": cols, "rows": rows, "last_row": a["final_norm_w"][None, :]}


def kernel(**inputs):
    import concourse.bacc as bacc
    from concourse.bass_utils import run_bass_kernel_spmd

    nc = bacc.Bacc("TRN2", target_bir_lowering=False, num_devices=1)
    arrays, args = {}, []
    for name, value in lay_out(inputs).items():
        value = np.ascontiguousarray(value)
        arrays[f"in_{name}"] = value
        args.append(nc.dram_tensor(f"in_{name}", value.shape, mybir.dt.from_np(value.dtype),
                                   kind="ExternalInput").ap())
    out = nc.dram_tensor("out", (T, D), mybir.dt.float32, kind="ExternalOutput").ap()
    hybrid_block(nc, *args, out)
    got = run_bass_kernel_spmd(nc, [arrays], core_ids=[0])
    return got.results[0]["out"].reshape(1, T, D)
```

```python
from contextlib import ExitStack

import numpy as np

import concourse.bass as bass
from concourse import mybir

D = 1024
T = 512
M = 256
P = 128
KT = D // P
TT = T // P
MT = M // P
EPS = 1e-6
H = 4
C = 128
LEVELS = [64, 32, 16, 8, 4, 2, 1]
DH = 8
NOPE, ROPE, VD, LAT, QL = 64, 32, 64, 128, 256
IDX = 64
TOPK = 128
SM = QL + LAT + ROPE + IDX + DH
CKV, KR, KI, WI = QL, QL + LAT, QL + LAT + ROPE, QL + LAT + ROPE + IDX
DSA_SCALE = (NOPE + ROPE) ** -0.5
MEM_SCALE = P ** -0.5
NEG = -1.0e30
TAKEN = -3.0e38
FT = 4 * D // P
HALF = FT // 2
FINAL = [(0, 4), (4, 7), (7, 8)]

U_KM = 0
U_VM = U_KM + H
U_SMALL = U_VM + 4
U_MQ = U_SMALL + 4
U_HF = U_MQ + H
U_MERGE_MEM = U_HF + H
U_HQ = U_MERGE_MEM + 12
U_HG = U_HQ + H
U_HV = U_HG + H
U_MERGE_HG = U_HV + 4
U_MERGE_DSA = U_MERGE_HG + 12
U_OUT = U_MERGE_DSA + 12
U_MLP = U_OUT + 8
UNITS = U_MLP + 2 * (HALF + HALF)
STAGES = 2
SLOTS = 4

K_IDENT, K_ONES, K_TRI = 0, 128, 256
N_CONST = 384
HC = C // 2
N_MASK = len(LEVELS) * HC + C
N_ROPE = TT * 192
V_ATTN, V_MEM, V_HG, V_LB = 0, 8, 16, 20
N_COLS = 28
R_Q, R_KV, R_KI = 0, QL, QL + LAT
N_ROWS = QL + LAT + IDX
W_QI, W_QR, W_UQ, W_UK = 0, 1024, 1536, 2560
N_WDSA = 3072

MERGE_AT = [5, 8, 11, 13, 16, 19, 21, 24, 27, 30]
GATED_AT = MERGE_AT[1::3]
AHEAD = 3
QR_HEADS, QR_AT = [1, 3, 0, 2, 5, 7, 4, 6], [0, 32, 128, 160]
ROUNDS = TOPK // 8
EARLY = 7
WIDTH = [P * (t + 1) for t in range(TT)]
BIAS_AT = [P * t * (t + 1) // 2 for t in range(TT)]
SPREAD = [0, 0] + [min(24, 2 * n + n // 2) for n in range(11)]
WORK_AT = [0, 0, WIDTH[1], WIDTH[1] + WIDTH[2]]


def bank_turns():
    uses, used, filled, turn = [], [0] * 8, [0] * 8, {}

    def use(key, bank, by_unit=False):
        turn[key] = (bank, used[bank], filled[bank])
        used[bank] += 1
        filled[bank] += not by_unit

    A, G, B = [0, 1, 2, 3], [4, 5], [6, 7]
    for k in range(KT):
        use(("memT", k), A[k % 4])
    for h in range(H):
        use(("km", h), G[h % 2], True)
    for mt in range(MT):
        use(("vm", mt), B[mt], True)
    for k in range(KT):
        use(("xT", k), (A + G)[k % 6])
    for t in range(TT):
        use(("small", t), A[t], True)
    for h in range(H):
        use(("mq", h), G[h % 2], True)
    for n in range(5):
        use(("smallT", n), A[n % 4])
    for t in range(TT):
        use(("qi", t), B[0])
        use(("qr", t), B[1])
    for h in range(H):
        use(("hf", h), G[h % 2], True)
        for half in range(2):
            g = 2 * h + half
            use(("mL", g), A[g % 2])
            use(("mP", g), A[2])
        use(("mO", h), A[3])
    for n in range(8):
        use(("qT", n), A[n % 4])
    for t in range(1, TT):
        for h in range(DH):
            use(("score", t, h), A[h % 4])
    for b in range(3):
        for j in range(KT):
            use(("gate", b, j), G[j % 2], True)
            use(("branch", b, j), B[j % 2], True)
        if b == 0:
            for h in range(H):
                use(("hq", h), G[h % 2], True)
            for n in range(len(LEVELS) + 1):
                for h in range(H):
                    use(("level", n, h), A[h])
            for h in range(H):
                use(("hg", h), G[h % 2], True)
            for t in range(TT):
                use(("hv", t), (G + B)[t], True)
            for h in range(H):
                use(("kdT", h), A[h])
            for h in range(H):
                use(("U", h), A[h])
            for h in range(H):
                use(("o", h), A[h])
            for h in range(H):
                use(("oss", h), A[h])
            for p in range(DH // 2):
                use(("qn", p), (G + B)[p])
            for p in range(DH // 2):
                use(("kn", p), A[p])
        if b == 1:
            for i in range(TT * DH):
                use(("S", i), A[i % 2])
                use(("PT", i), A[2])
                if i % 4 == 0:
                    use(("PV", i // 4), A[3])
            for p in range(DH // 2):
                use(("ob", p), A[p])
    for t in range(TT):
        use(("out", 0, t), A[t], True)
    for t in range(TT):
        use(("out", 1, t), (G + B)[t], t == TT - 1)
    for part in range(2):
        for t in range(TT):
            use(("mT", t, part), A[t])
    for half in range(2):
        for f in range(HALF):
            use(("up", half, f), G[f % 2], True)
        for j in range(KT):
            use(("down", half, j), B[j % 2], True)
            if half:
                use(("yT", j), A[j % 2])
    return turn


def hybrid_block(nc, x, mem, stream, wdsa, wuv, const, rope, masks, cols, rows, mid_row, last_row, out):
    f32, r32, u8 = mybir.dt.float32, mybir.dt.float32r, mybir.dt.uint8
    ALU, ACT, AX = mybir.AluOpType, mybir.ActivationFunctionType, mybir.AxisListType
    TURN = bank_turns()

    base = -(-nc.sbuf_base // 32) * 32
    top = [base]

    def place(name, shape, dt, at=None):
        size = int(np.prod(shape[1:])) * (1 if dt == u8 else 4)
        if at is None:
            at = top[0]
            top[0] += -(-size // 32) * 32
        return nc.alloc_sbuf_tensor_at(name, shape, dt, offset=at)

    stage = place("stage", [P, STAGES, D], f32)
    w_hi = place("w_hi", [P, SLOTS, D], r32)
    w_lo = place("w_lo", [P, SLOTS, D], r32)
    ACT_HI = top[0]
    act_hi = place("act_hi", [P, KT, T], r32)
    x_sq = place("x_sq", [P, D], f32, ACT_HI)
    act_lo = place("act_lo", [P, KT, T], r32)
    cst = place("cst", [P, N_CONST], f32)
    msk = place("msk", [P, N_MASK], u8)
    col = place("col", [P, N_COLS], f32)
    gate = place("gate", [P, 2, T], f32)
    stat = place("stat", [P, 232], f32)
    XR = top[0]
    xs = place("xs", [P, TT, D], f32)
    merged = place("merged", [P, KT, T], f32, XR)
    HB = top[0]
    top[0] += 8 * 8192
    R = [HB + 8192 * n for n in range(8)]
    DL = top[0]
    small = place("small", [P, TT, SM], f32)
    wd = place("wd", [P, N_WDSA], f32)
    cqT = place("cqT", [P, 2, T], f32)
    qrT = place("qrT", [P, DH // 2, T], f32)
    ckvT = place("ckvT", [P, T], f32)
    krT = place("krT", [P, T], f32)
    KI_AT = top[0]
    kiT = place("kiT", [P, T], f32)
    w_uv = place("w_uv", [P, DH * VD], f32, KI_AT)
    WORK = top[0]
    work = place("work", [P, WIDTH[1] + WIDTH[2] + WIDTH[3]], f32)
    rp = place("rp", [P, TT, 192], f32, WORK)
    BIAS = top[0]
    bias = place("bias", [P, sum(WIDTH)], f32)
    row = place("row", [P, N_ROWS], f32, BIAS)
    memn = place("memn", [P, MT, D], f32, R[0])
    mn_hi = place("mn_hi", [P, KT, M], r32, R[4])
    mem_sq2 = place("mem_sq2", [P, D], f32, R[5])
    mem_sq = place("mem_sq", [P, D], f32, R[4])
    mn_lo = place("mn_lo", [P, KT, M], r32, R[5])
    kmT = place("kmT", [P, H, M], f32, R[6])
    vm = place("vm", [P, MT, H * P], f32, R[6] + 4096)
    mqT = place("mqT", [P, H, T], f32, R[7])
    mP = place("mP", [P, 2, 2, M], f32, R[0])
    mPT = place("mPT", [P, 2, MT, 2 * P], f32, R[0] + 4096)
    oc_hi = place("oc_hi", [P, H, T], r32, R[1])
    oc_lo = place("oc_lo", [P, H, T], r32, R[2])
    qi_nat = place("qi_nat", [P, TT, DH * IDX], f32, R[4])
    qr_nat = place("qr_nat", [P, TT, DH * ROPE], f32, R[5])
    tmp1 = place("tmp1", [P, T], f32, R[5] + 4096)
    tmp2 = place("tmp2", [P, T], f32, R[5] + 6144)
    relu = place("relu", [P, 2, T], f32, R[5] + 4096)
    kr4 = place("kr4", [P, TT, P], f32, R[5])
    ki2 = place("ki2", [P, TT, P], f32, R[5] + 2048)
    qiT = place("qiT", [P, 4, T], f32, R[6])
    b = place("b", [P, H, T], f32, R[0])
    q = place("q", [P, H, T], f32, R[1])
    k = place("k", [P, H, T], f32, R[2])
    th = place("th", [P, H, T], f32, R[3])
    msk32 = place("msk32", [P, N_MASK], f32, R[3])
    v = place("v", [P, TT, H * P], f32, R[3])
    E = place("E", [P, H, T], f32, R[4])
    G = place("G", [P, H, T], f32, R[5])
    A = place("A", [P, H, T], f32, R[6])
    silu2 = place("silu2", [P, H, T], f32, R[7])
    kd = place("kd", [P, H, T], f32, R[4])
    S = place("S", [P, H, 3, P], f32, R[5])
    o = place("o", [P, H, T], f32, R[2])
    osq = place("osq", [P, H, T], f32, R[4])
    orstd = place("orstd", [P, H, T], f32, R[6])
    oa_hi = place("oa_hi", [P, H, T], r32, R[0])
    oa_lo = place("oa_lo", [P, H, T], r32, R[1])
    qh = place("qh", [P, DH, T], f32, R[4])
    kh = place("kh", [P, DH, T], f32, DL + TT * SM * 4)
    prob = place("prob", [P, 4, T], f32, R[6])
    probT = place("probT", [P, 4, T], f32, R[7])
    olat = place("olat", [P, DH, T], f32, R[2])
    ob_hi = place("ob_hi", [P, 4, T], r32, DL + TT * SM * 4)
    ob_lo = place("ob_lo", [P, 4, T], r32, DL + TT * SM * 4 + 8192)
    mg_hi = place("mg_hi", [P, KT, T], r32, R[0])
    mg_lo = place("mg_lo", [P, KT, T], r32, R[2])
    h1 = place("h1", [P, TT, D], f32, R[4])
    hn = place("hn", [P, TT, D], f32, R[6])
    u_hi = place("u_hi", [P, HALF, T], r32, R[0])
    u_lo = place("u_lo", [P, HALF, T], r32, DL)
    ypart = place("ypart", [P, KT, T], f32, R[6])
    ysum = place("ysum", [P, 2, T], f32, DL + 32768)
    fin_row = place("fin_row", [P, D], f32, DL + 32768 + 4096)
    mlp_row = place("mlp_row", [P, D], f32, DL + 32768 + 8192)

    ident, ones = cst[:, K_IDENT:K_IDENT + P], cst[:, K_ONES:K_ONES + P]
    tri = cst[:, K_TRI:K_TRI + P]
    st = [0]

    def stats(n):
        st[0] += n
        return stat[:, st[0] - n:st[0]]

    m_ss, m_rs = stats(2), stats(2)
    x_ss, x_rs = stats(4), stats(4)
    s_ss = stats(12)
    s_rs = stats(12)
    lbx = stats(4 * 6)
    c0, c1, c2, c3 = stats(4), stats(4), stats(4), stats(4)
    m_max, m_nb, m_sum, m_inv = stats(16), stats(16), stats(16), stats(16)
    m8 = stats(8)
    d_max, d_sum, d_inv = stats(4), stats(4), stats(4)
    h_ss, h_rs2 = stats(8), stats(4)
    y_ss, y_rs = stats(12), stats(4)
    newton = stats(24)
    eps = stats(1)
    tick, tick_out, tick_act = stats(1), stats(1), stats(1)

    ctx = ExitStack()
    with ctx:
        bank = [ctx.enter_context(nc.psum_tensor(f"bank{n}", [P, T], f32)) for n in range(8)]

        def sem(name):
            return ctx.enter_context(nc.semaphore(name))

        stage_in = [sem(f"stage_in{n}") for n in range(STAGES)]
        hi_split, unit_split, unit_done = sem("hi_split"), sem("unit_split"), sem("unit_done")
        bank_full = [sem(f"bank_full{n}") for n in range(8)]
        bank_taken = [sem(f"bank_taken{n}") for n in range(8)]
        mem_in = [sem(f"mem_in{mt}") for mt in range(MT)]
        const_in, rope_in, row_in = sem("const_in"), sem("rope_in"), sem("row_in")
        x_in = [sem(f"x_in{t}") for t in range(TT)]
        wd_in, uv_in, xr_in, fin_in = sem("wd_in"), sem("uv_in"), sem("xr_in"), sem("fin_in")
        ticked = sem("ticked")
        dve_step, act_step = sem("dve_step"), sem("act_step")
        mem_squared, mem_rms, mem_normed = sem("mem_squared"), sem("mem_rms"), sem("mem_normed")
        x_rms, x_normed = sem("x_rms"), sem("x_normed")
        mem_hi_made, x_hi_made = sem("mem_hi_made"), sem("x_hi_made")
        small_rms, small_ready = sem("small_rms"), sem("small_ready")
        lb_diff, lb_exp = sem("lb_diff"), sem("lb_exp")
        q_roped, rope_copied, kn_even = sem("q_roped"), sem("rope_copied"), sem("kn_even")
        mem_maxed, mem_exped, mem_prob = sem("mem_maxed"), sem("mem_exped"), sem("mem_prob")
        oc_hi_made = sem("oc_hi_made")
        score_summed, bias_ready = sem("score_summed"), sem("bias_ready")
        gate_used, merged_added, merged_hi_made, merged_ready = (
            sem("gate_used"), sem("merged_added"), sem("merged_hi_made"), sem("merged_ready"))
        f_ready, log_f_ready, decay_ready = sem("f_ready"), sem("log_f_ready"), sem("decay_ready")
        diff_ready, exp_ready, G_ready, A_ready = (
            sem("diff_ready"), sem("exp_ready"), sem("G_ready"), sem("A_ready"))
        qd_ready, S_ready = sem("qd_ready"), sem("S_ready")
        silu_tanh = sem("silu_tanh")
        osq_ready, orstd_ready, oa_made, oa_hi_made, oa_ready = (
            sem("osq_ready"), sem("orstd_ready"), sem("oa_made"), sem("oa_hi_made"), sem("oa_ready"))
        logit_maxed, exped, prob_ready = sem("logit_maxed"), sem("exped"), sem("prob_ready")
        ob_hi_made = sem("ob_hi_made")
        h_squared, y_rms, h_weighted, m_hi_made = (
            sem("h_squared"), sem("y_rms"), sem("h_weighted"), sem("m_hi_made"))
        up_squared, up_hi_made, up_ready = sem("up_squared"), sem("up_hi_made"), sem("up_ready")
        y_squared, y_summed, y_rstd, y_weighted = sem("y_squared"), sem("y_summed"), sem("y_rstd"), sem("y_weighted")
        res_ready, last_ready, stored = sem("res_ready"), sem("last_ready"), sem("stored")

        def full(e, key):
            n, _, fills = TURN[key]
            e.wait_ge(bank_full[n], fills + 1)

        def taken(e, key):
            n, uses, _ = TURN[key]
            e.wait_ge(bank_taken[n], uses + 1)

        def free(e, key):
            n, uses, _ = TURN[key]
            if uses:
                e.wait_ge(bank_taken[n], uses)

        def bank_of(key):
            return bank[TURN[key][0]]

        def take(instruction, key):
            instruction.then_inc(bank_taken[TURN[key][0]], 1)

        block = ctx.enter_context(nc.Block())

        @block.sync
        def _(sp):
            for u in range(STAGES):
                sp.dma_start(stage[:, u, :], stream[u]).then_inc(stage_in[u], 16)
            with sp.Fori(1, UNITS // STAGES) as i:
                for s in range(STAGES):
                    sp.wait_ge(unit_split, (i - 1) * STAGES + s + 1)
                    sp.dma_start(stage[:, s, :], stream[i * STAGES + s]).then_inc(stage_in[s], 16)
            for t in range(TT):
                if t < TT - 1:
                    sp.wait_ge(res_ready, t + 1)
                else:
                    sp.wait_ge(last_ready, 1)
                sp.dma_start(out[t * P:(t + 1) * P, :], h1[:, t, :]).then_inc(stored, 16)
            sp.wait_ge(stored, 16 * TT)

        @block.gpsimd
        def _(pool):
            def split(u, s, first):
                g = s % STAGES
                pool.wait_ge(stage_in[g], (u // STAGES + 1) * 16 if first else (u - s) * 8 + (s // STAGES + 1) * 16)
                if not first:
                    pool.wait_ge(unit_done, u - (SLOTS - 1))
                    pool.wait_ge(ticked, u - (SLOTS - 1))
                    pool.tensor_tensor(tick_out, tick, tick, ALU.add).then_inc(ticked, 1)
                pool.tensor_scalar(w_hi[:, s, :], stage[:, g, :], 1.0, 1.0, ALU.mult, ALU.mult).then_inc(hi_split, 1)
                pool.wait_ge(hi_split, u + 1)
                pool.tensor_tensor(w_lo[:, s, :], stage[:, g, :], w_hi[:, s, :].bitcast(f32),
                                   ALU.subtract).then_inc(unit_split, 1)

            pool.memset(tick, 0.0).then_inc(ticked, 1)
            for s in range(SLOTS):
                split(s, s, True)
            with pool.Fori(1, UNITS // SLOTS) as i:
                for s in range(SLOTS):
                    split(i * SLOTS + s, s, False)

        @block.tensor
        def _(pe):
            def w(u):
                return u % SLOTS

            def three(out_ap, l_hi, l_lo, r_hi, r_lo, first, last):
                pe.matmul(out_ap, l_hi, r_hi, start=first, stop=False)
                pe.matmul(out_ap, l_hi, r_lo, start=False, stop=False)
                return pe.matmul(out_ap, l_lo, r_hi, start=False, stop=last)

            def t_unit(s, out_ap, a_hi, a_lo):
                for kk in range(KT):
                    ws = slice(kk * P, (kk + 1) * P)
                    last = three(out_ap, w_hi[:, s, ws], w_lo[:, s, ws], a_hi[:, kk, :], a_lo[:, kk, :],
                                 kk == 0, kk == KT - 1)
                last.then_inc(unit_done, 1)

            def n_unit(s, pair, pairs, outs, a_hi, a_lo, width):
                for kk in range(2):
                    kx = 2 * pair + kk
                    ws = slice(kk * 512, kk * 512 + width)
                    for t, out_ap in enumerate(outs):
                        ts = slice(t * P, (t + 1) * P)
                        last = three(out_ap, a_hi[:, kx, ts], a_lo[:, kx, ts], w_hi[:, s, ws], w_lo[:, s, ws],
                                     kx == 0, kx == 2 * pairs - 1)
                last.then_inc(unit_done, 1)

            def project(what, h, u0):
                pe.wait_ge(unit_split, u0 + h + 1)
                free(pe, (what, h))
                t_unit(w(u0 + h), bank_of((what, h))[:], act_hi, act_lo)

            def merge_unit(br, n, o_hi, o_lo, u0):
                pe.wait_ge(unit_split, u0 + n + 1)
                jp, part = n // 3, n % 3
                if part < 2:
                    j = 2 * jp + part
                    free(pe, ("gate", br, j))
                    t_unit(w(u0 + n), bank_of(("gate", br, j))[:], act_hi, act_lo)
                else:
                    for jj in range(2):
                        j = 2 * jp + jj
                        free(pe, ("branch", br, j))
                        for kk in range(4):
                            ws = slice((4 * jj + kk) * P, (4 * jj + kk + 1) * P)
                            last = three(bank_of(("branch", br, j))[:], w_hi[:, w(u0 + n), ws],
                                         w_lo[:, w(u0 + n), ws], o_hi[:, kk, :], o_lo[:, kk, :],
                                         kk == 0, kk == 3)
                    last.then_inc(unit_done, 1)

            def transposes(key, sources):
                free(pe, key)
                for n, src in enumerate(sources):
                    last = pe.transpose(bank_of(key)[:, n * P:(n + 1) * P], src, ident)
                last.then_inc(bank_full[TURN[key][0]], 1)

            def filled(instruction, key):
                instruction.then_inc(bank_full[TURN[key][0]], 1)

            pe.wait_ge(const_in, 48)
            pe.wait_ge(mem_normed, MT)
            for kk in range(KT):
                transposes(("memT", kk), [memn[:, mt, kk * P:(kk + 1) * P] for mt in range(MT)])
            for kk in range(KT):
                taken(pe, ("memT", kk))
            for h in range(H):
                pe.wait_ge(unit_split, U_KM + h + 1)
                free(pe, ("km", h))
                t_unit(w(U_KM + h), bank_of(("km", h))[:, 0:M], mn_hi, mn_lo)
            pe.wait_ge(x_normed, TT)
            for kk in range(KT):
                transposes(("xT", kk), [xs[:, t, kk * P:(kk + 1) * P] for t in range(TT)])
            for n in range(4):
                pe.wait_ge(unit_split, U_VM + n + 1)
                n_unit(w(U_VM + n), n, 4, [bank_of(("vm", mt))[:] for mt in range(MT)], mn_hi, mn_lo, 512)
            for kk in range(KT):
                taken(pe, ("xT", kk))
            for n in range(4):
                pe.wait_ge(unit_split, U_SMALL + n + 1)
                if n == 0:
                    for t in range(TT):
                        free(pe, ("small", t))
                n_unit(w(U_SMALL + n), n, 4, [bank_of(("small", t))[:, 0:SM] for t in range(TT)],
                       act_hi, act_lo, SM)
            for h in range(H):
                project("mq", h, U_MQ)
            pe.wait_ge(small_ready, 1)
            transposes(("smallT", 0), [small[:, t, 0:P] for t in range(TT)])
            transposes(("smallT", 1), [small[:, t, P:2 * P] for t in range(TT)])
            transposes(("smallT", 2), [small[:, t, CKV:CKV + P] for t in range(TT)])
            transposes(("smallT", 3), [kr4[:, t, :] for t in range(TT)])
            transposes(("smallT", 4), [ki2[:, t, :] for t in range(TT)])

            def token_queries(key, t, at, n):
                free(pe, (key, t))
                for kk in range(2):
                    last = pe.matmul(bank_of((key, t))[:, 0:n], cqT[:, kk, t * P:(t + 1) * P],
                                     wd[:, at + kk * n:at + (kk + 1) * n], start=kk == 0, stop=kk == 1)
                filled(last, (key, t))

            def mem_logits(g):
                h, half = g // 2, g % 2
                free(pe, ("mL", g))
                for n in range(2):
                    t = 2 * half + n
                    last = pe.matmul(bank_of(("mL", g))[:, n * M:(n + 1) * M], mqT[:, h, t * P:(t + 1) * P],
                                     kmT[:, h, :], start=True, stop=True)
                filled(last, ("mL", g))

            def mem_transposes(g):
                pe.wait_ge(mem_prob, g + 1)
                transposes(("mP", g), [mP[:, g % 2, n, mt * P:(mt + 1) * P] for mt in range(MT) for n in range(2)])

            def mem_values(g):
                h, half = g // 2, g % 2
                taken(pe, ("mP", g))
                if half == 0:
                    free(pe, ("mO", h))
                for mt in range(MT):
                    last = pe.matmul(bank_of(("mO", h))[:, half * M:(half + 1) * M],
                                     vm[:, mt, h * P:(h + 1) * P], mPT[:, g % 2, mt, :],
                                     start=mt == 0, stop=mt == MT - 1)
                if half:
                    filled(last, ("mO", h))

            taken(pe, ("mq", H - 2))
            taken(pe, ("mq", H - 1))
            taken(pe, ("km", H - 2))
            taken(pe, ("km", H - 1))
            taken(pe, ("vm", 0))
            taken(pe, ("vm", 1))
            taken(pe, ("smallT", 0))
            taken(pe, ("smallT", 1))
            pe.wait_ge(wd_in, 16)
            mem_logits(0)
            mem_logits(1)
            for n in range(4):
                project("hf", n, U_HF)
                mem_transposes(2 * n)
                if n < 3:
                    mem_logits(2 * n + 2)
                token_queries("qi", n, W_QI, 512)
                mem_values(2 * n)
                mem_transposes(2 * n + 1)
                if n < 3:
                    mem_logits(2 * n + 3)
                token_queries("qr", n, W_QR, 256)
                mem_values(2 * n + 1)
            for p in range(2):
                taken(pe, ("mO", 2 * p + 1))
            taken(pe, ("smallT", 4))
            scores = [(t, h) for t in range(1, TT) for h in range(DH)]
            for n in range(12):
                merge_unit(0, n, oc_hi, oc_lo, U_MERGE_MEM)
                if n == 1:
                    pe.wait_ge(q_roped, TT)
                    for m in range(4):
                        transposes(("qT", m), [qi_nat[:, t, m * P:(m + 1) * P] for t in range(TT)])
                    for p in range(DH // 2):
                        free(pe, ("qT", 4 + p))
                        for t in range(TT):
                            last = pe.transpose(bank_of(("qT", 4 + p))[0:96, t * P:(t + 1) * P],
                                                qr_nat[:, t, QR_AT[p]:QR_AT[p] + 96], ident)
                        filled(last, ("qT", 4 + p))
                if n == 2:
                    for m in range(4):
                        taken(pe, ("qT", m))
                for t, h in scores[SPREAD[n]:SPREAD[n + 1]]:
                    free(pe, ("score", t, h))
                    hs = slice(IDX * (h % 2), IDX * (h % 2) + IDX)
                    filled(pe.matmul(bank_of(("score", t, h))[:, 0:WIDTH[t]], qiT[hs, h // 2, t * P:(t + 1) * P],
                                     kiT[hs, 0:WIDTH[t]], start=True, stop=True), ("score", t, h))
            for h in range(H):
                project("hq", h, U_HQ)
            for n in range(len(LEVELS) + 1):
                diagonal = n == len(LEVELS)
                if not diagonal:
                    pe.wait_ge(G_ready, n + 1)
                for h in range(H):
                    free(pe, ("level", n, h))
                    for c in range(TT):
                        cs = slice(c * C, (c + 1) * C)
                        if diagonal:
                            last = pe.matmul(bank_of(("level", n, h))[:, cs], k[:, h, cs], q[:, h, cs],
                                             start=True, stop=True)
                        else:
                            m = LEVELS[n]
                            second = G[:, h, cs].rearrange("p (n s m) -> p n s m", s=2, m=m)[:, :, 1, :]
                            dst = bank_of(("level", n, h))[:, c * HC:(c + 1) * HC]
                            last = pe.matmul(dst.rearrange("p (n m) -> p n m", m=m), G[:, h, cs], second,
                                             start=True, stop=True)
                    filled(last, ("level", n, h))
                if n < H:
                    project("hg", n, U_HG)
                else:
                    pe.wait_ge(unit_split, U_HV + n - H + 1)
                    if n == H:
                        for t in range(TT):
                            free(pe, ("hv", t))
                    n_unit(w(U_HV + n - H), n - H, 4, [bank_of(("hv", t))[:] for t in range(TT)],
                           act_hi, act_lo, 512)
            pe.wait_ge(G_ready, len(LEVELS) + 1)
            for h in range(H):
                transposes(("kdT", h), [G[:, h, c * C:(c + 1) * C] for c in range(TT - 1)])
            for t in range(TT):
                taken(pe, ("hv", t))
            for h in range(H):
                taken(pe, ("kdT", h))
                free(pe, ("U", h))
                for c in range(TT - 1):
                    cs = slice(c * C, (c + 1) * C)
                    last = pe.matmul(bank_of(("U", h))[:, cs], kd[:, h, cs], v[:, c, h * P:(h + 1) * P],
                                     start=True, stop=True)
                filled(last, ("U", h))
            pe.wait_ge(A_ready, H)
            pe.wait_ge(qd_ready, 1)
            for h in range(H):
                free(pe, ("o", h))
                pe.wait_ge(S_ready, 3 * (h + 1))
                for c in range(TT):
                    cs = slice(c * C, (c + 1) * C)
                    last = pe.matmul(bank_of(("o", h))[:, cs], v[:, c, h * P:(h + 1) * P], A[:, h, cs],
                                     start=True, stop=c == 0)
                    if c:
                        last = pe.matmul(bank_of(("o", h))[:, cs], S[:, h, c - 1, :], q[:, h, cs],
                                         start=False, stop=True)
                filled(last, ("o", h))
            for p in range(DH // 2):
                free(pe, ("qn", p))
                for kk in range(2):
                    last = pe.matmul(bank_of(("qn", p))[:], wd[:, W_UQ + kk * 512 + p * P:W_UQ + kk * 512 + (p + 1) * P],
                                     cqT[:, kk, :], start=kk == 0, stop=kk == 1)
                filled(last, ("qn", p))
            for h in range(H):
                pe.wait_ge(osq_ready, h + 1)
                free(pe, ("oss", h))
                filled(pe.matmul(bank_of(("oss", h))[:], ones, osq[:, h, :], start=True, stop=True), ("oss", h))
            for p in range(DH // 2):
                free(pe, ("kn", p))
                filled(pe.matmul(bank_of(("kn", p))[:], wd[:, W_UK + p * P:W_UK + (p + 1) * P], ckvT[:],
                                 start=True, stop=True), ("kn", p))

            def logits(i):
                t, h = i // DH, i % DH
                if i < DH:
                    taken(pe, ("qn", h // 2))
                    taken(pe, ("kn", h // 2))
                free(pe, ("S", i))
                parts = P if h % 2 else NOPE + ROPE
                filled(pe.matmul(bank_of(("S", i))[:, 0:WIDTH[t]], qh[0:parts, h, t * P:(t + 1) * P],
                                 kh[0:parts, h, 0:WIDTH[t]], start=True, stop=True), ("S", i))

            def prob_transposes(i):
                pe.wait_ge(prob_ready, i + 1)
                transposes(("PT", i), [prob[:, i % 4, s * P:(s + 1) * P] for s in range(i // DH + 1)])

            def latent_values(i):
                t, h = i // DH, i % DH
                taken(pe, ("PT", i))
                if i % 4 == 0:
                    free(pe, ("PV", i // 4))
                for s in range(t + 1):
                    last = pe.matmul(bank_of(("PV", i // 4))[:, (h % 4) * P:(h % 4 + 1) * P],
                                     small[:, s, CKV:CKV + LAT], probT[:, i % 4, s * P:(s + 1) * P],
                                     start=s == 0, stop=s == t)
                if i % 4 == 3:
                    filled(last, ("PV", i // 4))

            steps = TT * DH
            merge_unit(1, 0, oa_hi, oa_lo, U_MERGE_HG)
            merge_unit(1, 1, oa_hi, oa_lo, U_MERGE_HG)
            pe.wait_ge(rope_copied, 4)
            for i in range(AHEAD):
                logits(i)
            for i in range(steps):
                if i == MERGE_AT[0]:
                    pe.wait_ge(oa_ready, H)
                if i in MERGE_AT:
                    merge_unit(1, 2 + MERGE_AT.index(i), oa_hi, oa_lo, U_MERGE_HG)
                if i + AHEAD < steps:
                    logits(i + AHEAD)
                prob_transposes(i)
                if i:
                    latent_values(i - 1)
            merge_unit(2, 0, ob_hi, ob_lo, U_MERGE_DSA)
            latent_values(steps - 1)
            pe.wait_ge(uv_in, 16)
            taken(pe, ("PV", steps // 4 - 1))
            for p in range(DH // 2):
                free(pe, ("ob", p))
                for n in range(2):
                    h = 2 * p + n
                    last = pe.matmul(bank_of(("ob", p))[VD * n:VD * (n + 1), :], w_uv[:, h * VD:(h + 1) * VD],
                                     olat[:, h, :], start=True, stop=True)
                filled(last, ("ob", p))
            merge_unit(2, 1, ob_hi, ob_lo, U_MERGE_DSA)
            for p in range(DH // 2):
                taken(pe, ("ob", p))
            for n in range(2, 12):
                merge_unit(2, n, ob_hi, ob_lo, U_MERGE_DSA)
            def middle_transposes(t, part):
                pe.wait_ge(h_weighted, part * TT + t + 1)
                transposes(("mT", t, part), [hn[:, t, kk * P:(kk + 1) * P] for kk in range(4 * part, 4 * part + 4)])

            for half in range(2):
                for n in range(4):
                    u = U_OUT + 4 * half + n
                    pe.wait_ge(unit_split, u + 1)
                    pe.wait_ge(merged_ready, 2 * n + 2)
                    if n == 0:
                        for t in range(TT):
                            free(pe, ("out", half, t))
                    if half == 0 or n < 3:
                        n_unit(w(u), n, 4, [bank_of(("out", half, t))[:] for t in range(TT)], mg_hi, mg_lo, 512)
                        if half and n == 1:
                            for t in range(TT):
                                middle_transposes(t, 0)
                        continue
                    for t in range(TT):
                        ts = slice(t * P, (t + 1) * P)
                        for kk in range(2):
                            ws = slice(kk * 512, (kk + 1) * 512)
                            last = three(bank_of(("out", half, t))[:], mg_hi[:, 2 * n + kk, ts], mg_lo[:, 2 * n + kk, ts],
                                         w_hi[:, w(u), ws], w_lo[:, w(u), ws], False, kk == 1)
                        if t < TT - 1:
                            filled(last, ("out", half, t))
                    last.then_inc(unit_done, 1)
            pe.wait_ge(unit_split, U_MLP + 1)
            for t in range(TT):
                taken(pe, ("mT", t, 0))
            free(pe, ("up", 0, 0))
            for kk in range(4):
                ws = slice(kk * P, (kk + 1) * P)
                three(bank_of(("up", 0, 0))[:], w_hi[:, w(U_MLP), ws], w_lo[:, w(U_MLP), ws],
                      act_hi[:, kk, :], act_lo[:, kk, :], kk == 0, False)

            def first_tile(t):
                ts = slice(t * P, (t + 1) * P)
                taken(pe, ("mT", t, 1))
                for kk in range(4, KT):
                    ws = slice(kk * P, (kk + 1) * P)
                    last = three(bank_of(("up", 0, 0))[:, ts], w_hi[:, w(U_MLP), ws], w_lo[:, w(U_MLP), ws],
                                 act_hi[:, kk, ts], act_lo[:, kk, ts], False, kk == KT - 1 and t == TT - 1)
                if t == TT - 1:
                    last.then_inc(unit_done, 1)

            for t in range(TT):
                middle_transposes(t, 1)
                if t:
                    first_tile(t - 1)
            first_tile(TT - 1)
            for half in range(2):
                u_up = U_MLP + half * 2 * HALF
                u_down = u_up + HALF

                def up_tile(i, s, half=half, u_up=u_up):
                    g, uses, _ = TURN["up", half, s]
                    pe.wait_ge(unit_split, i * SLOTS + (u_up + s + 1))
                    pe.wait_ge(bank_taken[g], i * (SLOTS // 2) + uses)
                    t_unit(s, bank[g][:], act_hi, act_lo)

                for s in range(0 if half else 1, SLOTS):
                    up_tile(0, s)
                with pe.Fori(1, HALF // SLOTS) as i:
                    for s in range(SLOTS):
                        up_tile(i, s)

                def down_tile(i, n, half=half, u_down=u_down):
                    g, uses, _ = TURN["down", half, n]
                    for part in range(2):
                        s = 2 * n + part
                        pe.wait_ge(unit_split, i * SLOTS + (u_down + s + 1))
                        if part == 0:
                            pe.wait_ge(bank_taken[g], i + uses)
                        pe.wait_ge(up_ready, half * HALF + 8 * part + 8)
                        for kk in range(8):
                            ws = slice(kk * P, (kk + 1) * P)
                            f = 8 * part + kk
                            last = three(bank[g][:], w_hi[:, s, ws], w_lo[:, s, ws], u_hi[:, f, :], u_lo[:, f, :],
                                         f == 0, f == HALF - 1)
                        last.then_inc(unit_done, 1)

                def back(i, n):
                    g, uses, _ = TURN["down", 1, n]
                    a, a_uses, _ = TURN["yT", n]
                    pe.wait_ge(bank_taken[g], i + (uses + 1))
                    pe.wait_ge(bank_taken[a], i + a_uses)
                    for t in range(TT):
                        last = pe.transpose(bank[a][:, t * P:(t + 1) * P], ysum[:, n, t * P:(t + 1) * P], ident)
                    last.then_inc(bank_full[a], 1)

                if half == 0:
                    with pe.Fori(0, KT // 2) as i:
                        down_tile(i, 0)
                        down_tile(i, 1)
                else:
                    down_tile(0, 0)
                    down_tile(0, 1)
                    back(0, 0)
                    with pe.Fori(1, KT // 2) as i:
                        down_tile(i, 0)
                        back(i - 1, 1)
                        down_tile(i, 1)
                        back(i, 0)
                    back(KT // 2 - 1, 1)

        @block.scalar
        def _(act):
            count = [0]

            def link(instruction):
                count[0] += 1
                instruction.then_inc(act_step, 1)
                act.wait_ge(act_step, count[0])

            for mt in range(MT):
                act.dma_start(memn[:, mt, :], mem[mt * P:(mt + 1) * P, :]).then_inc(mem_in[mt], 16)
            act.dma_start(cst[:], const).then_inc(const_in, 16)
            act.dma_start(col[:], cols).then_inc(const_in, 16)
            act.dma_start(msk32[:], masks).then_inc(const_in, 16)
            for t in range(TT):
                act.dma_start(xs[:, t, :], x[t * P:(t + 1) * P, :]).then_inc(x_in[t], 16)

            def rms(out_ap, in_ap, size, done, bias=None):
                act.activation(out_ap, in_ap, ACT.Sqrt, scale=1.0 / size, bias=eps if bias is None else bias).then_inc(done, 1)

            act.wait_ge(mem_in[0], 16)
            act.activation(mem_sq[:], memn[:, 0, :], ACT.Square, accum_out=m_ss[:, 0:1]).then_inc(mem_squared, 1)
            act.wait_ge(mem_squared, 2)
            rms(m_rs, m_ss, D, mem_rms)
            act.wait_ge(const_in, 48)
            for kk in range(KT):
                full(act, ("memT", kk))
                act.activation(mn_hi[:, kk, :], bank_of(("memT", kk))[:, 0:M], ACT.Copy,
                               scale=col[:, V_MEM + kk:V_MEM + kk + 1]).then_inc(mem_hi_made, 1)
            for t in range(TT):
                act.wait_ge(x_in[t], 16)
                link(act.activation(x_sq[:], xs[:, t, :], ACT.Square, accum_out=x_ss[:, t:t + 1]))
            rms(x_rs, x_ss, D, x_rms)
            for h in range(H):
                act.wait_ge(unit_done, U_KM + h + 1)
                take(act.activation(kmT[:, h, :], bank_of(("km", h))[:, 0:M], ACT.Copy), ("km", h))
            for kk in range(KT):
                full(act, ("xT", kk))
                act.activation(act_hi[:, kk, :], bank_of(("xT", kk))[:], ACT.Copy,
                               scale=col[:, V_ATTN + kk:V_ATTN + kk + 1]).then_inc(x_hi_made, 1)
            act.dma_start(rp[:], rope.rearrange("p (n c) -> p n c", c=192)).then_inc(rope_in, 16)
            act.dma_start(row[:], rows.to_broadcast([P, N_ROWS])).then_inc(row_in, 16)
            for mt in range(MT):
                act.wait_ge(unit_done, U_VM + 4)
                take(act.activation(vm[:, mt, :], bank_of(("vm", mt))[:], ACT.Copy), ("vm", mt))
            act.dma_start(wd[:], wdsa).then_inc(wd_in, 16)
            for t in range(TT):
                act.wait_ge(unit_done, U_SMALL + 4)
                take(act.activation(small[:, t, :], bank_of(("small", t))[:, 0:SM], ACT.Copy), ("small", t))
                taken(act, ("small", t))
                for n, (at, size) in enumerate(((0, QL), (CKV, LAT), (KI, IDX))):
                    link(act.activation(tmp1[:, 0:size], small[:, t, at:at + size], ACT.Square,
                                        accum_out=s_ss[:, 3 * t + n:3 * t + n + 1]))
            ss3, rs3 = (ap.rearrange("p (t n) -> p t n", n=3) for ap in (s_ss, s_rs))
            for n, size in enumerate((QL, LAT, IDX)):
                rms(rs3[:, :, n], ss3[:, :, n], size, small_rms)
            for h in range(H):
                act.wait_ge(unit_done, U_MQ + h + 1)
                take(act.activation(mqT[:, h, :], bank_of(("mq", h))[:], ACT.Copy), ("mq", h))
            for n, dst in enumerate((cqT[:, 0, :], cqT[:, 1, :], ckvT[:], krT[:], kiT[:])):
                full(act, ("smallT", n))
                take(act.activation(dst, bank_of(("smallT", n))[:], ACT.Copy), ("smallT", n))

            act.wait_ge(lb_diff, 1)
            act.activation(lbx[:, 12:20], lbx[:, 4:12], ACT.Exp).then_inc(lb_exp, 1)

            def mem_exp(g):
                act.wait_ge(mem_maxed, g + 1)
                for n in range(2):
                    c = 2 * g + n
                    last = act.activation(mP[:, g % 2, n, :], bank_of(("mL", g))[:, n * M:(n + 1) * M], ACT.Exp,
                                          bias=m_nb[:, c:c + 1], scale=MEM_SCALE, accum_out=m_sum[:, c:c + 1])
                    if n == 0:
                        link(last)
                take(last, ("mL", g))

            def mem_copy(g):
                full(act, ("mP", g))
                take(act.activation(mPT[:, g % 2, :, :], bank_of(("mP", g))[:].rearrange("p (a c) -> p a c", a=2), ACT.Copy), ("mP", g))
                if g % 2:
                    full(act, ("mO", g // 2))
                    act.activation(oc_hi[:, g // 2, :], bank_of(("mO", g // 2))[:], ACT.Copy).then_inc(oc_hi_made, 1)

            def hf_tanh(h):
                act.wait_ge(unit_done, U_HF + h + 1)
                take(act.activation(th[:, h, :], bank_of(("hf", h))[:], ACT.Tanh, scale=0.5), ("hf", h))

            mem_exp(0)
            for g in range(1, 2 * H):
                if g >= 2:
                    full(act, ("mP", g - 2))
                mem_exp(g)
                mem_copy(g - 1)
                if g % 2:
                    hf_tanh(g // 2)
            mem_copy(2 * H - 1)

            def gate_tanh(br, j, u0):
                act.wait_ge(unit_done, u0 + 3 * (j // 2) + j % 2 + 1)
                if 8 * br + j >= 2:
                    act.wait_ge(gate_used, 8 * br + j - 1)
                take(act.activation(gate[:, j % 2, :], bank_of(("gate", br, j))[:], ACT.Tanh, scale=0.5),
                     ("gate", br, j))

            def level_decays(n):
                act.wait_ge(diff_ready, n + 1)
                if n < len(LEVELS):
                    halves = E[:].rearrange("p h (n s m) -> p (h n) s m", s=2, m=LEVELS[n])
                    act.activation(halves[:, :, 0, :], halves[:, :, 0, :], ACT.Exp, scale=-1.0).then_inc(exp_ready, 1)
                    act.activation(halves[:, :, 1, :], halves[:, :, 1, :], ACT.Exp).then_inc(exp_ready, 1)
                else:
                    act.activation(E[:], E[:], ACT.Exp).then_inc(exp_ready, 2)

            scores = [(t, h) for t in range(1, TT) for h in range(DH)]
            for n in range(12):
                if n % 3 < 2:
                    gate_tanh(0, 2 * (n // 3) + n % 3, U_MERGE_MEM)
                if n == 1:
                    for m in range(8):
                        full(act, ("qT", m))
                        dst, rows_used = (qiT[:, m, :], P) if m < 4 else (qrT[0:96, m - 4, :], 96)
                        take(act.activation(dst, bank_of(("qT", m))[0:rows_used, :], ACT.Copy), ("qT", m))
                for m in range(SPREAD[n], SPREAD[n + 1]):
                    t, h = scores[m]
                    full(act, ("score", t, h))
                    if m >= 2:
                        act.wait_ge(score_summed, m - 1)
                    take(act.activation(relu[:, m % 2, 0:WIDTH[t]], bank_of(("score", t, h))[:, 0:WIDTH[t]],
                                        ACT.Relu, scale=IDX ** -0.5), ("score", t, h))
                if n == 2:
                    act.wait_ge(f_ready, 1)
                    act.activation(b[:], b[:], ACT.Ln).then_inc(log_f_ready, 1)
                if n == 4:
                    level_decays(0)
            act.dma_start(w_uv[:], wuv).then_inc(uv_in, 16)
            for h in range(H):
                act.wait_ge(unit_done, U_HQ + h + 1)
                take(act.activation(q[:, h, :], bank_of(("hq", h))[:], ACT.Copy), ("hq", h))
            for n in range(len(LEVELS) + 1):
                if n:
                    level_decays(n)
                if 1 <= n <= H:
                    act.wait_ge(unit_done, U_HG + n)
                    if n >= 3:
                        taken(act, ("hg", n - 3))
                    act.activation(gate[:, (n - 1) % 2, :], bank_of(("hg", n - 1))[:], ACT.Tanh,
                                   scale=0.5).then_inc(silu_tanh, 1)
            act.wait_ge(exp_ready, 2 * len(LEVELS) + 2)
            act.activation(b[:], b[:], ACT.Exp).then_inc(decay_ready, 1)
            for t in range(TT):
                act.wait_ge(unit_done, U_HV + 4)
                take(act.activation(v[:, t, :], bank_of(("hv", t))[:], ACT.Copy), ("hv", t))
            for h in range(H):
                full(act, ("kdT", h))
                act.wait_ge(G_ready, len(LEVELS) + 1)
                take(act.activation(kd[:, h, 0:3 * C], bank_of(("kdT", h))[:, 0:3 * C], ACT.Copy), ("kdT", h))
            for h in range(H):
                full(act, ("U", h))
            for h in range(H):
                full(act, ("o", h))
                act.activation(osq[:, h, :], bank_of(("o", h))[:], ACT.Square).then_inc(osq_ready, 1)
                take(act.activation(o[:, h, :], bank_of(("o", h))[:], ACT.Copy), ("o", h))
            for h in range(H):
                full(act, ("oss", h))
                take(act.activation(orstd[:, h, :], bank_of(("oss", h))[:], ACT.Ln, scale=1.0 / P, bias=eps),
                     ("oss", h))
            for p in range(DH // 2):
                full(act, ("qn", p))
                link(act.activation(qh[0:NOPE, 2 * p, :], bank_of(("qn", p))[0:NOPE, :], ACT.Copy))
                take(act.activation(qh[NOPE:P, 2 * p + 1, :], bank_of(("qn", p))[NOPE:P, :], ACT.Copy), ("qn", p))
            for h in range(H):
                taken(act, ("oss", h))
                act.activation(orstd[:, h, :], orstd[:, h, :], ACT.Exp, scale=-0.5).then_inc(orstd_ready, 1)
            full(act, ("kn", DH // 2 - 1))
            for p in range(DH // 2):
                act.activation(kh[0:NOPE, 2 * p, :], bank_of(("kn", p))[0:NOPE, :], ACT.Copy).then_inc(kn_even, 1)
                act.wait_ge(oa_made, p + 1)
                act.activation(oa_hi[:, p, :], o[:, p, :], ACT.Copy).then_inc(oa_hi_made, 1)

            steps = TT * DH

            def sparse_exp(i):
                t = i // DH
                act.wait_ge(logit_maxed, i + 1)
                act.activation(prob[:, i % 4, 0:WIDTH[t]], prob[:, i % 4, 0:WIDTH[t]], ACT.Exp,
                               bias=d_max[:, i % 4:i % 4 + 1], accum_out=d_sum[:, i % 4:i % 4 + 1]).then_inc(exped, 1)

            def sparse_copy(i):
                t = i // DH
                full(act, ("PT", i))
                if i >= 8 and i % 4 == 0:
                    full(act, ("PV", i // 4 - 1))
                take(act.activation(probT[:, i % 4, 0:WIDTH[t]], bank_of(("PT", i))[:, 0:WIDTH[t]], ACT.Copy),
                     ("PT", i))
                if i % 4 == 3:
                    g = i // 4
                    full(act, ("PV", g))
                    act.wait_ge(oa_ready, H)
                    hs, ts = 4 * (g % 2), slice((g // 2) * P, (g // 2 + 1) * P)
                    take(act.activation(olat[:, hs:hs + 4, ts], bank_of(("PV", g))[:].rearrange("p (a c) -> p a c", a=4), ACT.Copy), ("PV", g))

            gate_tanh(1, 0, U_MERGE_HG)
            gate_tanh(1, 1, U_MERGE_HG)
            for i in range(AHEAD):
                sparse_exp(i)
            for i in range(steps):
                if i in MERGE_AT and (2 + MERGE_AT.index(i)) % 3 < 2:
                    n = 2 + MERGE_AT.index(i)
                    gate_tanh(1, 2 * (n // 3) + n % 3, U_MERGE_HG)
                sparse_copy(i)
                if i + AHEAD < steps:
                    sparse_exp(i + AHEAD)
            for p in range(DH // 2):
                full(act, ("ob", p))
                act.activation(ob_hi[:, p, :], bank_of(("ob", p))[:], ACT.Copy).then_inc(ob_hi_made, 1)
            act.dma_start(fin_row[:], last_row.to_broadcast([P, D])).then_inc(fin_in, 16)
            act.dma_start(mlp_row[:], mid_row.to_broadcast([P, D])).then_inc(fin_in, 16)
            act.dma_start(h1[:], x.rearrange("(n p) d -> p n d", p=P)).then_inc(xr_in, 16)
            for n in range(12):
                if n % 3 < 2:
                    gate_tanh(2, 2 * (n // 3) + n % 3, U_MERGE_DSA)
                else:
                    for j in (2 * (n // 3), 2 * (n // 3) + 1):
                        act.wait_ge(merged_added, KT + j + 1)
                        act.activation(mg_hi[:, j, :], merged[:, j, :], ACT.Copy, scale=0.5).then_inc(merged_hi_made, 1)
            for part in range(2):
                for t in range(TT):
                    full(act, ("mT", t, part))
                    act.activation(act_hi[:, 4 * part:4 * part + 4, t * P:(t + 1) * P],
                                   bank_of(("mT", t, part))[:].rearrange("p (a c) -> p a c", a=4),
                                   ACT.Copy).then_inc(m_hi_made, 1)
                for t in range(TT):
                    last = act.activation(gate[:, t % 2, :], h1[:, t, part * 512:(part + 1) * 512], ACT.Square,
                                          accum_out=h_ss[:, part * TT + t:part * TT + t + 1])
                    if part * TT + t < 2 * TT - 1:
                        link(last)
            last.then_inc(h_squared, 1)
            act.wait_ge(h_squared, 1)
            for half in range(2):
                u_up = U_MLP + half * 2 * HALF

                def relu_tile(i, s, first, half=half, u_up=u_up):
                    g, _, _ = TURN["up", half, s]
                    act.wait_ge(unit_done, i * SLOTS + (u_up + s + 1))
                    if not first:
                        act.wait_ge(up_ready, i * SLOTS + (half * HALF + s - 1))
                    act.activation(gate[:, s % 2, :], bank[g][:], ACT.Relu).then_inc(bank_taken[g], 1)

                def hi_tile(i, s, half=half):
                    act.wait_ge(up_squared, i * SLOTS + (half * HALF + s + 1))
                    act.activation(u_hi[:, i * SLOTS + s, :], gate[:, s % 2, :], ACT.Copy).then_inc(up_hi_made, 1)

                for s in range(SLOTS):
                    relu_tile(0, s, s < 2 and half == 0)
                    hi_tile(0, s)
                with act.Fori(1, HALF // SLOTS) as i:
                    for s in range(SLOTS):
                        relu_tile(i, s, False)
                        hi_tile(i, s)
                if half == 0:
                    u_down = u_up + HALF
                    with act.Fori(0, KT // 2) as i:
                        for n in range(2):
                            g, _, _ = TURN["down", 0, n]
                            act.wait_ge(unit_done, i * SLOTS + (u_down + 2 * n + 2))
                            act.activation(ypart[:, i * 2 + n, :], bank[g][:], ACT.Copy).then_inc(bank_taken[g], 1)
            link(act.activation(tick_act, eps, ACT.Sqrt))
            for g, (j0, j1) in enumerate(FINAL):
                taken(act, ("yT", j1 - 1))
                for t in range(TT):
                    n = (j1 - j0) * P
                    last = act.activation(gate[:, t % 2, 0:n], h1[:, t, j0 * P:j1 * P], ACT.Square,
                                          accum_out=y_ss[:, 4 * g + t:4 * g + t + 1])
                    if t < TT - 1:
                        link(last)
                last.then_inc(y_squared, 1)
                act.wait_ge(y_squared, g + 1)
            act.wait_ge(y_summed, 1)
            rms(y_rs, y_ss[:, 0:4], D, y_rms)
            act.wait_ge(y_rstd, 1)
            act.wait_ge(y_weighted, len(FINAL))
            act.activation(h1[:, TT - 1, :], h1[:, TT - 1, :], ACT.Copy, scale=y_rs[:, TT - 1:TT]).then_inc(last_ready, 1)

        @block.vector
        def _(dve):
            count = [0]

            def link(instruction):
                count[0] += 1
                instruction.then_inc(dve_step, 1)
                dve.wait_ge(dve_step, count[0])

            def rstd(root, total, size, done, count=1):
                n = root.shape[-1]
                mean, sq = newton[:, 0:n], newton[:, 12:12 + n]
                link(dve.tensor_scalar(mean, total, 1.0 / size, EPS, ALU.mult, ALU.add))
                dve.wait_ge(done, count)
                link(dve.reciprocal(root, root))
                link(dve.tensor_tensor(sq, root, root, ALU.mult))
                link(dve.scalar_tensor_tensor(sq, sq, -0.5, mean, ALU.mult, ALU.mult))
                return dve.scalar_tensor_tensor(root, sq, 1.5, root, ALU.add, ALU.mult)

            link(dve.memset(eps, EPS))
            dve.wait_ge(mem_in[1], 16)
            dve.tensor_tensor_reduce(out=mem_sq2[:], in0=memn[:, 1, :], in1=memn[:, 1, :], scale=1.0, scalar=0.0,
                                     op0=ALU.mult, op1=ALU.add, accum_out=m_ss[:, 1:2]).then_inc(mem_squared, 1)
            dve.wait_ge(mem_squared, 2)
            link(rstd(m_rs, m_ss, D, mem_rms))
            for mt in range(MT):
                dve.tensor_scalar(memn[:, mt, :], memn[:, mt, :], m_rs[:, mt:mt + 1], None,
                                  ALU.mult).then_inc(mem_normed, 1)
            dve.wait_ge(const_in, 48)
            a0, a1 = col[:, V_LB:V_LB + 4], col[:, V_LB + 4:V_LB + 8]
            link(dve.tensor_tensor(lbx[:, 0:4], a0, a1, ALU.max))
            link(dve.tensor_tensor(lbx[:, 4:8], a0, lbx[:, 0:4], ALU.subtract))
            dve.tensor_tensor(lbx[:, 8:12], a1, lbx[:, 0:4], ALU.subtract).then_inc(lb_diff, 1)
            for kk in range(KT):
                dve.wait_ge(mem_hi_made, kk + 1)
                take(dve.scalar_tensor_tensor(mn_lo[:, kk, :], bank_of(("memT", kk))[:, 0:M],
                                              col[:, V_MEM + kk:V_MEM + kk + 1], mn_hi[:, kk, :].bitcast(f32),
                                              ALU.mult, ALU.subtract), ("memT", kk))
            link(dve.tensor_copy(msk[:], msk32[:]))
            dve.wait_ge(x_rms, 1)
            link(rstd(x_rs, x_ss, D, x_rms))
            for t in range(TT):
                dve.tensor_scalar(xs[:, t, :], xs[:, t, :], x_rs[:, t:t + 1], None, ALU.mult).then_inc(x_normed, 1)
            for kk in range(KT):
                dve.wait_ge(x_hi_made, kk + 1)
                take(dve.scalar_tensor_tensor(act_lo[:, kk, :], bank_of(("xT", kk))[:],
                                              col[:, V_ATTN + kk:V_ATTN + kk + 1], act_hi[:, kk, :].bitcast(f32),
                                              ALU.mult, ALU.subtract), ("xT", kk))
            dve.wait_ge(small_rms, 3)
            for n, size in enumerate((QL, LAT, IDX)):
                part = lambda ap: ap.rearrange("p (t n) -> p n t", n=3)[:, n, :]
                link(rstd(part(s_rs), part(s_ss), size, small_rms, 3))
            dve.wait_ge(row_in, 16)
            dve.wait_ge(rope_in, 16)
            for n, (at, size, r0) in enumerate(((0, QL, R_Q), (CKV, LAT, R_KV), (KI, IDX, R_KI))):
                for t in range(TT):
                    part = small[:, t, at:at + size]
                    link(dve.scalar_tensor_tensor(part, part, s_rs[:, 3 * t + n:3 * t + n + 1],
                                                  row[:, r0:r0 + size], ALU.mult, ALU.mult))

            def rotate(dst, src, cc, ss, half, t1, t2):
                link(dve.tensor_tensor(t1, src, cc, ALU.mult))
                link(dve.tensor_tensor(t2[..., 0:half], src[..., half:2 * half], ss[..., 0:half], ALU.mult))
                link(dve.tensor_tensor(t2[..., half:2 * half], src[..., 0:half], ss[..., half:2 * half], ALU.mult))
                return dve.tensor_tensor(dst, t1, t2, ALU.add)

            link(rotate(kr4[:, :, 0:ROPE], small[:, :, KR:KR + ROPE], rp[:, :, 128:160], rp[:, :, 160:192], ROPE // 2,
                        tmp1[:, 0:TT * ROPE].rearrange("p (t c) -> p t c", c=ROPE),
                        tmp2[:, 0:TT * ROPE].rearrange("p (t c) -> p t c", c=ROPE)))
            link(dve.memset(kr4[:, :, ROPE:2 * ROPE], 0.0))
            link(dve.tensor_copy(kr4[:, :, 2 * ROPE:4 * ROPE], kr4[:, :, 0:2 * ROPE]))
            link(rotate(ki2[:, :, 0:IDX], small[:, :, KI:KI + IDX], rp[:, :, 0:64], rp[:, :, 64:128], IDX // 2,
                        tmp1[:, 0:TT * IDX].rearrange("p (t c) -> p t c", c=IDX),
                        tmp2[:, 0:TT * IDX].rearrange("p (t c) -> p t c", c=IDX)))
            link(dve.tensor_copy(ki2[:, :, IDX:2 * IDX], ki2[:, :, 0:IDX]))
            dve.tensor_scalar(small[:, :, WI:WI + DH], small[:, :, WI:WI + DH], DH ** -0.5, None,
                              ALU.mult).then_inc(small_ready, 1)

            for key in (("smallT", 3), ("smallT", 4)):
                full(dve, key)

            def rotate_queries(t):
                for key, dst, width, at in (("qi", qi_nat, IDX, 0), ("qr", qr_nat, ROPE, 128)):
                    full(dve, (key, t))
                    heads = lambda ap: ap.rearrange("p (h c) -> p h c", c=width)
                    n = DH * width
                    cc = rp[:, t, at:at + width].unsqueeze(1).to_broadcast([P, DH, width])
                    ss = rp[:, t, at + width:at + 2 * width].unsqueeze(1).to_broadcast([P, DH, width])
                    src = heads(bank_of((key, t))[:, 0:n])
                    t1, t2 = heads(tmp1[:, 0:n]), heads(tmp2[:, 0:n])
                    half = width // 2
                    link(dve.tensor_tensor(t1, src, cc, ALU.mult))
                    link(dve.tensor_tensor(t2[:, :, 0:half], src[:, :, half:width], ss[:, :, 0:half], ALU.mult))
                    take(dve.tensor_tensor(t2[:, :, half:width], src[:, :, 0:half], ss[:, :, half:width], ALU.mult),
                         (key, t))
                    taken(dve, (key, t))
                    last = dve.tensor_tensor(heads(dst[:, t, :]), t1, t2, ALU.add)
                    if key == "qi":
                        link(last)
                last.then_inc(q_roped, 1)
                dve.wait_ge(q_roped, t + 1)

            def mem_max(g):
                full(dve, ("mL", g))
                cs = slice(2 * g, 2 * g + 2)
                link(dve.tensor_reduce(m_max[:, cs], bank_of(("mL", g))[:].rearrange("p (a c) -> p a c", a=2),
                                       axis=AX.X, op=ALU.max))
                dve.tensor_scalar(m_nb[:, cs], m_max[:, cs], -MEM_SCALE, None, ALU.mult).then_inc(mem_maxed, 1)

            def mem_norm(g):
                taken(dve, ("mL", g))
                cs = slice(2 * g, 2 * g + 2)
                link(dve.reciprocal(m_inv[:, cs], m_sum[:, cs]))
                for n in range(2):
                    c = 2 * g + n
                    last = dve.tensor_scalar(mP[:, g % 2, n, :], mP[:, g % 2, n, :], m_inv[:, c:c + 1], None, ALU.mult)
                    if n == 0:
                        link(last)
                last.then_inc(mem_prob, 1)
                if g >= 3 and g % 2:
                    oc_low(g // 2 - 1)

            def oc_low(h):
                dve.wait_ge(oc_hi_made, h + 1)
                take(dve.tensor_tensor(oc_lo[:, h, :], bank_of(("mO", h))[:], oc_hi[:, h, :].bitcast(f32),
                                       ALU.subtract), ("mO", h))

            mem_max(0)
            mem_max(1)
            for g in range(2 * H):
                mem_norm(g)
                if g + 2 < 2 * H:
                    mem_max(g + 2)
                if g % 2:
                    rotate_queries(g // 2)
            oc_low(H - 1)
            dve.wait_ge(lb_exp, 1)
            link(dve.tensor_tensor(lbx[:, 20:24], lbx[:, 12:16], lbx[:, 16:20], ALU.add))
            link(dve.reciprocal(lbx[:, 20:24], lbx[:, 20:24]))
            link(dve.tensor_tensor(lbx[:, 0:4], lbx[:, 12:16], lbx[:, 20:24], ALU.mult))
            link(dve.tensor_scalar(c1, lbx[:, 0:4], -0.5, 0.5, ALU.mult, ALU.add))
            link(dve.tensor_tensor(c0, lbx[:, 0:4], c1, ALU.add))
            link(dve.tensor_scalar(c2, c0, -1.0, 1.0, ALU.mult, ALU.add))
            link(dve.tensor_scalar(c3, c1, -1.0, None, ALU.mult))

            def gated(br, j, u0):
                taken(dve, ("gate", br, j))
                dve.wait_ge(unit_done, u0 + 3 * (j // 2) + 3)
                if br == 0:
                    take(dve.scalar_tensor_tensor(merged[:, j, :], gate[:, j % 2, :], 1.0,
                                                  bank_of(("branch", br, j))[:], ALU.add, ALU.mult), ("branch", br, j))
                    dve.memset(lbx[:, 0:1], 0.0).then_inc(gate_used, 1)
                else:
                    take(dve.scalar_tensor_tensor(gate[:, j % 2, :], gate[:, j % 2, :], 1.0,
                                                  bank_of(("branch", br, j))[:], ALU.add, ALU.mult), ("branch", br, j))
                    taken(dve, ("branch", br, j))
                    link(dve.tensor_tensor(merged[:, j, :], merged[:, j, :], gate[:, j % 2, :], ALU.add))
                    dve.memset(lbx[:, 0:1], 0.0).then_inc(gate_used, 1)
                dve.wait_ge(gate_used, 8 * br + j + 1)

            def differences(n):
                m = (LEVELS + [0])[n]
                if m:
                    pairs = b[:].rearrange("p h (n m) -> p (h n) m", m=2 * m)
                    ref = pairs[:, :, m - 1:m].to_broadcast([P, H * T // (2 * m), 2 * m])
                    dve.tensor_tensor(E[:].rearrange("p h (n m) -> p (h n) m", m=2 * m), pairs, ref,
                                      ALU.subtract).then_inc(diff_ready, 1)
                else:
                    chunks = b[:].rearrange("p h (n m) -> p (h n) m", m=C)
                    ref = chunks[:, :, C - 1:C].to_broadcast([P, H * TT, C])
                    dve.tensor_tensor(E[:].rearrange("p h (n m) -> p (h n) m", m=C), ref, chunks,
                                      ALU.subtract).then_inc(diff_ready, 1)

            scores = [(t, h) for t in range(1, TT) for h in range(DH)]
            dve.wait_ge(x_normed, TT)

            def keys_of(t):
                return work[:, WORK_AT[t]:WORK_AT[t] + WIDTH[t]]

            def topk_round(t, r):
                if r == 0:
                    own = keys_of(t)[:, t * P:WIDTH[t]]
                    link(dve.tensor_tensor(own, own, tri, ALU.add))
                link(dve.max(m8, keys_of(t)))
                link(dve.match_replace(keys_of(t), m8, keys_of(t), TAKEN))
                if r == ROUNDS - 1:
                    link(dve.tensor_scalar(bias[:, BIAS_AT[t]:BIAS_AT[t] + WIDTH[t]], keys_of(t), TAKEN, NEG,
                                           ALU.not_equal, ALU.mult))

            link(dve.tensor_copy(bias[:, 0:P], tri))
            for n in range(12):
                if n % 3 == 2:
                    for jj in range(2):
                        gated(0, 2 * (n // 3) + jj, U_MERGE_MEM)
                for m in range(SPREAD[n], SPREAD[n + 1]):
                    t, h = scores[m]
                    taken(dve, ("score", t, h))
                    acc = work[:, WORK_AT[t]:WORK_AT[t] + WIDTH[t]]
                    wi = small[:, t, WI + h:WI + h + 1]
                    if h == 0:
                        dve.tensor_scalar(acc, relu[:, m % 2, 0:WIDTH[t]], wi, None, ALU.mult).then_inc(score_summed, 1)
                    else:
                        dve.scalar_tensor_tensor(acc, relu[:, m % 2, 0:WIDTH[t]], wi, acc, ALU.mult,
                                                 ALU.add).then_inc(score_summed, 1)
                    dve.wait_ge(score_summed, m + 1)
                    if t > 1:
                        for r in range(2 * h, 2 * h + 2):
                            topk_round(t - 1, r)
                if n == 1:
                    for h in range(H):
                        taken(dve, ("hf", h))
                        last = dve.tensor_scalar(b[:, h, :], th[:, h, :], c1[:, h:h + 1], c0[:, h:h + 1], ALU.mult, ALU.add)
                    last.then_inc(f_ready, 1)
                if n == 3:
                    dve.wait_ge(log_f_ready, 1)
                    for h in range(H):
                        for c in range(TT):
                            seg = b[:, h, c * C:(c + 1) * C]
                            last = dve.tensor_tensor_scan(seg, ones, seg, 0.0, ALU.mult, ALU.add)
                    link(last)
                    full(dve, ("qT", 7))
                    differences(0)
            half0 = lambda ap, side: ap.rearrange("p h (n s m) -> p (h n) s m", s=2, m=LEVELS[0])[:, :, side, :]
            for h in range(H):
                last = dve.tensor_scalar(k[:, h, :], th[:, h, :], c3[:, h:h + 1], c2[:, h:h + 1], ALU.mult, ALU.add)
            link(last)
            dve.wait_ge(exp_ready, 2)
            dve.tensor_tensor(half0(G[:], 0), half0(k[:], 0), half0(E[:], 0), ALU.mult)
            full(dve, ("score", TT - 1, DH - 1))
            link(dve.memset(A[:], 0.0))
            for h in range(H):
                taken(dve, ("hq", h))
                hs = slice(h, h + 1)
                last = dve.tensor_tensor(half0(G[:, hs, :], 1), half0(q[:, hs, :], 1), half0(E[:, hs, :], 1), ALU.mult)
            last.then_inc(G_ready, 1)
            for n, m in enumerate(LEVELS):
                if n:
                    dve.wait_ge(exp_ready, 2 * n + 2)
                    for h in range(H):
                        full(dve, ("level", n - 1, h))
                    view = lambda ap: ap[:].rearrange("p h (n s m) -> p (h n) s m", s=2, m=m)
                    link(dve.tensor_tensor(view(G)[:, :, 0, :], view(k)[:, :, 0, :], view(E)[:, :, 0, :], ALU.mult))
                    dve.tensor_tensor(view(G)[:, :, 1, :], view(q)[:, :, 1, :], view(E)[:, :, 1, :],
                                      ALU.mult).then_inc(G_ready, 1)
                dve.wait_ge(G_ready, n + 1)
                differences(n + 1)
                if 1 <= n <= H:
                    dve.wait_ge(silu_tanh, n)
                    take(dve.scalar_tensor_tensor(silu2[:, n - 1, :], gate[:, (n - 1) % 2, :], 1.0,
                                                  bank_of(("hg", n - 1))[:], ALU.add, ALU.mult), ("hg", n - 1))
                for h in range(H):
                    full(dve, ("level", n, h))
                    blocks = HC // m
                    src = bank_of(("level", n, h))[:, 0:TT * HC].rearrange("p (c n m) -> p c n m", c=TT, m=m)
                    dst = A[:, h, :].rearrange("p (c n s m) -> p c n s m", c=TT, s=2, m=m)[:, :, :, 1, :]
                    own = msk[:, n * HC:(n + 1) * HC].rearrange("p (n m) -> p n m", m=m)
                    take(dve.copy_predicated(dst, own.unsqueeze(1).to_broadcast([P, TT, blocks, m]), src),
                         ("level", n, h))
                    taken(dve, ("level", n, h))
                if n < EARLY:
                    topk_round(TT - 1, n)
            n = len(LEVELS)
            for h in range(H):
                full(dve, ("level", n, h))
                src = bank_of(("level", n, h))[:].rearrange("p (c m) -> p c m", m=C)
                dst = A[:, h, :].rearrange("p (c m) -> p c m", m=C)
                take(dve.copy_predicated(dst, msk[:, n * HC:n * HC + C].unsqueeze(1).to_broadcast([P, TT, C]), src),
                     ("level", n, h))
                taken(dve, ("level", n, h))
            link(dve.memset(lbx[:, 0:1], 0.0))
            dve.memset(lbx[:, 0:1], 0.0).then_inc(A_ready, H)
            dve.wait_ge(exp_ready, 2 * len(LEVELS) + 2)
            dve.tensor_tensor(G[:], k[:], E[:], ALU.mult).then_inc(G_ready, 1)
            dve.wait_ge(decay_ready, 1)
            dve.tensor_tensor(q[:], q[:], b[:], ALU.mult).then_inc(qd_ready, 1)
            for h in range(H):
                full(dve, ("kdT", h))
            for h in range(H):
                full(dve, ("U", h))
                for c in range(TT - 1):
                    got = bank_of(("U", h))[:, c * C:(c + 1) * C]
                    if c == 0:
                        last = dve.tensor_copy(S[:, h, c, :], got)
                    else:
                        last = dve.scalar_tensor_tensor(S[:, h, c, :], S[:, h, c - 1, :],
                                                        b[:, h, (c + 1) * C - 1:(c + 1) * C], got, ALU.mult, ALU.add)
                    last.then_inc(S_ready, 1)
                    dve.wait_ge(S_ready, 3 * h + c + 1)
                take(dve.memset(lbx[:, 0:1], 0.0), ("U", h))
                taken(dve, ("U", h))
            full(dve, ("oss", H - 1))
            even = lambda tile: tile[64:96].rearrange("p (a two) t -> p a two t", two=2)[:, :, 0, :]
            odd = lambda tile: tile[0:64].rearrange("p (a two) t -> p a two t", two=2)[:, :, 1, :]
            dve.tensor_copy(even(qh), qrT[64:96]).then_inc(rope_copied, 1)
            dve.tensor_copy(odd(qh), qrT[0:64]).then_inc(rope_copied, 1)
            full(dve, ("kn", DH // 2 - 1))
            dve.tensor_copy(even(kh), krT[64:96].unsqueeze(1).to_broadcast([32, DH // 2, T])).then_inc(rope_copied, 1)
            dve.tensor_copy(odd(kh), krT[0:64].unsqueeze(1).to_broadcast([64, DH // 2, T])).then_inc(rope_copied, 1)
            for h in range(H):
                dve.wait_ge(orstd_ready, h + 1)
                link(dve.scalar_tensor_tensor(o[:, h, :], o[:, h, :], col[:, V_HG + h:V_HG + h + 1],
                                              orstd[:, h, :], ALU.mult, ALU.mult))
                dve.scalar_tensor_tensor(o[:, h, :], o[:, h, :], 0.5, silu2[:, h, :], ALU.mult,
                                         ALU.mult).then_inc(oa_made, 1)
            for p in range(DH // 2):
                dve.wait_ge(kn_even, p + 1)
                take(dve.tensor_copy(kh[NOPE:P, 2 * p + 1, :], bank_of(("kn", p))[NOPE:P, :]), ("kn", p))

            def oa_low(h):
                dve.wait_ge(oa_hi_made, h + 1)
                dve.tensor_tensor(oa_lo[:, h, :], o[:, h, :], oa_hi[:, h, :].bitcast(f32),
                                  ALU.subtract).then_inc(oa_ready, 1)

            steps = TT * DH

            def masked_max(i):
                t = i // DH
                full(dve, ("S", i))
                if i >= 4:
                    full(dve, ("PT", i - 4))
                p = prob[:, i % 4, 0:WIDTH[t]]
                take(dve.scalar_tensor_tensor(p, bank_of(("S", i))[:, 0:WIDTH[t]], DSA_SCALE,
                                              bias[:, BIAS_AT[t]:BIAS_AT[t] + WIDTH[t]], ALU.mult, ALU.add), ("S", i))
                taken(dve, ("S", i))
                dve.tensor_reduce(d_max[:, i % 4:i % 4 + 1], p, axis=AX.X, op=ALU.max, negate=True).then_inc(logit_maxed, 1)

            def normalise(i):
                t = i // DH
                dve.wait_ge(exped, i + 1)
                link(dve.reciprocal(d_inv[:, i % 4:i % 4 + 1], d_sum[:, i % 4:i % 4 + 1]))
                p = prob[:, i % 4, 0:WIDTH[t]]
                dve.tensor_scalar(p, p, d_inv[:, i % 4:i % 4 + 1], None, ALU.mult).then_inc(prob_ready, 1)

            for i in range(AHEAD):
                masked_max(i)
            done = EARLY
            normalise(0)
            for i in range(steps):
                if i + 1 < steps:
                    normalise(i + 1)
                if i in GATED_AT:
                    for jj in range(2):
                        gated(1, 2 * GATED_AT.index(i) + jj, U_MERGE_HG)
                for _ in range(2 if i in MERGE_AT and i not in GATED_AT else 0):
                    if done < ROUNDS:
                        topk_round(TT - 1, done)
                        done += 1
                if i + AHEAD < steps:
                    masked_max(i + AHEAD)
                if i < H // 2:
                    oa_low(2 * i)
                    oa_low(2 * i + 1)
            for jj in range(2):
                gated(1, KT - 2 + jj, U_MERGE_HG)
            for p in range(DH // 2):
                dve.wait_ge(ob_hi_made, p + 1)
                take(dve.tensor_tensor(ob_lo[:, p, :], bank_of(("ob", p))[:], ob_hi[:, p, :].bitcast(f32),
                                       ALU.subtract), ("ob", p))
            for jp in range(4):
                for j in (2 * jp, 2 * jp + 1):
                    gated(2, j, U_MERGE_DSA)
                    dve.memset(lbx[:, 0:1], 0.0).then_inc(merged_added, KT + 1 if j == 0 else 1)
                for j in (2 * jp, 2 * jp + 1):
                    dve.wait_ge(merged_hi_made, j + 1)
                    dve.scalar_tensor_tensor(mg_lo[:, j, :], merged[:, j, :], 0.5, mg_hi[:, j, :].bitcast(f32),
                                             ALU.mult, ALU.subtract).then_inc(merged_ready, 1)
            dve.wait_ge(xr_in, 16)

            def add_residual(half, t):
                if half and t < TT - 1:
                    full(dve, ("out", half, t))
                else:
                    dve.wait_ge(unit_done, U_OUT + 4 * half + 4)
                part = h1[:, t, half * 512:(half + 1) * 512]
                take(dve.tensor_tensor(part, part, bank_of(("out", half, t))[:], ALU.add), ("out", half, t))

            def weigh_middle(half, t):
                hs = slice(half * 512, (half + 1) * 512)
                taken(dve, ("out", half, t))
                dve.tensor_tensor(hn[:, t, hs], h1[:, t, hs], mlp_row[:, hs], ALU.mult).then_inc(h_weighted, 1)

            def lo_of_middle(t, part):
                dve.wait_ge(m_hi_made, part * TT + t + 1)
                ks, ts = slice(4 * part, 4 * part + 4), slice(t * P, (t + 1) * P)
                take(dve.tensor_tensor(act_lo[:, ks, ts], bank_of(("mT", t, part))[:].rearrange("p (a c) -> p a c", a=4),
                                       act_hi[:, ks, ts].bitcast(f32), ALU.subtract), ("mT", t, part))

            dve.wait_ge(fin_in, 32)
            for half in range(2):
                for t in range(TT):
                    add_residual(half, t)
                    weigh_middle(half, t)
                    if half and t:
                        lo_of_middle(t - 1, 1)
                if half == 0:
                    for t in range(TT):
                        lo_of_middle(t, 0)
            lo_of_middle(TT - 1, 1)
            for half in range(2):
                with dve.Fori(0, HALF // SLOTS) as i:
                    for s in range(SLOTS):
                        g, uses, _ = TURN["up", half, s]
                        dve.wait_ge(bank_taken[g], i * (SLOTS // 2) + (uses + 1))
                        dve.tensor_tensor(gate[:, s % 2, :], gate[:, s % 2, :], gate[:, s % 2, :],
                                          ALU.mult).then_inc(up_squared, 1)
                        dve.wait_ge(up_hi_made, i * SLOTS + (half * HALF + s + 1))
                        dve.tensor_tensor(u_lo[:, i * SLOTS + s, :], gate[:, s % 2, :],
                                          u_hi[:, i * SLOTS + s, :].bitcast(f32), ALU.subtract).then_inc(up_ready, 1)
            u_down = U_MLP + 3 * HALF
            dve.wait_ge(h_squared, 1)
            link(dve.tensor_tensor(h_rs2, h_ss[:, 0:TT], h_ss[:, TT:2 * TT], ALU.add))
            link(dve.tensor_scalar(h_rs2, h_rs2, 1.0 / D, EPS, ALU.mult, ALU.add))
            link(dve.reciprocal(h_rs2, h_rs2))

            def residual(j):
                full(dve, ("yT", j))
                for t in range(TT):
                    part = h1[:, t, j * P:(j + 1) * P]
                    last = dve.scalar_tensor_tensor(part, bank_of(("yT", j))[:, t * P:(t + 1) * P], h_rs2[:, t:t + 1],
                                                    part, ALU.mult, ALU.add)
                take(last, ("yT", j))

            def weigh(g):
                j0, j1 = FINAL[g]
                n = (j1 - j0) * P
                dve.wait_ge(y_squared, g + 1)
                part = h1[:, :, j0 * P:j1 * P]
                dve.tensor_tensor(part, part, fin_row[:, j0 * P:j1 * P].unsqueeze(1).to_broadcast([P, TT, n]),
                                  ALU.mult).then_inc(y_weighted, 1)

            for j in range(KT):
                dve.wait_ge(unit_done, u_down + 2 * j + 2)
                if j >= 2:
                    full(dve, ("yT", j - 2))
                take(dve.tensor_tensor(ysum[:, j % 2, :], bank_of(("down", 1, j))[:], ypart[:, j, :], ALU.add),
                     ("down", 1, j))
                if j:
                    residual(j - 1)
                if j == FINAL[0][1] + 1:
                    weigh(0)
            residual(KT - 1)
            weigh(1)
            dve.wait_ge(y_squared, len(FINAL))
            y_all = y_ss[:, 0:4]
            link(dve.tensor_tensor(y_all, y_all, y_ss[:, 4:8], ALU.add))
            dve.tensor_tensor(y_all, y_all, y_ss[:, 8:12], ALU.add).then_inc(y_summed, 1)
            weigh(2)
            dve.wait_ge(y_summed, 1)
            rstd(y_rs, y_all, D, y_rms).then_inc(y_rstd, 1)
            dve.wait_ge(y_rstd, 1)
            dve.wait_ge(y_weighted, len(FINAL))
            for t in range(TT - 1):
                dve.tensor_scalar(h1[:, t, :], h1[:, t, :], y_rs[:, t:t + 1], None, ALU.mult).then_inc(res_ready, 1)


def constants():
    s, t = np.arange(P)[:, None], np.arange(P)[None, :]
    const = np.zeros((P, N_CONST), np.float32)
    const[:, K_IDENT:K_IDENT + P] = s == t
    const[:, K_ONES:K_ONES + P] = 1.0
    const[:, K_TRI:K_TRI + P] = np.where(t <= s, 0.0, NEG)

    def pair(m):
        return (s // (2 * m) == t // (2 * m)) & (s % (2 * m) < m) & (t % (2 * m) >= m)

    masks = [pair(m)[:, (np.arange(P) % (2 * m)) >= m] for m in LEVELS] + [s == t]
    masks = np.concatenate(masks, axis=1).astype(np.float32)
    rope = np.zeros((P, TT, 192), np.float32)
    pos = np.arange(T, dtype=np.float32)
    at = 0
    for d in (IDX, ROPE):
        inv = (np.float32(10000.0) ** (-np.arange(0, d, 2, dtype=np.float32) / np.float32(d))).astype(np.float32)
        ang = pos[:, None] * inv[None, :]
        cos, sin = np.cos(ang), np.sin(ang)
        table = np.concatenate([cos, cos, -sin, sin], axis=1)
        rope[:, :, at:at + 2 * d] = table.reshape(TT, P, 2 * d).transpose(1, 0, 2)
        at += 2 * d
    return const, masks, rope.reshape(P, N_ROPE)


def lay_out(inputs):
    a = {n: np.asarray(v) for n, v in inputs.items()}
    w_in, w_kv = a["w_in"][0], a["w_mem_kv"][0]
    hq, hf, hv, hg, sm = (n * 512 for n in range(5))
    mq, gates = sm + SM, sm + SM + 512

    def t_units(w, c0, n):
        return w[:, c0:c0 + n * P].reshape(KT, P, n, P).transpose(2, 1, 0, 3).reshape(n, P, D)

    def n_units(w, c0):
        return w[:, c0:c0 + 512].reshape(4, 2, P, 512).transpose(0, 2, 1, 3).reshape(4, P, D)

    def merge_units(n, w):
        g = t_units(w_in, gates + n * D, KT).reshape(4, 2, P, D)
        br = w.reshape(4, P, 4, 2, P).transpose(2, 1, 3, 0, 4).reshape(4, 1, P, D)
        return np.concatenate([g, br], axis=1).reshape(12, P, D)

    up, down = a["w_mlp_up"][0], a["w_mlp_down"][0]
    mlp = []
    for half in range(2):
        mlp.append(t_units(up, half * HALF * P, HALF))
        rows = down[half * HALF * P:(half + 1) * HALF * P]
        mlp.append(rows.reshape(2, 8, P, KT, P).transpose(3, 0, 2, 1, 4).reshape(HALF, P, D))
    stream = np.concatenate([
        t_units(w_kv, 0, H), n_units(w_kv, 512), n_units(w_in, sm), t_units(w_in, mq, H), t_units(w_in, hf, H),
        merge_units(2, a["w_br_mem"][0]), t_units(w_in, hq, H), t_units(w_in, hg, H), n_units(w_in, hv),
        merge_units(0, a["w_br_hgrn"][0]), merge_units(1, a["w_br_dsa"][0]),
        n_units(a["w_out"][0], 0), n_units(a["w_out"][0], 512)] + mlp)

    def rows_of(w, n):
        return w.reshape(2, P, n).transpose(1, 0, 2).reshape(P, 2 * n)

    uk = a["dsa_w_uk"][0].transpose(2, 0, 1).reshape(LAT, DH * NOPE)
    qr = a["dsa_w_qr"][0].reshape(QL, DH, ROPE)[:, QR_HEADS].reshape(QL, DH * ROPE)
    wdsa = np.concatenate([rows_of(a["dsa_w_qidx"][0], 512), rows_of(qr, 256),
                           rows_of(a["dsa_w_uq"][0], 512), uk], axis=1)
    wuv = a["dsa_w_uv"][0].transpose(1, 0, 2).reshape(LAT, DH * VD)
    cols = np.concatenate([a["attn_norm_w"].reshape(KT, P), a["mem_norm_w"].reshape(KT, P),
                           a["hgrn_out_norm_w"].reshape(H, P),
                           a["hgrn_lower_bounds"].reshape(2 * H, P)]).T
    rows = np.concatenate([a["dsa_q_norm_w"], a["dsa_kv_norm_w"], a["dsa_kidx_norm_w"]], axis=1)
    const, masks, rope = constants()
    return {"x": a["x"][0], "mem": a["mem"][0], "stream": stream, "wdsa": wdsa, "wuv": wuv, "const": const,
            "rope": rope, "masks": masks, "cols": cols, "rows": rows, "mid_row": a["mlp_norm_w"], "last_row": a["final_norm_w"][None, :]}


def kernel(**inputs):
    import concourse.bacc as bacc
    from concourse.bass_utils import run_bass_kernel_spmd

    nc = bacc.Bacc("TRN2", target_bir_lowering=False, num_devices=1)
    arrays, args = {}, []
    for name, value in lay_out(inputs).items():
        value = np.ascontiguousarray(value)
        arrays[f"in_{name}"] = value
        args.append(nc.dram_tensor(f"in_{name}", value.shape, mybir.dt.from_np(value.dtype),
                                   kind="ExternalInput").ap())
    out = nc.dram_tensor("out", (T, D), mybir.dt.float32, kind="ExternalOutput").ap()
    hybrid_block(nc, *args, out)
    got = run_bass_kernel_spmd(nc, [arrays], core_ids=[0])
    return got.results[0]["out"].reshape(1, T, D)
```

```python
from contextlib import ExitStack

import numpy as np

from concourse import mybir

D = 1024
T = 512
M = 256
P = 128
KT = D // P
TT = T // P
MT = M // P
EPS = 1e-6
H = 4
C = 128
LEVELS = [64, 32, 16, 8, 4, 2, 1]
DH = 8
NOPE, ROPE, VD, LAT, QL = 64, 32, 64, 128, 256
IDX = 64
TOPK = 128
SM = QL + LAT + ROPE + IDX + DH
CKV, KR, KI, WI = QL, QL + LAT, QL + LAT + ROPE, QL + LAT + ROPE + IDX
DSA_SCALE = (NOPE + ROPE) ** -0.5
MEM_SCALE = P ** -0.5
NEG = -1.0e30
TAKEN = -3.0e38
FT = 4 * D // P
HALF = FT // 2

U_KM = 0
U_VM = U_KM + H
U_SMALL = U_VM + 4
U_MQ = U_SMALL + 4
U_HF = U_MQ + H
U_MERGE_MEM = U_HF + H
U_HQ = U_MERGE_MEM + 12
U_HG = U_HQ + H
U_HV = U_HG + H
U_MERGE_HG = U_HV + 4
U_MERGE_DSA = U_MERGE_HG + 12
U_OUT = U_MERGE_DSA + 12
U_MLP = U_OUT + 8
UNITS = U_MLP + 2 * (HALF + HALF)
STAGES = 2
SLOTS = 4

K_IDENT, K_ONES, K_TRI = 0, 128, 256
N_CONST = 384
HC = C // 2
N_MASK = len(LEVELS) * HC + C
N_ROPE = TT * 192
V_ATTN, V_MEM, V_HG, V_LB = 0, 8, 16, 20
N_COLS = 28
R_Q, R_KV, R_KI = 0, QL, QL + LAT
N_ROWS = QL + LAT + IDX
W_QI, W_QR, W_UQ, W_UK = 0, 1024, 1536, 2560
N_WDSA = 3072

MERGE_AT = [6, 8, 11, 13, 16, 19, 21, 24, 27, 30]
GATED_AT = MERGE_AT[1::3]
AHEAD = 3
QR_HEADS, QR_AT = [1, 3, 0, 2, 5, 7, 4, 6], [0, 32, 128, 160]
ROUNDS = TOPK // 8
EARLY = 7
WIDTH = [P * (t + 1) for t in range(TT)]
BIAS_AT = [P * t * (t + 1) // 2 for t in range(TT)]
SPREAD = [0, 0] + [min(24, 2 * n + n // 2) for n in range(11)]
WORK_AT = [0, 0, WIDTH[1], WIDTH[1] + WIDTH[2]]


def bank_turns():
    uses, used, filled, turn = [], [0] * 8, [0] * 8, {}

    def use(key, bank, by_unit=False):
        turn[key] = (bank, used[bank], filled[bank])
        used[bank] += 1
        filled[bank] += not by_unit

    A, G, B = [0, 1, 2, 3], [4, 5], [6, 7]
    for k in range(KT):
        use(("memT", k), k)
    use(("m_row",), B[0])
    for h in range(H):
        use(("km", h), G[h % 2], True)
    for mt in range(MT):
        use(("vm", mt), B[mt], True)
    for k in range(KT):
        use(("xT", k), (A + G)[k % 6])
    for t in range(TT):
        use(("small", t), A[t], True)
    for h in range(H):
        use(("mq", h), G[h % 2], True)
    for n in range(5):
        use(("smallT", n), A[n % 4])
    for t in range(TT):
        use(("qi", t), B[0])
        use(("qr", t), B[1])
    for h in range(H):
        use(("hf", h), G[h % 2], True)
        for half in range(2):
            g = 2 * h + half
            use(("mL", g), A[g % 2])
            use(("mP", g), A[2])
        use(("mO", h), A[3])
    for n in range(8):
        use(("qT", n), A[n % 4])
    for t in range(1, TT):
        for h in range(DH):
            use(("score", t, h), A[h % 4])
    for b in range(3):
        for j in range(KT):
            use(("gate", b, j), G[j % 2], True)
            use(("branch", b, j), B[j % 2], True)
        if b == 0:
            for h in range(H):
                use(("hq", h), G[h % 2], True)
            for n in range(len(LEVELS) + 1):
                for h in range(H):
                    use(("level", n, h), A[h])
            for h in range(H):
                use(("hg", h), G[h % 2], True)
            for t in range(TT):
                use(("hv", t), (G + B)[t], True)
            for h in range(H):
                use(("kdT", h), A[h])
            for h in range(H):
                use(("U", h), A[h])
            for h in range(H):
                use(("o", h), A[h])
            for h in range(H):
                use(("oss", h), A[h])
            for p in range(DH // 2):
                use(("qn", p), (G + B)[p])
            for p in range(DH // 2):
                use(("kn", p), A[p])
        if b == 1:
            for i in range(TT * DH):
                use(("S", i), A[i % 2])
                use(("PT", i), A[2])
                if i % 4 == 0:
                    use(("PV", i // 4), A[3])
            for p in range(DH // 2):
                use(("ob", p), A[p])
    for t in range(TT):
        use(("out", 0, t), A[t], True)
    for t in range(TT):
        use(("out", 1, t), (G + B)[t], t == TT - 1)
    for part in range(2):
        for t in range(TT):
            use(("mT", t, part), A[t])
    for half in range(2):
        for f in range(HALF):
            use(("up", half, f), G[f % 2], True)
        for t in range(TT):
            use(("down", half, 0, t), A[t], t == TT - 1)
        for t in range(TT):
            use(("down", half, 1, t), (G + B)[t], t == TT - 1)
    return turn


def hybrid_block(nc, x, mem, stream, wdsa, wuv, const, rope, masks, cols, rows, mid_row, last_row, out):
    f32, r32, u8 = mybir.dt.float32, mybir.dt.float32r, mybir.dt.uint8
    ALU, ACT, AX = mybir.AluOpType, mybir.ActivationFunctionType, mybir.AxisListType
    TURN = bank_turns()

    base = -(-nc.sbuf_base // 32) * 32
    top = [base]

    def place(name, shape, dt, at=None):
        size = int(np.prod(shape[1:])) * (1 if dt == u8 else 4)
        if at is None:
            at = top[0]
            top[0] += -(-size // 32) * 32
        return nc.alloc_sbuf_tensor_at(name, shape, dt, offset=at)

    stage = place("stage", [P, STAGES, D], f32)
    w_hi = place("w_hi", [P, SLOTS, D], r32)
    w_lo = place("w_lo", [P, SLOTS, D], r32)
    ACT_HI = top[0]
    act_hi = place("act_hi", [P, KT, T], r32)
    x_sq = place("x_sq", [P, D], f32, ACT_HI)
    act_lo = place("act_lo", [P, KT, T], r32)
    cst = place("cst", [P, N_CONST], f32)
    msk = place("msk", [P, N_MASK], u8)
    col = place("col", [P, N_COLS], f32)
    gate = place("gate", [P, 2, T], f32)
    stat = place("stat", [P, 240], f32)
    XR = top[0]
    xs = place("xs", [P, TT, D], f32)
    merged = place("merged", [P, KT, T], f32, XR)
    HB = top[0]
    top[0] += 8 * 8192
    R = [HB + 8192 * n for n in range(8)]
    DL = top[0]
    small = place("small", [P, TT, SM], f32)
    wd = place("wd", [P, N_WDSA], f32)
    cqT = place("cqT", [P, 2, T], f32)
    qrT = place("qrT", [P, DH // 2, T], f32)
    ckvT = place("ckvT", [P, T], f32)
    krT = place("krT", [P, T], f32)
    KI_AT = top[0]
    kiT = place("kiT", [P, T], f32)
    w_uv = place("w_uv", [P, DH * VD], f32, KI_AT)
    WORK = top[0]
    work = place("work", [P, WIDTH[1] + WIDTH[2] + WIDTH[3]], f32)
    rp = place("rp", [P, TT, 192], f32, WORK)
    BIAS = top[0]
    bias = place("bias", [P, sum(WIDTH)], f32)
    row = place("row", [P, N_ROWS], f32, BIAS)
    memn = place("memn", [P, MT, D], f32, R[0])
    mn_hi = place("mn_hi", [P, KT, M], r32, R[4])
    mem_sq2 = place("mem_sq2", [P, D], f32, R[2])
    mem_sq = place("mem_sq", [P, D], f32, R[1])
    mn_lo = place("mn_lo", [P, KT, M], r32, R[5])
    kmT = place("kmT", [P, H, M], f32, R[6])
    m_diag = place("m_diag", [P, M], f32, R[7])
    m_row = place("m_row", [P, M], f32, R[7] + 1024)
    vm = place("vm", [P, MT, H * P], f32, R[6] + 4096)
    mqT = place("mqT", [P, H, T], f32, R[7])
    mP = place("mP", [P, 2, 2, M], f32, R[0])
    mPT = place("mPT", [P, 2, MT, 2 * P], f32, R[0] + 4096)
    oc_hi = place("oc_hi", [P, H, T], r32, R[1])
    oc_lo = place("oc_lo", [P, H, T], r32, R[2])
    qi_nat = place("qi_nat", [P, TT, DH * IDX], f32, R[4])
    qr_nat = place("qr_nat", [P, TT, DH * ROPE], f32, R[5])
    tmp1 = place("tmp1", [P, T], f32, R[5] + 4096)
    tmp2 = place("tmp2", [P, T], f32, R[5] + 6144)
    relu = place("relu", [P, 2, T], f32, R[5] + 4096)
    kr4 = place("kr4", [P, TT, P], f32, R[5])
    ki2 = place("ki2", [P, TT, P], f32, R[5] + 2048)
    qi_parts = place("qi_parts", [P, DH, T], r32, R[6])
    ki_hi = place("ki_hi", [P, T], r32, R[5])
    ki_lo = place("ki_lo", [P, T], r32, R[5] + 2048)
    b = place("b", [P, H, T], f32, R[0])
    q = place("q", [P, H, T], f32, R[1])
    k = place("k", [P, H, T], f32, R[2])
    th = place("th", [P, H, T], f32, R[3])
    msk32 = place("msk32", [P, N_MASK], f32, R[3])
    v = place("v", [P, TT, H * P], f32, R[3])
    E = place("E", [P, H, T], f32, R[4])
    G = place("G", [P, H, T], f32, R[5])
    A = place("A", [P, H, T], f32, R[6])
    silu2 = place("silu2", [P, H, T], f32, R[7])
    kd = place("kd", [P, H, T], f32, R[4])
    S = place("S", [P, H, 3, P], f32, R[5])
    o = place("o", [P, H, T], f32, R[2])
    osq = place("osq", [P, H, T], f32, R[4])
    orstd = place("orstd", [P, H, T], f32, R[6])
    oa_hi = place("oa_hi", [P, H, T], r32, R[0])
    oa_lo = place("oa_lo", [P, H, T], r32, R[1])
    qh = place("qh", [P, DH, T], f32, R[4])
    kh = place("kh", [P, DH, T], f32, DL + TT * SM * 4)
    prob = place("prob", [P, 4, T], f32, R[6])
    probT = place("probT", [P, 4, T], f32, R[7])
    olat = place("olat", [P, DH, T], f32, R[2])
    ob_hi = place("ob_hi", [P, 4, T], r32, DL + TT * SM * 4)
    ob_lo = place("ob_lo", [P, 4, T], r32, DL + TT * SM * 4 + 8192)
    mg_hi = place("mg_hi", [P, KT, T], r32, R[0])
    mg_lo = place("mg_lo", [P, KT, T], r32, R[2])
    h1 = place("h1", [P, TT, D], f32, R[4])
    res = place("res", [P, TT, D], f32, ACT_HI)
    hn = place("hn", [P, TT, D], f32, R[6])
    u_hi = place("u_hi", [P, HALF, T], r32, R[0])
    u_lo = place("u_lo", [P, HALF, T], r32, DL)
    fin_row = place("fin_row", [P, D], f32, DL + 32768 + 4096)
    mlp_row = place("mlp_row", [P, D], f32, DL + 32768 + 8192)

    ident, ones = cst[:, K_IDENT:K_IDENT + P], cst[:, K_ONES:K_ONES + P]
    tri = cst[:, K_TRI:K_TRI + P]
    st = [0]

    def stats(n):
        st[0] += n
        return stat[:, st[0] - n:st[0]]

    m_ss, m_rs = stats(2), stats(2)
    x_ss, x_rs = stats(4), stats(4)
    s_ss = stats(12)
    s_rs = stats(12)
    lbx = stats(4 * 6)
    c0, c1, c2, c3 = stats(4), stats(4), stats(4), stats(4)
    m_max, m_nb, m_sum, m_inv = stats(16), stats(16), stats(16), stats(16)
    m8 = stats(8)
    d_max, d_sum, d_inv = stats(4), stats(4), stats(4)
    h_ss, h_rs2 = stats(8), stats(4)
    y_ss, y_ss2, y_ms, y_rs = stats(4), stats(4), stats(4), stats(4)
    newton = stats(24)
    eps = stats(1)
    tick, tick_out, tick_act = stats(1), stats(1), stats(1)

    ctx = ExitStack()
    with ctx:
        bank = [ctx.enter_context(nc.psum_tensor(f"bank{n}", [P, T], f32)) for n in range(8)]

        def sem(name):
            return ctx.enter_context(nc.semaphore(name))

        stage_in = [sem(f"stage_in{n}") for n in range(STAGES)]
        hi_split, unit_split, unit_done = sem("hi_split"), sem("unit_split"), sem("unit_done")
        bank_full = [sem(f"bank_full{n}") for n in range(8)]
        bank_taken = [sem(f"bank_taken{n}") for n in range(8)]
        mem_in = [sem(f"mem_in{mt}") for mt in range(MT)]
        ident_in, const_in, rope_in, row_in = sem("ident_in"), sem("const_in"), sem("rope_in"), sem("row_in")
        x_in = [sem(f"x_in{t}") for t in range(TT)]
        wd_in, uv_in, xr_in, fin_in = sem("wd_in"), sem("uv_in"), sem("xr_in"), sem("fin_in")
        ticked = sem("ticked")
        dve_step, act_step = sem("dve_step"), sem("act_step")
        mem_squared, mem_rms, diag_ready = sem("mem_squared"), sem("mem_rms"), sem("diag_ready")
        x_rms, x_normed = sem("x_rms"), sem("x_normed")
        mem_hi_made, x_hi_made = sem("mem_hi_made"), sem("x_hi_made")
        small_rms, small_ready = sem("small_rms"), sem("small_ready")
        lb_diff, lb_exp = sem("lb_diff"), sem("lb_exp")
        q_roped, rope_copied, kn_even, qi_hi_made, ki_split = (
            sem("q_roped"), sem("rope_copied"), sem("kn_even"), sem("qi_hi_made"), sem("ki_split"))
        mem_maxed, mem_prob = sem("mem_maxed"), sem("mem_prob")
        oc_hi_made = sem("oc_hi_made")
        score_summed = sem("score_summed")
        gate_used, merged_added, merged_hi_made, merged_ready = (
            sem("gate_used"), sem("merged_added"), sem("merged_hi_made"), sem("merged_ready"))
        f_ready, log_f_ready, decay_ready = sem("f_ready"), sem("log_f_ready"), sem("decay_ready")
        diff_ready, exp_ready, G_ready, A_ready = (
            sem("diff_ready"), sem("exp_ready"), sem("G_ready"), sem("A_ready"))
        qd_ready, S_ready = sem("qd_ready"), sem("S_ready")
        silu_tanh = sem("silu_tanh")
        osq_ready, orstd_ready, oa_made, oa_hi_made, oa_ready = (
            sem("osq_ready"), sem("orstd_ready"), sem("oa_made"), sem("oa_hi_made"), sem("oa_ready"))
        logit_maxed, exped, prob_ready = sem("logit_maxed"), sem("exped"), sem("prob_ready")
        ob_hi_made = sem("ob_hi_made")
        h_squared, y_rms, h_weighted, m_hi_made = (
            sem("h_squared"), sem("y_rms"), sem("h_weighted"), sem("m_hi_made"))
        up_squared, up_hi_made, up_ready = sem("up_squared"), sem("up_hi_made"), sem("up_ready")
        y_mean, y_rstd, y_weighted = sem("y_mean"), sem("y_rstd"), sem("y_weighted")
        res_ready, last_ready, stored = sem("res_ready"), sem("last_ready"), sem("stored")

        def full(e, key):
            n, _, fills = TURN[key]
            e.wait_ge(bank_full[n], fills + 1)

        def taken(e, key):
            n, uses, _ = TURN[key]
            e.wait_ge(bank_taken[n], uses + 1)

        def free(e, key):
            n, uses, _ = TURN[key]
            if uses:
                e.wait_ge(bank_taken[n], uses)

        def bank_of(key):
            return bank[TURN[key][0]]

        def take(instruction, key):
            instruction.then_inc(bank_taken[TURN[key][0]], 1)

        block = ctx.enter_context(nc.Block())

        @block.sync
        def _(sp):
            for u in range(STAGES):
                sp.dma_start(stage[:, u, :], stream[u]).then_inc(stage_in[u], 16)
            with sp.Fori(1, UNITS // STAGES) as i:
                for s in range(STAGES):
                    sp.wait_ge(unit_split, (i - 1) * STAGES + s + 1)
                    sp.dma_start(stage[:, s, :], stream[i * STAGES + s]).then_inc(stage_in[s], 16)
            for t in range(TT):
                if t < TT - 1:
                    sp.wait_ge(res_ready, t + 1)
                else:
                    sp.wait_ge(last_ready, 1)
                sp.dma_start(out[t * P:(t + 1) * P, :], res[:, t, :]).then_inc(stored, 16)
            sp.wait_ge(stored, 16 * TT)

        @block.gpsimd
        def _(pool):
            def split(u, s, first):
                g = s % STAGES
                pool.wait_ge(stage_in[g], (u // STAGES + 1) * 16 if first else (u - s) * 8 + (s // STAGES + 1) * 16)
                if not first:
                    pool.wait_ge(unit_done, u - (SLOTS - 1))
                    pool.wait_ge(ticked, u - (SLOTS - 1))
                    pool.tensor_tensor(tick_out, tick, tick, ALU.add).then_inc(ticked, 1)
                pool.tensor_scalar(w_hi[:, s, :], stage[:, g, :], 1.0, 1.0, ALU.mult, ALU.mult).then_inc(hi_split, 1)
                pool.wait_ge(hi_split, u + 1)
                pool.tensor_tensor(w_lo[:, s, :], stage[:, g, :], w_hi[:, s, :].bitcast(f32),
                                   ALU.subtract).then_inc(unit_split, 1)

            pool.memset(tick, 0.0).then_inc(ticked, 1)
            for s in range(SLOTS):
                split(s, s, True)
            with pool.Fori(1, UNITS // SLOTS) as i:
                for s in range(SLOTS):
                    split(i * SLOTS + s, s, False)
            pool.wait_ge(fin_in, 32)
            for t in range(TT):
                taken(pool, ("down", 1, 1, t))
                pool.tensor_tensor(res[:, t, 512:D], h1[:, t, 512:D], fin_row[:, 512:D], ALU.mult).then_inc(y_weighted, 1)

        @block.tensor
        def _(pe):
            def w(u):
                return u % SLOTS

            def three(out_ap, l_hi, l_lo, r_hi, r_lo, first, last):
                pe.matmul(out_ap, l_hi, r_hi, start=first, stop=False)
                pe.matmul(out_ap, l_hi, r_lo, start=False, stop=False)
                return pe.matmul(out_ap, l_lo, r_hi, start=False, stop=last)

            def t_unit(s, out_ap, a_hi, a_lo):
                for kk in range(KT):
                    ws = slice(kk * P, (kk + 1) * P)
                    last = three(out_ap, w_hi[:, s, ws], w_lo[:, s, ws], a_hi[:, kk, :], a_lo[:, kk, :],
                                 kk == 0, kk == KT - 1)
                last.then_inc(unit_done, 1)

            def n_unit(s, pair, pairs, outs, a_hi, a_lo, width):
                for kk in range(2):
                    kx = 2 * pair + kk
                    ws = slice(kk * 512, kk * 512 + width)
                    for t, out_ap in enumerate(outs):
                        ts = slice(t * P, (t + 1) * P)
                        last = three(out_ap, a_hi[:, kx, ts], a_lo[:, kx, ts], w_hi[:, s, ws], w_lo[:, s, ws],
                                     kx == 0, kx == 2 * pairs - 1)
                last.then_inc(unit_done, 1)

            def last_n_unit(s, pair, keys, a_hi, a_lo, by_tile):
                for t, key in enumerate(keys):
                    ts = slice(t * P, (t + 1) * P)
                    for kk in range(2):
                        ws = slice(kk * 512, (kk + 1) * 512)
                        last = three(bank_of(key)[:], a_hi[:, 2 * pair + kk, ts], a_lo[:, 2 * pair + kk, ts],
                                     w_hi[:, s, ws], w_lo[:, s, ws], False, kk == 1)
                    if by_tile and t < TT - 1:
                        filled(last, key)
                last.then_inc(unit_done, 1)

            def project(what, h, u0):
                pe.wait_ge(unit_split, u0 + h + 1)
                free(pe, (what, h))
                t_unit(w(u0 + h), bank_of((what, h))[:], act_hi, act_lo)

            def merge_unit(br, n, o_hi, o_lo, u0):
                pe.wait_ge(unit_split, u0 + n + 1)
                jp, part = n // 3, n % 3
                if part < 2:
                    j = 2 * jp + part
                    free(pe, ("gate", br, j))
                    t_unit(w(u0 + n), bank_of(("gate", br, j))[:], act_hi, act_lo)
                else:
                    for jj in range(2):
                        j = 2 * jp + jj
                        free(pe, ("branch", br, j))
                        for kk in range(4):
                            ws = slice((4 * jj + kk) * P, (4 * jj + kk + 1) * P)
                            last = three(bank_of(("branch", br, j))[:], w_hi[:, w(u0 + n), ws],
                                         w_lo[:, w(u0 + n), ws], o_hi[:, kk, :], o_lo[:, kk, :],
                                         kk == 0, kk == 3)
                    last.then_inc(unit_done, 1)

            def transposes(key, sources):
                free(pe, key)
                for n, src in enumerate(sources):
                    last = pe.transpose(bank_of(key)[:, n * P:(n + 1) * P], src, ident)
                last.then_inc(bank_full[TURN[key][0]], 1)

            def filled(instruction, key):
                instruction.then_inc(bank_full[TURN[key][0]], 1)

            pe.wait_ge(ident_in, 16)
            for mt in range(MT):
                pe.wait_ge(mem_in[mt], 16)
            for kk in range(KT):
                transposes(("memT", kk), [memn[:, mt, kk * P:(kk + 1) * P] for mt in range(MT)])
            for kk in range(KT):
                taken(pe, ("memT", kk))
            for h in range(H):
                pe.wait_ge(unit_split, U_KM + h + 1)
                free(pe, ("km", h))
                t_unit(w(U_KM + h), bank_of(("km", h))[:, 0:M], mn_hi, mn_lo)
                if h == 0:
                    pe.wait_ge(diag_ready, 1)
                    filled(pe.matmul(bank_of(("m_row",))[:, 0:M], ones, m_diag[:], start=True, stop=True), ("m_row",))
            pe.wait_ge(x_normed, TT)
            for kk in range(KT):
                transposes(("xT", kk), [xs[:, t, kk * P:(kk + 1) * P] for t in range(TT)])
            for n in range(4):
                pe.wait_ge(unit_split, U_VM + n + 1)
                n_unit(w(U_VM + n), n, 4, [bank_of(("vm", mt))[:] for mt in range(MT)], mn_hi, mn_lo, 512)
            for kk in range(KT):
                taken(pe, ("xT", kk))
            for n in range(4):
                pe.wait_ge(unit_split, U_SMALL + n + 1)
                if n == 0:
                    for t in range(TT):
                        free(pe, ("small", t))
                n_unit(w(U_SMALL + n), n, 4, [bank_of(("small", t))[:, 0:SM] for t in range(TT)],
                       act_hi, act_lo, SM)
            for h in range(H):
                project("mq", h, U_MQ)
            pe.wait_ge(small_ready, 1)
            transposes(("smallT", 0), [small[:, t, 0:P] for t in range(TT)])
            transposes(("smallT", 1), [small[:, t, P:2 * P] for t in range(TT)])
            transposes(("smallT", 2), [small[:, t, CKV:CKV + P] for t in range(TT)])
            transposes(("smallT", 3), [kr4[:, t, :] for t in range(TT)])
            transposes(("smallT", 4), [ki2[:, t, :] for t in range(TT)])

            def token_queries(key, t, at, n):
                free(pe, (key, t))
                for kk in range(2):
                    last = pe.matmul(bank_of((key, t))[:, 0:n], cqT[:, kk, t * P:(t + 1) * P],
                                     wd[:, at + kk * n:at + (kk + 1) * n], start=kk == 0, stop=kk == 1)
                filled(last, (key, t))

            def mem_logits(g):
                h, half = g // 2, g % 2
                free(pe, ("mL", g))
                for n in range(2):
                    t = 2 * half + n
                    last = pe.matmul(bank_of(("mL", g))[:, n * M:(n + 1) * M], mqT[:, h, t * P:(t + 1) * P],
                                     kmT[:, h, :], start=True, stop=True)
                filled(last, ("mL", g))

            def mem_transposes(g):
                pe.wait_ge(mem_prob, g + 1)
                transposes(("mP", g), [mP[:, g % 2, n, mt * P:(mt + 1) * P] for mt in range(MT) for n in range(2)])

            def mem_values(g):
                h, half = g // 2, g % 2
                taken(pe, ("mP", g))
                if half == 0:
                    free(pe, ("mO", h))
                for mt in range(MT):
                    last = pe.matmul(bank_of(("mO", h))[:, half * M:(half + 1) * M],
                                     vm[:, mt, h * P:(h + 1) * P], mPT[:, g % 2, mt, :],
                                     start=mt == 0, stop=mt == MT - 1)
                if half:
                    filled(last, ("mO", h))

            taken(pe, ("mq", H - 2))
            taken(pe, ("mq", H - 1))
            taken(pe, ("km", H - 2))
            taken(pe, ("km", H - 1))
            taken(pe, ("vm", 0))
            taken(pe, ("vm", 1))
            taken(pe, ("smallT", 0))
            taken(pe, ("smallT", 1))
            pe.wait_ge(wd_in, 16)
            mem_logits(0)
            mem_logits(1)
            for n in range(4):
                project("hf", n, U_HF)
                mem_transposes(2 * n)
                if n < 3:
                    mem_logits(2 * n + 2)
                token_queries("qi", n, W_QI, 512)
                mem_values(2 * n)
                mem_transposes(2 * n + 1)
                if n < 3:
                    mem_logits(2 * n + 3)
                token_queries("qr", n, W_QR, 256)
                mem_values(2 * n + 1)
            scores = [(t, h) for t in range(1, TT) for h in range(DH)]
            for n in range(12):
                if n == 2:
                    for h in range(H):
                        taken(pe, ("mO", h))
                merge_unit(0, n, oc_hi, oc_lo, U_MERGE_MEM)
                if n == 1:
                    pe.wait_ge(q_roped, TT)
                    for p in range(DH // 2):
                        free(pe, ("qT", p))
                        for t in range(TT):
                            last = pe.transpose(bank_of(("qT", p))[0:96, t * P:(t + 1) * P],
                                                qr_nat[:, t, QR_AT[p]:QR_AT[p] + 96], ident)
                        filled(last, ("qT", p))
                    for m in range(4):
                        transposes(("qT", 4 + m), [qi_nat[:, t, m * P:(m + 1) * P] for t in range(TT)])
                if n == 2:
                    pe.wait_ge(ki_split, 2)
                    for m in range(4, 8):
                        taken(pe, ("qT", m))
                for t, h in scores[SPREAD[n]:SPREAD[n + 1]]:
                    free(pe, ("score", t, h))
                    hs, ts = slice(IDX * (h % 2), IDX * (h % 2) + IDX), slice(t * P, (t + 1) * P)
                    out_ap = bank_of(("score", t, h))[:, 0:WIDTH[t]]
                    pe.matmul(out_ap, qi_parts[:, h, ts], ki_hi[:, 0:WIDTH[t]], start=True, stop=False)
                    filled(pe.matmul(out_ap, qi_parts[hs, h, ts], ki_lo[hs, 0:WIDTH[t]], start=False, stop=True),
                           ("score", t, h))
            for h in range(H):
                project("hq", h, U_HQ)
            project("hg", 0, U_HG)
            for n in range(len(LEVELS) + 1):
                diagonal = n == len(LEVELS)
                if not diagonal:
                    pe.wait_ge(G_ready, n + 1)
                for h in range(H):
                    free(pe, ("level", n, h))
                    for c in range(TT):
                        cs = slice(c * C, (c + 1) * C)
                        if diagonal:
                            last = pe.matmul(bank_of(("level", n, h))[:, cs], k[:, h, cs], q[:, h, cs],
                                             start=True, stop=True)
                        else:
                            m = LEVELS[n]
                            second = G[:, h, cs].rearrange("p (n s m) -> p n s m", s=2, m=m)[:, :, 1, :]
                            dst = bank_of(("level", n, h))[:, c * HC:(c + 1) * HC]
                            last = pe.matmul(dst.rearrange("p (n m) -> p n m", m=m), G[:, h, cs], second,
                                             start=True, stop=True)
                    filled(last, ("level", n, h))
                if n < H - 1:
                    project("hg", n + 1, U_HG)
                elif not diagonal:
                    part = n - (H - 1)
                    pe.wait_ge(unit_split, U_HV + part + 1)
                    if part == 0:
                        for t in range(TT):
                            free(pe, ("hv", t))
                    n_unit(w(U_HV + part), part, 4, [bank_of(("hv", t))[:] for t in range(TT)],
                           act_hi, act_lo, 512)
            pe.wait_ge(G_ready, len(LEVELS) + 1)
            for h in range(H):
                transposes(("kdT", h), [G[:, h, c * C:(c + 1) * C] for c in range(TT - 1)])
            for t in range(TT):
                taken(pe, ("hv", t))
            for h in range(H):
                taken(pe, ("kdT", h))
                free(pe, ("U", h))
                for c in range(TT - 1):
                    cs = slice(c * C, (c + 1) * C)
                    last = pe.matmul(bank_of(("U", h))[:, cs], kd[:, h, cs], v[:, c, h * P:(h + 1) * P],
                                     start=True, stop=True)
                filled(last, ("U", h))
            pe.wait_ge(A_ready, H)
            pe.wait_ge(qd_ready, 1)
            for h in range(H):
                free(pe, ("o", h))
                pe.wait_ge(S_ready, 3 * (h + 1))
                for c in range(TT):
                    cs = slice(c * C, (c + 1) * C)
                    last = pe.matmul(bank_of(("o", h))[:, cs], v[:, c, h * P:(h + 1) * P], A[:, h, cs],
                                     start=True, stop=c == 0)
                    if c:
                        last = pe.matmul(bank_of(("o", h))[:, cs], S[:, h, c - 1, :], q[:, h, cs],
                                         start=False, stop=True)
                filled(last, ("o", h))
            for p in range(DH // 2):
                free(pe, ("qn", p))
                for kk in range(2):
                    last = pe.matmul(bank_of(("qn", p))[:], wd[:, W_UQ + kk * 512 + p * P:W_UQ + kk * 512 + (p + 1) * P],
                                     cqT[:, kk, :], start=kk == 0, stop=kk == 1)
                filled(last, ("qn", p))
            for h in range(H):
                pe.wait_ge(osq_ready, h + 1)
                free(pe, ("oss", h))
                filled(pe.matmul(bank_of(("oss", h))[:], ones, osq[:, h, :], start=True, stop=True), ("oss", h))
            for p in range(DH // 2):
                free(pe, ("kn", p))
                filled(pe.matmul(bank_of(("kn", p))[:], wd[:, W_UK + p * P:W_UK + (p + 1) * P], ckvT[:],
                                 start=True, stop=True), ("kn", p))

            def logits(i):
                t, h = i // DH, i % DH
                if i < DH:
                    taken(pe, ("qn", h // 2))
                    taken(pe, ("kn", h // 2))
                free(pe, ("S", i))
                parts = P if h % 2 else NOPE + ROPE
                filled(pe.matmul(bank_of(("S", i))[:, 0:WIDTH[t]], qh[0:parts, h, t * P:(t + 1) * P],
                                 kh[0:parts, h, 0:WIDTH[t]], start=True, stop=True), ("S", i))

            def prob_transposes(i):
                pe.wait_ge(prob_ready, i + 1)
                transposes(("PT", i), [prob[:, i % 4, s * P:(s + 1) * P] for s in range(i // DH + 1)])

            def latent_values(i):
                t, h = i // DH, i % DH
                taken(pe, ("PT", i))
                if i % 4 == 0:
                    free(pe, ("PV", i // 4))
                for s in range(t + 1):
                    last = pe.matmul(bank_of(("PV", i // 4))[:, (h % 4) * P:(h % 4 + 1) * P],
                                     small[:, s, CKV:CKV + LAT], probT[:, i % 4, s * P:(s + 1) * P],
                                     start=s == 0, stop=s == t)
                if i % 4 == 3:
                    filled(last, ("PV", i // 4))

            steps = TT * DH
            merge_unit(1, 0, oa_hi, oa_lo, U_MERGE_HG)
            merge_unit(1, 1, oa_hi, oa_lo, U_MERGE_HG)
            pe.wait_ge(rope_copied, 4)
            for i in range(AHEAD):
                logits(i)
            for i in range(steps):
                if i == MERGE_AT[0]:
                    pe.wait_ge(oa_ready, H)
                if i in MERGE_AT:
                    merge_unit(1, 2 + MERGE_AT.index(i), oa_hi, oa_lo, U_MERGE_HG)
                if i + AHEAD < steps:
                    logits(i + AHEAD)
                prob_transposes(i)
                if i:
                    latent_values(i - 1)
            merge_unit(2, 0, ob_hi, ob_lo, U_MERGE_DSA)
            latent_values(steps - 1)
            pe.wait_ge(uv_in, 16)
            taken(pe, ("PV", steps // 4 - 1))
            for p in range(DH // 2):
                free(pe, ("ob", p))
                for n in range(2):
                    h = 2 * p + n
                    last = pe.matmul(bank_of(("ob", p))[VD * n:VD * (n + 1), :], w_uv[:, h * VD:(h + 1) * VD],
                                     olat[:, h, :], start=True, stop=True)
                filled(last, ("ob", p))
            merge_unit(2, 1, ob_hi, ob_lo, U_MERGE_DSA)
            for p in range(DH // 2):
                taken(pe, ("ob", p))
            for n in range(2, 12):
                merge_unit(2, n, ob_hi, ob_lo, U_MERGE_DSA)
            def middle_transposes(t, part):
                pe.wait_ge(h_weighted, part * TT + t + 1)
                transposes(("mT", t, part), [hn[:, t, kk * P:(kk + 1) * P] for kk in range(4 * part, 4 * part + 4)])

            for half in range(2):
                for n in range(4):
                    u = U_OUT + 4 * half + n
                    pe.wait_ge(unit_split, u + 1)
                    pe.wait_ge(merged_ready, 2 * n + 2)
                    if n == 0:
                        for t in range(TT):
                            free(pe, ("out", half, t))
                    if half == 0 or n < 3:
                        n_unit(w(u), n, 4, [bank_of(("out", half, t))[:] for t in range(TT)], mg_hi, mg_lo, 512)
                        if half and n == 1:
                            for t in range(TT):
                                middle_transposes(t, 0)
                        continue
                    last_n_unit(w(u), n, [("out", half, t) for t in range(TT)], mg_hi, mg_lo, half == 1)
            pe.wait_ge(unit_split, U_MLP + 1)
            for t in range(TT):
                taken(pe, ("mT", t, 0))
            free(pe, ("up", 0, 0))
            for kk in range(4):
                ws = slice(kk * P, (kk + 1) * P)
                three(bank_of(("up", 0, 0))[:], w_hi[:, w(U_MLP), ws], w_lo[:, w(U_MLP), ws],
                      act_hi[:, kk, :], act_lo[:, kk, :], kk == 0, False)

            def first_tile(t):
                ts = slice(t * P, (t + 1) * P)
                taken(pe, ("mT", t, 1))
                for kk in range(4, KT):
                    ws = slice(kk * P, (kk + 1) * P)
                    last = three(bank_of(("up", 0, 0))[:, ts], w_hi[:, w(U_MLP), ws], w_lo[:, w(U_MLP), ws],
                                 act_hi[:, kk, ts], act_lo[:, kk, ts], False, kk == KT - 1 and t == TT - 1)
                if t == TT - 1:
                    last.then_inc(unit_done, 1)

            for t in range(TT):
                middle_transposes(t, 1)
                if t:
                    first_tile(t - 1)
            first_tile(TT - 1)
            for half in range(2):
                u_up = U_MLP + half * 2 * HALF
                u_down = u_up + HALF

                def up_tile(i, s, half=half, u_up=u_up):
                    g, uses, _ = TURN["up", half, s]
                    pe.wait_ge(unit_split, i * SLOTS + (u_up + s + 1))
                    pe.wait_ge(bank_taken[g], i * (SLOTS // 2) + uses)
                    t_unit(s, bank[g][:], act_hi, act_lo)

                for s in range(0 if half else 1, SLOTS):
                    up_tile(0, s)
                with pe.Fori(1, HALF // SLOTS) as i:
                    for s in range(SLOTS):
                        up_tile(i, s)

                for c in range(2):
                    keys = [("down", half, c, t) for t in range(TT)]
                    for n in range(KT):
                        u = u_down + KT * c + n
                        pe.wait_ge(unit_split, u + 1)
                        pe.wait_ge(up_ready, half * HALF + 2 * n + 2)
                        if n == 0:
                            for key in keys:
                                free(pe, key)
                        if n < KT - 1:
                            n_unit(w(u), n, KT, [bank_of(key)[:] for key in keys], u_hi, u_lo, 512)
                        else:
                            last_n_unit(w(u), n, keys, u_hi, u_lo, True)

        @block.scalar
        def _(act):
            count = [0]

            def link(instruction):
                count[0] += 1
                instruction.then_inc(act_step, 1)
                act.wait_ge(act_step, count[0])

            act.dma_start(cst[:], const).then_inc(ident_in, 16)
            for mt in range(MT):
                act.dma_start(memn[:, mt, :], mem[mt * P:(mt + 1) * P, :]).then_inc(mem_in[mt], 16)
            act.dma_start(col[:], cols).then_inc(const_in, 16)
            act.dma_start(msk32[:], masks).then_inc(const_in, 16)

            def rms(out_ap, in_ap, size, done, bias=None):
                act.activation(out_ap, in_ap, ACT.Sqrt, scale=1.0 / size, bias=eps if bias is None else bias).then_inc(done, 1)

            act.wait_ge(mem_in[0], 16)
            act.activation(mem_sq[:], memn[:, 0, :], ACT.Square, accum_out=m_ss[:, 0:1]).then_inc(mem_squared, 1)
            for t in range(TT):
                act.dma_start(xs[:, t, :], x[t * P:(t + 1) * P, :]).then_inc(x_in[t], 16)
            act.wait_ge(const_in, 32)
            for kk in range(KT):
                full(act, ("memT", kk))
                act.activation(mn_hi[:, kk, :], bank_of(("memT", kk))[:, 0:M], ACT.Copy,
                               scale=col[:, V_MEM + kk:V_MEM + kk + 1]).then_inc(mem_hi_made, 1)
            act.wait_ge(mem_squared, 2)
            rms(m_rs, m_ss, D, mem_rms)
            for t in range(TT):
                act.wait_ge(x_in[t], 16)
                link(act.activation(x_sq[:], xs[:, t, :], ACT.Square, accum_out=x_ss[:, t:t + 1]))
            rms(x_rs, x_ss, D, x_rms)
            for kk in range(KT):
                full(act, ("xT", kk))
                act.activation(act_hi[:, kk, :], bank_of(("xT", kk))[:], ACT.Copy,
                               scale=col[:, V_ATTN + kk:V_ATTN + kk + 1]).then_inc(x_hi_made, 1)
            act.dma_start(rp[:], rope.rearrange("p (n c) -> p n c", c=192)).then_inc(rope_in, 16)
            act.dma_start(row[:], rows.to_broadcast([P, N_ROWS])).then_inc(row_in, 16)
            for mt in range(MT):
                act.wait_ge(unit_done, U_VM + 4)
                take(act.activation(vm[:, mt, :], bank_of(("vm", mt))[:], ACT.Copy, scale=m_rs[:, mt:mt + 1]),
                     ("vm", mt))
            act.dma_start(wd[:], wdsa).then_inc(wd_in, 16)
            for t in range(TT):
                act.wait_ge(unit_done, U_SMALL + 4)
                take(act.activation(small[:, t, :], bank_of(("small", t))[:, 0:SM], ACT.Copy), ("small", t))
                taken(act, ("small", t))
                for n, (at, size) in enumerate(((0, QL), (CKV, LAT), (KI, IDX))):
                    link(act.activation(tmp1[:, 0:size], small[:, t, at:at + size], ACT.Square,
                                        accum_out=s_ss[:, 3 * t + n:3 * t + n + 1]))
            ss3, rs3 = (ap.rearrange("p (t n) -> p t n", n=3) for ap in (s_ss, s_rs))
            for n, size in enumerate((QL, LAT, IDX)):
                rms(rs3[:, :, n], ss3[:, :, n], size, small_rms)
            for h in range(H):
                act.wait_ge(unit_done, U_MQ + h + 1)
                take(act.activation(mqT[:, h, :], bank_of(("mq", h))[:], ACT.Copy), ("mq", h))
            for n, dst in enumerate((cqT[:, 0, :], cqT[:, 1, :], ckvT[:], krT[:], kiT[:])):
                full(act, ("smallT", n))
                take(act.activation(dst, bank_of(("smallT", n))[:], ACT.Copy), ("smallT", n))

            act.wait_ge(lb_diff, 1)
            act.activation(lbx[:, 12:20], lbx[:, 4:12], ACT.Exp).then_inc(lb_exp, 1)

            def mem_exp(g):
                act.wait_ge(mem_maxed, g + 1)
                for n in range(2):
                    c = 2 * g + n
                    last = act.activation(mP[:, g % 2, n, :], bank_of(("mL", g))[:, n * M:(n + 1) * M], ACT.Exp,
                                          bias=m_nb[:, c:c + 1], scale=MEM_SCALE, accum_out=m_sum[:, c:c + 1])
                    if n == 0:
                        link(last)
                take(last, ("mL", g))

            def mem_copy(g):
                full(act, ("mP", g))
                take(act.activation(mPT[:, g % 2, :, :], bank_of(("mP", g))[:].rearrange("p (a c) -> p a c", a=2), ACT.Copy), ("mP", g))
                if g % 2:
                    full(act, ("mO", g // 2))
                    act.activation(oc_hi[:, g // 2, :], bank_of(("mO", g // 2))[:], ACT.Copy).then_inc(oc_hi_made, 1)

            def hf_tanh(h):
                act.wait_ge(unit_done, U_HF + h + 1)
                take(act.activation(th[:, h, :], bank_of(("hf", h))[:], ACT.Tanh, scale=0.5), ("hf", h))

            mem_exp(0)
            for g in range(1, 2 * H):
                if g >= 2:
                    full(act, ("mP", g - 2))
                mem_exp(g)
                mem_copy(g - 1)
                if g % 2:
                    hf_tanh(g // 2)
            mem_copy(2 * H - 1)

            def gate_tanh(br, j, u0):
                act.wait_ge(unit_done, u0 + 3 * (j // 2) + j % 2 + 1)
                if 8 * br + j >= 2:
                    act.wait_ge(gate_used, 8 * br + j - 1)
                take(act.activation(gate[:, j % 2, :], bank_of(("gate", br, j))[:], ACT.Tanh, scale=0.5),
                     ("gate", br, j))

            def level_decays(n):
                act.wait_ge(diff_ready, n + 1)
                if n < len(LEVELS):
                    halves = E[:].rearrange("p h (n s m) -> p (h n) s m", s=2, m=LEVELS[n])
                    act.activation(halves[:, :, 0, :], halves[:, :, 0, :], ACT.Exp, scale=-1.0).then_inc(exp_ready, 1)
                    act.activation(halves[:, :, 1, :], halves[:, :, 1, :], ACT.Exp).then_inc(exp_ready, 1)
                else:
                    act.activation(E[:], E[:], ACT.Exp).then_inc(exp_ready, 2)

            scores = [(t, h) for t in range(1, TT) for h in range(DH)]
            for n in range(12):
                if n % 3 < 2:
                    gate_tanh(0, 2 * (n // 3) + n % 3, U_MERGE_MEM)
                if n == 1:
                    for m in range(4):
                        full(act, ("qT", m))
                        take(act.activation(qrT[0:96, m, :], bank_of(("qT", m))[0:96, :], ACT.Copy), ("qT", m))
                    for m in range(4):
                        src = bank_of(("qT", 4 + m))
                        full(act, ("qT", 4 + m))
                        act.activation(qi_parts[0:64, 2 * m, :], src[0:64, :], ACT.Copy).then_inc(qi_hi_made, 1)
                        act.activation(qi_parts[64:P, 2 * m + 1, :], src[64:P, :], ACT.Copy).then_inc(qi_hi_made, 1)
                    act.activation(ki_hi[:], kiT[:], ACT.Copy).then_inc(ki_split, 1)
                for m in range(SPREAD[n], SPREAD[n + 1]):
                    t, h = scores[m]
                    full(act, ("score", t, h))
                    if m >= 2:
                        act.wait_ge(score_summed, m - 1)
                    take(act.activation(relu[:, m % 2, 0:WIDTH[t]], bank_of(("score", t, h))[:, 0:WIDTH[t]],
                                        ACT.Relu, scale=IDX ** -0.5), ("score", t, h))
                if n == 2:
                    act.wait_ge(f_ready, 1)
                    act.activation(b[:], b[:], ACT.Ln).then_inc(log_f_ready, 1)
                if n == 4:
                    level_decays(0)
            act.dma_start(w_uv[:], wuv).then_inc(uv_in, 16)
            for h in range(H):
                act.wait_ge(unit_done, U_HQ + h + 1)
                take(act.activation(q[:, h, :], bank_of(("hq", h))[:], ACT.Copy), ("hq", h))
            for n in range(len(LEVELS) + 1):
                if n:
                    level_decays(n)
                if n < H:
                    act.wait_ge(unit_done, U_HG + n + 1)
                    if n >= 2:
                        taken(act, ("hg", n - 2))
                    else:
                        act.wait_ge(gate_used, KT - 1 + n)
                    act.activation(gate[:, n % 2, :], bank_of(("hg", n))[:], ACT.Tanh,
                                   scale=0.5).then_inc(silu_tanh, 1)
            act.wait_ge(exp_ready, 2 * len(LEVELS) + 2)
            act.activation(b[:], b[:], ACT.Exp).then_inc(decay_ready, 1)
            for t in range(TT):
                act.wait_ge(unit_done, U_HV + 4)
                take(act.activation(v[:, t, :], bank_of(("hv", t))[:], ACT.Copy), ("hv", t))
            for h in range(H):
                full(act, ("kdT", h))
                act.wait_ge(G_ready, len(LEVELS) + 1)
                take(act.activation(kd[:, h, 0:3 * C], bank_of(("kdT", h))[:, 0:3 * C], ACT.Copy), ("kdT", h))
            for h in range(H):
                full(act, ("U", h))
            for h in range(H):
                full(act, ("o", h))
                act.activation(osq[:, h, :], bank_of(("o", h))[:], ACT.Square).then_inc(osq_ready, 1)
                take(act.activation(o[:, h, :], bank_of(("o", h))[:], ACT.Copy, scale=col[:, V_HG + h:V_HG + h + 1]),
                     ("o", h))
            for h in range(H):
                full(act, ("oss", h))
                take(act.activation(orstd[:, h, :], bank_of(("oss", h))[:], ACT.Ln, scale=1.0 / P, bias=eps),
                     ("oss", h))
            for p in range(DH // 2):
                full(act, ("qn", p))
                link(act.activation(qh[0:NOPE, 2 * p, :], bank_of(("qn", p))[0:NOPE, :], ACT.Copy))
                take(act.activation(qh[NOPE:P, 2 * p + 1, :], bank_of(("qn", p))[NOPE:P, :], ACT.Copy), ("qn", p))
            for h in range(H):
                taken(act, ("oss", h))
                act.activation(orstd[:, h, :], orstd[:, h, :], ACT.Exp, scale=-0.5).then_inc(orstd_ready, 1)
            full(act, ("kn", DH // 2 - 1))
            for p in range(DH // 2):
                act.activation(kh[0:NOPE, 2 * p, :], bank_of(("kn", p))[0:NOPE, :], ACT.Copy).then_inc(kn_even, 1)
                act.wait_ge(oa_made, p + 1)
                act.activation(oa_hi[:, p, :], o[:, p, :], ACT.Copy).then_inc(oa_hi_made, 1)

            steps = TT * DH

            def sparse_exp(i):
                t = i // DH
                act.wait_ge(logit_maxed, i + 1)
                act.activation(prob[:, i % 4, 0:WIDTH[t]], prob[:, i % 4, 0:WIDTH[t]], ACT.Exp,
                               bias=d_max[:, i % 4:i % 4 + 1], accum_out=d_sum[:, i % 4:i % 4 + 1]).then_inc(exped, 1)

            def sparse_copy(i):
                t = i // DH
                full(act, ("PT", i))
                take(act.activation(probT[:, i % 4, 0:WIDTH[t]], bank_of(("PT", i))[:, 0:WIDTH[t]], ACT.Copy),
                     ("PT", i))

            def values_out(g):
                full(act, ("PV", g))
                act.wait_ge(oa_ready, H)
                hs, ts = 4 * (g % 2), slice((g // 2) * P, (g // 2 + 1) * P)
                take(act.activation(olat[:, hs:hs + 4, ts], bank_of(("PV", g))[:].rearrange("p (a c) -> p a c", a=4),
                                    ACT.Copy), ("PV", g))

            gate_tanh(1, 0, U_MERGE_HG)
            gate_tanh(1, 1, U_MERGE_HG)
            for i in range(AHEAD):
                sparse_exp(i)
            for i in range(steps):
                if i in MERGE_AT and (2 + MERGE_AT.index(i)) % 3 < 2:
                    n = 2 + MERGE_AT.index(i)
                    gate_tanh(1, 2 * (n // 3) + n % 3, U_MERGE_HG)
                sparse_copy(i)
                if i and i % 4 == 0:
                    values_out(i // 4 - 1)
                if i + AHEAD < steps:
                    sparse_exp(i + AHEAD)
            values_out(steps // 4 - 1)
            for p in range(DH // 2):
                full(act, ("ob", p))
                act.activation(ob_hi[:, p, :], bank_of(("ob", p))[:], ACT.Copy).then_inc(ob_hi_made, 1)
            act.dma_start(fin_row[:], last_row.to_broadcast([P, D])).then_inc(fin_in, 16)
            act.dma_start(mlp_row[:], mid_row.to_broadcast([P, D])).then_inc(fin_in, 16)
            act.dma_start(h1[:], x.rearrange("(n p) d -> p n d", p=P)).then_inc(xr_in, 16)
            for n in range(12):
                if n % 3 < 2:
                    gate_tanh(2, 2 * (n // 3) + n % 3, U_MERGE_DSA)
                else:
                    for j in (2 * (n // 3), 2 * (n // 3) + 1):
                        act.wait_ge(merged_added, KT + j + 1)
                        act.activation(mg_hi[:, j, :], merged[:, j, :], ACT.Copy, scale=0.5).then_inc(merged_hi_made, 1)
            for part in range(2):
                for t in range(TT):
                    full(act, ("mT", t, part))
                    act.activation(act_hi[:, 4 * part:4 * part + 4, t * P:(t + 1) * P],
                                   bank_of(("mT", t, part))[:].rearrange("p (a c) -> p a c", a=4),
                                   ACT.Copy).then_inc(m_hi_made, 1)
                for t in range(TT):
                    last = act.activation(gate[:, t % 2, :], h1[:, t, part * 512:(part + 1) * 512], ACT.Square,
                                          accum_out=h_ss[:, part * TT + t:part * TT + t + 1])
                    if part * TT + t < 2 * TT - 1:
                        link(last)
            last.then_inc(h_squared, 1)
            act.wait_ge(h_squared, 1)
            for half in range(2):
                u_up = U_MLP + half * 2 * HALF

                def relu_tile(i, s, first, half=half, u_up=u_up):
                    g, _, _ = TURN["up", half, s]
                    act.wait_ge(unit_done, i * SLOTS + (u_up + s + 1))
                    if not first:
                        act.wait_ge(up_ready, i * SLOTS + (half * HALF + s - 1))
                    act.activation(gate[:, s % 2, :], bank[g][:], ACT.Relu).then_inc(bank_taken[g], 1)

                def hi_tile(i, s, half=half):
                    act.wait_ge(up_squared, i * SLOTS + (half * HALF + s + 1))
                    act.activation(u_hi[:, i * SLOTS + s, :], gate[:, s % 2, :], ACT.Copy).then_inc(up_hi_made, 1)

                for s in range(SLOTS):
                    relu_tile(0, s, s < 2 and half == 0)
                    hi_tile(0, s)
                with act.Fori(1, HALF // SLOTS) as i:
                    for s in range(SLOTS):
                        relu_tile(i, s, False)
                        hi_tile(i, s)
            link(act.activation(tick_act, eps, ACT.Sqrt))
            for t in range(TT):
                taken(act, ("down", 1, 0, t))
                link(act.activation(gate[:, t % 2, :], h1[:, t, 0:512], ACT.Square, accum_out=y_ss[:, t:t + 1]))
            act.activation(y_ms, y_ss, ACT.Identity, scale=1.0 / D, bias=eps).then_inc(y_mean, 1)
            act.wait_ge(y_mean, 1)
            for t in range(TT):
                taken(act, ("down", 1, 1, t))
                link(act.activation(gate[:, t % 2, :], h1[:, t, 512:D], ACT.Square, accum_out=y_ss2[:, t:t + 1]))
                rms(y_rs[:, t:t + 1], y_ss2[:, t:t + 1], D, y_rms, bias=y_ms[:, t:t + 1])
            act.wait_ge(y_rstd, 2)
            act.wait_ge(y_weighted, TT)
            act.activation(res[:, TT - 1, :], res[:, TT - 1, :], ACT.Copy, scale=y_rs[:, TT - 1:TT]).then_inc(last_ready, 1)

        @block.vector
        def _(dve):
            count = [0]

            def link(instruction):
                count[0] += 1
                instruction.then_inc(dve_step, 1)
                dve.wait_ge(dve_step, count[0])

            def rstd(root, total, size, done, count=1):
                n = root.shape[-1]
                mean, sq = newton[:, 0:n], newton[:, 12:12 + n]
                link(dve.tensor_scalar(mean, total, 1.0 / size, EPS, ALU.mult, ALU.add))
                dve.wait_ge(done, count)
                link(dve.reciprocal(root, root))
                link(dve.tensor_tensor(sq, root, root, ALU.mult))
                link(dve.scalar_tensor_tensor(sq, sq, -0.5, mean, ALU.mult, ALU.mult))
                return dve.scalar_tensor_tensor(root, sq, 1.5, root, ALU.add, ALU.mult)

            link(dve.memset(eps, EPS))
            dve.wait_ge(mem_in[1], 16)
            dve.tensor_tensor_reduce(out=mem_sq2[:], in0=memn[:, 1, :], in1=memn[:, 1, :], scale=1.0, scalar=0.0,
                                     op0=ALU.mult, op1=ALU.add, accum_out=m_ss[:, 1:2]).then_inc(mem_squared, 1)
            dve.wait_ge(const_in, 32)
            for kk in range(KT):
                dve.wait_ge(mem_hi_made, kk + 1)
                take(dve.scalar_tensor_tensor(mn_lo[:, kk, :], bank_of(("memT", kk))[:, 0:M],
                                              col[:, V_MEM + kk:V_MEM + kk + 1], mn_hi[:, kk, :].bitcast(f32),
                                              ALU.mult, ALU.subtract), ("memT", kk))
            dve.wait_ge(mem_squared, 2)
            link(rstd(m_rs, m_ss, D, mem_rms))
            dve.wait_ge(ident_in, 16)
            for mt in range(MT):
                last = dve.tensor_scalar(m_diag[:, mt * P:(mt + 1) * P], ident, m_rs[:, mt:mt + 1], None, ALU.mult)
            last.then_inc(diag_ready, 1)
            dve.wait_ge(const_in, 32)
            a0, a1 = col[:, V_LB:V_LB + 4], col[:, V_LB + 4:V_LB + 8]
            link(dve.tensor_tensor(lbx[:, 0:4], a0, a1, ALU.max))
            link(dve.tensor_tensor(lbx[:, 4:8], a0, lbx[:, 0:4], ALU.subtract))
            dve.tensor_tensor(lbx[:, 8:12], a1, lbx[:, 0:4], ALU.subtract).then_inc(lb_diff, 1)
            full(dve, ("m_row",))
            take(dve.tensor_copy(m_row[:], bank_of(("m_row",))[:, 0:M]), ("m_row",))
            link(dve.tensor_copy(msk[:], msk32[:]))

            def keys_of_memory(h):
                dve.wait_ge(unit_done, U_KM + h + 1)
                take(dve.tensor_tensor(kmT[:, h, :], bank_of(("km", h))[:, 0:M], m_row[:], ALU.mult), ("km", h))

            keys_of_memory(0)
            keys_of_memory(1)
            dve.wait_ge(x_rms, 1)
            link(rstd(x_rs, x_ss, D, x_rms))
            for t in range(TT):
                dve.tensor_scalar(xs[:, t, :], xs[:, t, :], x_rs[:, t:t + 1], None, ALU.mult).then_inc(x_normed, 1)
            keys_of_memory(2)
            keys_of_memory(3)
            for kk in range(KT):
                dve.wait_ge(x_hi_made, kk + 1)
                take(dve.scalar_tensor_tensor(act_lo[:, kk, :], bank_of(("xT", kk))[:],
                                              col[:, V_ATTN + kk:V_ATTN + kk + 1], act_hi[:, kk, :].bitcast(f32),
                                              ALU.mult, ALU.subtract), ("xT", kk))
            dve.wait_ge(small_rms, 3)
            for n, size in enumerate((QL, LAT, IDX)):
                part = lambda ap: ap.rearrange("p (t n) -> p n t", n=3)[:, n, :]
                link(rstd(part(s_rs), part(s_ss), size, small_rms, 3))
            dve.wait_ge(row_in, 16)
            dve.wait_ge(rope_in, 16)
            for n, (at, size, r0) in enumerate(((0, QL, R_Q), (CKV, LAT, R_KV), (KI, IDX, R_KI))):
                for t in range(TT):
                    part = small[:, t, at:at + size]
                    link(dve.scalar_tensor_tensor(part, part, s_rs[:, 3 * t + n:3 * t + n + 1],
                                                  row[:, r0:r0 + size], ALU.mult, ALU.mult))

            def rotate(dst, src, cc, ss, half, t1, t2):
                link(dve.tensor_tensor(t1, src, cc, ALU.mult))
                link(dve.tensor_tensor(t2[..., 0:half], src[..., half:2 * half], ss[..., 0:half], ALU.mult))
                link(dve.tensor_tensor(t2[..., half:2 * half], src[..., 0:half], ss[..., half:2 * half], ALU.mult))
                return dve.tensor_tensor(dst, t1, t2, ALU.add)

            link(rotate(kr4[:, :, 0:ROPE], small[:, :, KR:KR + ROPE], rp[:, :, 128:160], rp[:, :, 160:192], ROPE // 2,
                        tmp1[:, 0:TT * ROPE].rearrange("p (t c) -> p t c", c=ROPE),
                        tmp2[:, 0:TT * ROPE].rearrange("p (t c) -> p t c", c=ROPE)))
            link(dve.memset(kr4[:, :, ROPE:2 * ROPE], 0.0))
            link(dve.tensor_copy(kr4[:, :, 2 * ROPE:4 * ROPE], kr4[:, :, 0:2 * ROPE]))
            link(rotate(ki2[:, :, 0:IDX], small[:, :, KI:KI + IDX], rp[:, :, 0:64], rp[:, :, 64:128], IDX // 2,
                        tmp1[:, 0:TT * IDX].rearrange("p (t c) -> p t c", c=IDX),
                        tmp2[:, 0:TT * IDX].rearrange("p (t c) -> p t c", c=IDX)))
            link(dve.tensor_copy(ki2[:, :, IDX:2 * IDX], ki2[:, :, 0:IDX]))
            dve.tensor_scalar(small[:, :, WI:WI + DH], small[:, :, WI:WI + DH], DH ** -0.5, None,
                              ALU.mult).then_inc(small_ready, 1)

            for key in (("smallT", 3), ("smallT", 4)):
                full(dve, key)

            def rotate_queries(t):
                for key, dst, width, at in (("qi", qi_nat, IDX, 0), ("qr", qr_nat, ROPE, 128)):
                    full(dve, (key, t))
                    heads = lambda ap: ap.rearrange("p (h c) -> p h c", c=width)
                    n = DH * width
                    cc = rp[:, t, at:at + width].unsqueeze(1).to_broadcast([P, DH, width])
                    ss = rp[:, t, at + width:at + 2 * width].unsqueeze(1).to_broadcast([P, DH, width])
                    src = heads(bank_of((key, t))[:, 0:n])
                    t1, t2 = heads(tmp1[:, 0:n]), heads(tmp2[:, 0:n])
                    half = width // 2
                    link(dve.tensor_tensor(t1, src, cc, ALU.mult))
                    link(dve.tensor_tensor(t2[:, :, 0:half], src[:, :, half:width], ss[:, :, 0:half], ALU.mult))
                    take(dve.tensor_tensor(t2[:, :, half:width], src[:, :, 0:half], ss[:, :, half:width], ALU.mult),
                         (key, t))
                    taken(dve, (key, t))
                    last = dve.tensor_tensor(heads(dst[:, t, :]), t1, t2, ALU.add)
                    if key == "qi":
                        link(last)
                last.then_inc(q_roped, 1)
                dve.wait_ge(q_roped, t + 1)

            def mem_max(g):
                full(dve, ("mL", g))
                cs = slice(2 * g, 2 * g + 2)
                link(dve.tensor_reduce(m_max[:, cs], bank_of(("mL", g))[:].rearrange("p (a c) -> p a c", a=2),
                                       axis=AX.X, op=ALU.max))
                dve.tensor_scalar(m_nb[:, cs], m_max[:, cs], -MEM_SCALE, None, ALU.mult).then_inc(mem_maxed, 1)

            def mem_norm(g):
                taken(dve, ("mL", g))
                cs = slice(2 * g, 2 * g + 2)
                link(dve.reciprocal(m_inv[:, cs], m_sum[:, cs]))
                for n in range(2):
                    c = 2 * g + n
                    last = dve.tensor_scalar(mP[:, g % 2, n, :], mP[:, g % 2, n, :], m_inv[:, c:c + 1], None, ALU.mult)
                    if n == 0:
                        link(last)
                last.then_inc(mem_prob, 1)

            def oc_low(h):
                dve.wait_ge(oc_hi_made, h + 1)
                take(dve.tensor_tensor(oc_lo[:, h, :], bank_of(("mO", h))[:], oc_hi[:, h, :].bitcast(f32),
                                       ALU.subtract), ("mO", h))

            mem_max(0)
            mem_max(1)
            for g in range(2 * H):
                if g and g % 2 == 0:
                    oc_low(g // 2 - 1)
                mem_norm(g)
                if g + 2 < 2 * H:
                    mem_max(g + 2)
                if g % 2:
                    rotate_queries(g // 2)
            oc_low(H - 1)
            dve.wait_ge(lb_exp, 1)
            link(dve.tensor_tensor(lbx[:, 20:24], lbx[:, 12:16], lbx[:, 16:20], ALU.add))
            link(dve.reciprocal(lbx[:, 20:24], lbx[:, 20:24]))
            link(dve.tensor_tensor(lbx[:, 0:4], lbx[:, 12:16], lbx[:, 20:24], ALU.mult))
            link(dve.tensor_scalar(c1, lbx[:, 0:4], -0.5, 0.5, ALU.mult, ALU.add))
            link(dve.tensor_tensor(c0, lbx[:, 0:4], c1, ALU.add))
            link(dve.tensor_scalar(c2, c0, -1.0, 1.0, ALU.mult, ALU.add))
            link(dve.tensor_scalar(c3, c1, -1.0, None, ALU.mult))

            def gated(br, j, u0):
                taken(dve, ("gate", br, j))
                dve.wait_ge(unit_done, u0 + 3 * (j // 2) + 3)
                if br == 0:
                    take(dve.scalar_tensor_tensor(merged[:, j, :], gate[:, j % 2, :], 1.0,
                                                  bank_of(("branch", br, j))[:], ALU.add, ALU.mult), ("branch", br, j))
                    dve.memset(lbx[:, 0:1], 0.0).then_inc(gate_used, 1)
                else:
                    take(dve.scalar_tensor_tensor(gate[:, j % 2, :], gate[:, j % 2, :], 1.0,
                                                  bank_of(("branch", br, j))[:], ALU.add, ALU.mult), ("branch", br, j))
                    taken(dve, ("branch", br, j))
                    link(dve.tensor_tensor(merged[:, j, :], merged[:, j, :], gate[:, j % 2, :], ALU.add))
                    dve.memset(lbx[:, 0:1], 0.0).then_inc(gate_used, 1)
                dve.wait_ge(gate_used, 8 * br + j + 1)

            def differences(n):
                m = (LEVELS + [0])[n]
                if m:
                    pairs = b[:].rearrange("p h (n m) -> p (h n) m", m=2 * m)
                    ref = pairs[:, :, m - 1:m].to_broadcast([P, H * T // (2 * m), 2 * m])
                    dve.tensor_tensor(E[:].rearrange("p h (n m) -> p (h n) m", m=2 * m), pairs, ref,
                                      ALU.subtract).then_inc(diff_ready, 1)
                else:
                    chunks = b[:].rearrange("p h (n m) -> p (h n) m", m=C)
                    ref = chunks[:, :, C - 1:C].to_broadcast([P, H * TT, C])
                    dve.tensor_tensor(E[:].rearrange("p h (n m) -> p (h n) m", m=C), ref, chunks,
                                      ALU.subtract).then_inc(diff_ready, 1)

            scores = [(t, h) for t in range(1, TT) for h in range(DH)]
            dve.wait_ge(x_normed, TT)

            def keys_of(t):
                return work[:, WORK_AT[t]:WORK_AT[t] + WIDTH[t]]

            def topk_round(t, r):
                if r == 0:
                    own = keys_of(t)[:, t * P:WIDTH[t]]
                    link(dve.tensor_tensor(own, own, tri, ALU.add))
                link(dve.max(m8, keys_of(t)))
                link(dve.match_replace(keys_of(t), m8, keys_of(t), TAKEN))
                if r == ROUNDS - 1:
                    link(dve.tensor_scalar(bias[:, BIAS_AT[t]:BIAS_AT[t] + WIDTH[t]], keys_of(t), TAKEN, NEG,
                                           ALU.not_equal, ALU.mult))

            link(dve.tensor_copy(bias[:, 0:P], tri))
            for n in range(12):
                if n == 1:
                    for m in range(4):
                        for odd_head in range(2):
                            hi = slice(64 * odd_head, 64 * odd_head + 64)
                            lo = slice(64 - 64 * odd_head, P - 64 * odd_head)
                            dve.wait_ge(qi_hi_made, 2 * m + odd_head + 1)
                            last = dve.tensor_tensor(qi_parts[lo, 2 * m + odd_head, :], bank_of(("qT", 4 + m))[hi, :],
                                                     qi_parts[hi, 2 * m + odd_head, :].bitcast(f32), ALU.subtract)
                            if odd_head == 0:
                                link(last)
                        take(last, ("qT", 4 + m))
                    dve.wait_ge(ki_split, 1)
                    dve.tensor_tensor(ki_lo[:], kiT[:], ki_hi[:].bitcast(f32), ALU.subtract).then_inc(ki_split, 1)
                if n % 3 == 2:
                    for jj in range(2):
                        gated(0, 2 * (n // 3) + jj, U_MERGE_MEM)
                for m in range(SPREAD[n], SPREAD[n + 1]):
                    t, h = scores[m]
                    taken(dve, ("score", t, h))
                    acc = work[:, WORK_AT[t]:WORK_AT[t] + WIDTH[t]]
                    wi = small[:, t, WI + h:WI + h + 1]
                    if h == 0:
                        dve.tensor_scalar(acc, relu[:, m % 2, 0:WIDTH[t]], wi, None, ALU.mult).then_inc(score_summed, 1)
                    else:
                        dve.scalar_tensor_tensor(acc, relu[:, m % 2, 0:WIDTH[t]], wi, acc, ALU.mult,
                                                 ALU.add).then_inc(score_summed, 1)
                    dve.wait_ge(score_summed, m + 1)
                    if t > 1:
                        for r in range(2 * h, 2 * h + 2):
                            topk_round(t - 1, r)
                if n == 1:
                    for h in range(H):
                        taken(dve, ("hf", h))
                        last = dve.tensor_scalar(b[:, h, :], th[:, h, :], c1[:, h:h + 1], c0[:, h:h + 1], ALU.mult, ALU.add)
                    last.then_inc(f_ready, 1)
                if n == 3:
                    dve.wait_ge(log_f_ready, 1)
                    for h in range(H):
                        for c in range(TT):
                            seg = b[:, h, c * C:(c + 1) * C]
                            last = dve.tensor_tensor_scan(seg, ones, seg, 0.0, ALU.mult, ALU.add)
                    link(last)
                    full(dve, ("qT", 7))
                    differences(0)
            half0 = lambda ap, side: ap.rearrange("p h (n s m) -> p (h n) s m", s=2, m=LEVELS[0])[:, :, side, :]
            for h in range(H):
                last = dve.tensor_scalar(k[:, h, :], th[:, h, :], c3[:, h:h + 1], c2[:, h:h + 1], ALU.mult, ALU.add)
            link(last)
            dve.wait_ge(exp_ready, 2)
            full(dve, ("score", TT - 1, DH - 1))
            dve.tensor_tensor(half0(G[:], 0), half0(k[:], 0), half0(E[:], 0), ALU.mult)
            link(dve.memset(A[:], 0.0))
            for h in range(H):
                taken(dve, ("hq", h))
                hs = slice(h, h + 1)
                last = dve.tensor_tensor(half0(G[:, hs, :], 1), half0(q[:, hs, :], 1), half0(E[:, hs, :], 1), ALU.mult)
            last.then_inc(G_ready, 1)
            for n, m in enumerate(LEVELS):
                if n:
                    dve.wait_ge(exp_ready, 2 * n + 2)
                    for h in range(H):
                        full(dve, ("level", n - 1, h))
                    view = lambda ap: ap[:].rearrange("p h (n s m) -> p (h n) s m", s=2, m=m)
                    link(dve.tensor_tensor(view(G)[:, :, 0, :], view(k)[:, :, 0, :], view(E)[:, :, 0, :], ALU.mult))
                    dve.tensor_tensor(view(G)[:, :, 1, :], view(q)[:, :, 1, :], view(E)[:, :, 1, :],
                                      ALU.mult).then_inc(G_ready, 1)
                dve.wait_ge(G_ready, n + 1)
                differences(n + 1)
                if n < H:
                    dve.wait_ge(silu_tanh, n + 1)
                    take(dve.scalar_tensor_tensor(silu2[:, n, :], gate[:, n % 2, :], 1.0,
                                                  bank_of(("hg", n))[:], ALU.add, ALU.mult), ("hg", n))
                for h in range(H):
                    full(dve, ("level", n, h))
                    blocks = HC // m
                    src = bank_of(("level", n, h))[:, 0:TT * HC].rearrange("p (c n m) -> p c n m", c=TT, m=m)
                    dst = A[:, h, :].rearrange("p (c n s m) -> p c n s m", c=TT, s=2, m=m)[:, :, :, 1, :]
                    own = msk[:, n * HC:(n + 1) * HC].rearrange("p (n m) -> p n m", m=m)
                    take(dve.copy_predicated(dst, own.unsqueeze(1).to_broadcast([P, TT, blocks, m]), src),
                         ("level", n, h))
                    taken(dve, ("level", n, h))
                if n < EARLY:
                    topk_round(TT - 1, n)
            dve.wait_ge(exp_ready, 2 * len(LEVELS) + 2)
            dve.tensor_tensor(G[:], k[:], E[:], ALU.mult).then_inc(G_ready, 1)
            n = len(LEVELS)
            for h in range(H):
                full(dve, ("level", n, h))
                src = bank_of(("level", n, h))[:].rearrange("p (c m) -> p c m", m=C)
                dst = A[:, h, :].rearrange("p (c m) -> p c m", m=C)
                take(dve.copy_predicated(dst, msk[:, n * HC:n * HC + C].unsqueeze(1).to_broadcast([P, TT, C]), src),
                     ("level", n, h))
                taken(dve, ("level", n, h))
            link(dve.memset(lbx[:, 0:1], 0.0))
            dve.memset(lbx[:, 0:1], 0.0).then_inc(A_ready, H)
            dve.wait_ge(decay_ready, 1)
            dve.tensor_tensor(q[:], q[:], b[:], ALU.mult).then_inc(qd_ready, 1)
            for h in range(H):
                full(dve, ("kdT", h))
            for h in range(H):
                full(dve, ("U", h))
                for c in range(TT - 1):
                    got = bank_of(("U", h))[:, c * C:(c + 1) * C]
                    if c == 0:
                        last = dve.tensor_copy(S[:, h, c, :], got)
                    else:
                        last = dve.scalar_tensor_tensor(S[:, h, c, :], S[:, h, c - 1, :],
                                                        b[:, h, (c + 1) * C - 1:(c + 1) * C], got, ALU.mult, ALU.add)
                    last.then_inc(S_ready, 1)
                    dve.wait_ge(S_ready, 3 * h + c + 1)
                take(dve.memset(lbx[:, 0:1], 0.0), ("U", h))
                taken(dve, ("U", h))
            for h in range(H):
                taken(dve, ("o", h))
                last = dve.scalar_tensor_tensor(o[:, h, :], o[:, h, :], 0.5, silu2[:, h, :], ALU.mult, ALU.mult)
            link(last)
            full(dve, ("oss", H - 1))
            even = lambda tile: tile[64:96].rearrange("p (a two) t -> p a two t", two=2)[:, :, 0, :]
            odd = lambda tile: tile[0:64].rearrange("p (a two) t -> p a two t", two=2)[:, :, 1, :]
            dve.tensor_copy(even(qh), qrT[64:96]).then_inc(rope_copied, 1)
            dve.tensor_copy(odd(qh), qrT[0:64]).then_inc(rope_copied, 1)
            full(dve, ("kn", DH // 2 - 1))
            dve.tensor_copy(even(kh), krT[64:96].unsqueeze(1).to_broadcast([32, DH // 2, T])).then_inc(rope_copied, 1)
            dve.tensor_copy(odd(kh), krT[0:64].unsqueeze(1).to_broadcast([64, DH // 2, T])).then_inc(rope_copied, 1)
            for h in range(H):
                dve.wait_ge(orstd_ready, h + 1)
                dve.tensor_tensor(o[:, h, :], o[:, h, :], orstd[:, h, :], ALU.mult).then_inc(oa_made, 1)

            def odd_keys(p):
                dve.wait_ge(kn_even, p + 1)
                take(dve.tensor_copy(kh[NOPE:P, 2 * p + 1, :], bank_of(("kn", p))[NOPE:P, :]), ("kn", p))

            odd_keys(0)
            odd_keys(1)

            def oa_low(h):
                dve.wait_ge(oa_hi_made, h + 1)
                dve.tensor_tensor(oa_lo[:, h, :], o[:, h, :], oa_hi[:, h, :].bitcast(f32),
                                  ALU.subtract).then_inc(oa_ready, 1)

            steps = TT * DH

            def masked_max(i):
                t = i // DH
                full(dve, ("S", i))
                if i >= 4:
                    full(dve, ("PT", i - 4))
                p = prob[:, i % 4, 0:WIDTH[t]]
                take(dve.scalar_tensor_tensor(p, bank_of(("S", i))[:, 0:WIDTH[t]], DSA_SCALE,
                                              bias[:, BIAS_AT[t]:BIAS_AT[t] + WIDTH[t]], ALU.mult, ALU.add), ("S", i))
                taken(dve, ("S", i))
                dve.tensor_reduce(d_max[:, i % 4:i % 4 + 1], p, axis=AX.X, op=ALU.max, negate=True).then_inc(logit_maxed, 1)

            def normalise(i):
                t = i // DH
                dve.wait_ge(exped, i + 1)
                link(dve.reciprocal(d_inv[:, i % 4:i % 4 + 1], d_sum[:, i % 4:i % 4 + 1]))
                p = prob[:, i % 4, 0:WIDTH[t]]
                dve.tensor_scalar(p, p, d_inv[:, i % 4:i % 4 + 1], None, ALU.mult).then_inc(prob_ready, 1)

            for i in range(AHEAD):
                masked_max(i)
            done = EARLY
            normalise(0)
            odd_keys(2)
            odd_keys(3)
            for i in range(steps):
                if i + 1 < steps:
                    normalise(i + 1)
                if i in GATED_AT:
                    for jj in range(2):
                        gated(1, 2 * GATED_AT.index(i) + jj, U_MERGE_HG)
                for _ in range(2 if i in MERGE_AT and i not in GATED_AT else 0):
                    if done < ROUNDS:
                        topk_round(TT - 1, done)
                        done += 1
                if i + AHEAD < steps:
                    masked_max(i + AHEAD)
                if i < H:
                    oa_low(i)
            for jj in range(2):
                gated(1, KT - 2 + jj, U_MERGE_HG)
            for p in range(DH // 2):
                dve.wait_ge(ob_hi_made, p + 1)
                take(dve.tensor_tensor(ob_lo[:, p, :], bank_of(("ob", p))[:], ob_hi[:, p, :].bitcast(f32),
                                       ALU.subtract), ("ob", p))
            for jp in range(4):
                for j in (2 * jp, 2 * jp + 1):
                    gated(2, j, U_MERGE_DSA)
                    dve.memset(lbx[:, 0:1], 0.0).then_inc(merged_added, KT + 1 if j == 0 else 1)
                for j in (2 * jp, 2 * jp + 1):
                    dve.wait_ge(merged_hi_made, j + 1)
                    dve.scalar_tensor_tensor(mg_lo[:, j, :], merged[:, j, :], 0.5, mg_hi[:, j, :].bitcast(f32),
                                             ALU.mult, ALU.subtract).then_inc(merged_ready, 1)
            dve.wait_ge(xr_in, 16)

            def add_residual(half, t):
                if half and t < TT - 1:
                    full(dve, ("out", half, t))
                else:
                    dve.wait_ge(unit_done, U_OUT + 4 * half + 4)
                part = h1[:, t, half * 512:(half + 1) * 512]
                take(dve.tensor_tensor(part, part, bank_of(("out", half, t))[:], ALU.add), ("out", half, t))

            def weigh_middle(half, t):
                hs = slice(half * 512, (half + 1) * 512)
                taken(dve, ("out", half, t))
                dve.tensor_tensor(hn[:, t, hs], h1[:, t, hs], mlp_row[:, hs], ALU.mult).then_inc(h_weighted, 1)

            def lo_of_middle(t, part):
                dve.wait_ge(m_hi_made, part * TT + t + 1)
                ks, ts = slice(4 * part, 4 * part + 4), slice(t * P, (t + 1) * P)
                take(dve.tensor_tensor(act_lo[:, ks, ts], bank_of(("mT", t, part))[:].rearrange("p (a c) -> p a c", a=4),
                                       act_hi[:, ks, ts].bitcast(f32), ALU.subtract), ("mT", t, part))

            dve.wait_ge(fin_in, 32)
            for half in range(2):
                for t in range(TT):
                    add_residual(half, t)
                    weigh_middle(half, t)
                    if half and t:
                        lo_of_middle(t - 1, 1)
                if half == 0:
                    for t in range(TT):
                        lo_of_middle(t, 0)
            lo_of_middle(TT - 1, 1)
            def down_residual(half, c, t):
                if t < TT - 1:
                    full(dve, ("down", half, c, t))
                else:
                    dve.wait_ge(unit_done, U_MLP + (2 * half + 1) * HALF + KT * (c + 1))
                part = h1[:, t, c * 512:(c + 1) * 512]
                take(dve.scalar_tensor_tensor(part, bank_of(("down", half, c, t))[:], h_rs2[:, t:t + 1], part,
                                              ALU.mult, ALU.add), ("down", half, c, t))

            for half in range(2):
                with dve.Fori(0, HALF // SLOTS) as i:
                    for s in range(SLOTS):
                        g, uses, _ = TURN["up", half, s]
                        dve.wait_ge(bank_taken[g], i * (SLOTS // 2) + (uses + 1))
                        dve.tensor_tensor(gate[:, s % 2, :], gate[:, s % 2, :], gate[:, s % 2, :],
                                          ALU.mult).then_inc(up_squared, 1)
                        dve.wait_ge(up_hi_made, i * SLOTS + (half * HALF + s + 1))
                        dve.tensor_tensor(u_lo[:, i * SLOTS + s, :], gate[:, s % 2, :],
                                          u_hi[:, i * SLOTS + s, :].bitcast(f32), ALU.subtract).then_inc(up_ready, 1)
                if half == 0:
                    dve.wait_ge(h_squared, 1)
                    link(dve.tensor_tensor(h_rs2, h_ss[:, 0:TT], h_ss[:, TT:2 * TT], ALU.add))
                    link(dve.tensor_scalar(h_rs2, h_rs2, 1.0 / D, EPS, ALU.mult, ALU.add))
                    link(dve.reciprocal(h_rs2, h_rs2))
                    for c in range(2):
                        for t in range(TT):
                            down_residual(0, c, t)
            for t in range(TT):
                down_residual(1, 0, t)
                taken(dve, ("down", 1, 0, t))
                dve.tensor_tensor(res[:, t, 0:512], h1[:, t, 0:512], fin_row[:, 0:512], ALU.mult)

            def last_rstd(pair):
                ts = slice(2 * pair, 2 * pair + 2)
                dve.wait_ge(y_rms, 2 * pair + 2)
                link(dve.tensor_tensor(y_ss2[:, ts], y_ss2[:, ts], y_ss[:, ts], ALU.add))
                rstd(y_rs[:, ts], y_ss2[:, ts], D, y_rms, 2 * pair + 2).then_inc(y_rstd, 1)
                dve.wait_ge(y_rstd, pair + 1)

            def scale_result(t):
                dve.wait_ge(y_weighted, t + 1)
                dve.tensor_scalar(res[:, t, :], res[:, t, :], y_rs[:, t:t + 1], None, ALU.mult).then_inc(res_ready, 1)

            down_residual(1, 1, 0)
            down_residual(1, 1, 1)
            down_residual(1, 1, 2)
            last_rstd(0)
            down_residual(1, 1, 3)
            scale_result(0)
            scale_result(1)
            last_rstd(1)
            scale_result(2)


def constants():
    s, t = np.arange(P)[:, None], np.arange(P)[None, :]
    const = np.zeros((P, N_CONST), np.float32)
    const[:, K_IDENT:K_IDENT + P] = s == t
    const[:, K_ONES:K_ONES + P] = 1.0
    const[:, K_TRI:K_TRI + P] = np.where(t <= s, 0.0, NEG)

    def pair(m):
        return (s // (2 * m) == t // (2 * m)) & (s % (2 * m) < m) & (t % (2 * m) >= m)

    masks = [pair(m)[:, (np.arange(P) % (2 * m)) >= m] for m in LEVELS] + [s == t]
    masks = np.concatenate(masks, axis=1).astype(np.float32)
    rope = np.zeros((P, TT, 192), np.float32)
    pos = np.arange(T, dtype=np.float32)
    at = 0
    for d in (IDX, ROPE):
        inv = (np.float32(10000.0) ** (-np.arange(0, d, 2, dtype=np.float32) / np.float32(d))).astype(np.float32)
        ang = pos[:, None] * inv[None, :]
        cos, sin = np.cos(ang), np.sin(ang)
        table = np.concatenate([cos, cos, -sin, sin], axis=1)
        rope[:, :, at:at + 2 * d] = table.reshape(TT, P, 2 * d).transpose(1, 0, 2)
        at += 2 * d
    return const, masks, rope.reshape(P, N_ROPE)


def lay_out(inputs):
    a = {n: np.asarray(v) for n, v in inputs.items()}
    w_in, w_kv = a["w_in"][0], a["w_mem_kv"][0]
    hq, hf, hv, hg, sm = (n * 512 for n in range(5))
    mq, gates = sm + SM, sm + SM + 512

    def t_units(w, c0, n):
        return w[:, c0:c0 + n * P].reshape(KT, P, n, P).transpose(2, 1, 0, 3).reshape(n, P, D)

    def n_units(w, c0):
        return w[:, c0:c0 + 512].reshape(4, 2, P, 512).transpose(0, 2, 1, 3).reshape(4, P, D)

    def merge_units(n, w):
        g = t_units(w_in, gates + n * D, KT).reshape(4, 2, P, D)
        br = w.reshape(4, P, 4, 2, P).transpose(2, 1, 3, 0, 4).reshape(4, 1, P, D)
        return np.concatenate([g, br], axis=1).reshape(12, P, D)

    up, down = a["w_mlp_up"][0], a["w_mlp_down"][0]
    mlp = []
    for half in range(2):
        mlp.append(t_units(up, half * HALF * P, HALF))
        rows = down[half * HALF * P:(half + 1) * HALF * P]
        mlp.append(rows.reshape(8, 2, P, 2, 512).transpose(3, 0, 2, 1, 4).reshape(HALF, P, D))
    stream = np.concatenate([
        t_units(w_kv, 0, H), n_units(w_kv, 512), n_units(w_in, sm), t_units(w_in, mq, H), t_units(w_in, hf, H),
        merge_units(2, a["w_br_mem"][0]), t_units(w_in, hq, H), t_units(w_in, hg, H), n_units(w_in, hv),
        merge_units(0, a["w_br_hgrn"][0]), merge_units(1, a["w_br_dsa"][0]),
        n_units(a["w_out"][0], 0), n_units(a["w_out"][0], 512)] + mlp)

    def rows_of(w, n):
        return w.reshape(2, P, n).transpose(1, 0, 2).reshape(P, 2 * n)

    uk = a["dsa_w_uk"][0].transpose(2, 0, 1).reshape(LAT, DH * NOPE)
    qr = a["dsa_w_qr"][0].reshape(QL, DH, ROPE)[:, QR_HEADS].reshape(QL, DH * ROPE)
    wdsa = np.concatenate([rows_of(a["dsa_w_qidx"][0], 512), rows_of(qr, 256),
                           rows_of(a["dsa_w_uq"][0], 512), uk], axis=1)
    wuv = a["dsa_w_uv"][0].transpose(1, 0, 2).reshape(LAT, DH * VD)
    cols = np.concatenate([a["attn_norm_w"].reshape(KT, P), a["mem_norm_w"].reshape(KT, P),
                           a["hgrn_out_norm_w"].reshape(H, P),
                           a["hgrn_lower_bounds"].reshape(2 * H, P)]).T
    rows = np.concatenate([a["dsa_q_norm_w"], a["dsa_kv_norm_w"], a["dsa_kidx_norm_w"]], axis=1)
    const, masks, rope = constants()
    return {"x": a["x"][0], "mem": a["mem"][0], "stream": stream, "wdsa": wdsa, "wuv": wuv, "const": const,
            "rope": rope, "masks": masks, "cols": cols, "rows": rows, "mid_row": a["mlp_norm_w"],
            "last_row": a["final_norm_w"][None, :]}


def kernel(**inputs):
    import concourse.bacc as bacc
    from concourse.bass_utils import run_bass_kernel_spmd

    nc = bacc.Bacc("TRN2", target_bir_lowering=False, num_devices=1)
    arrays, args = {}, []
    for name, value in lay_out(inputs).items():
        value = np.ascontiguousarray(value)
        arrays[f"in_{name}"] = value
        args.append(nc.dram_tensor(f"in_{name}", value.shape, mybir.dt.from_np(value.dtype),
                                   kind="ExternalInput").ap())
    out = nc.dram_tensor("out", (T, D), mybir.dt.float32, kind="ExternalOutput").ap()
    hybrid_block(nc, *args, out)
    got = run_bass_kernel_spmd(nc, [arrays], core_ids=[0])
    return got.results[0]["out"].reshape(1, T, D)
```
